# Optimizing a Trainium2 kernel written in Bass

```python
import functools
import jax, jax.numpy as jnp
from jax import lax
import numpy as np

D_MODEL = 2048
BATCH = 1
SEQ = 256
DEPTH = 2
DEC_BATCH = 8
DEC_SEQ = 8
PAST_LEN = 2048
PAGE_SIZE = 128

EXPAND = 2
E_WIDTH = EXPAND * D_MODEL
N_A = DEPTH // 2
N_B = DEPTH - N_A
DK_A = 128
H_A = D_MODEL // DK_A
DV_A = E_WIDTH // H_A
HD_B = 64
H_B = E_WIDTH // HD_B
KV_B = H_B // 8
G_B = H_B // KV_B
WINDOW = 128
N_META = 16
CHUNK = 16
EPS = 1e-6
NEG_BIG = -1e30
TINY = 1e-30

kernel_name = 'yoco_hgrn2_swa_sink_alibi_step'

def rmsnorm(x, g):
    x32 = x.astype(jnp.float32)
    y = x32 * lax.rsqrt(jnp.mean(x32 * x32, axis=-1, keepdims=True) + EPS)
    return (y * g.astype(jnp.float32)).astype(x.dtype)

def lower_bounds(lb_param):
    p = jax.nn.softmax(lb_param.astype(jnp.float32), axis=0)
    return jnp.cumsum(p, axis=0) - p[0]

def gla_chunk_scan(q, k, v, logf, s0):
    bsz, t_ = q.shape[:2]
    pad = (-t_) % CHUNK
    padw = ((0, 0), (0, pad), (0, 0), (0, 0))
    q, k, v, logf = [jnp.pad(a, padw) for a in (q, k, v, logf)]
    nc = (t_ + pad) // CHUNK

    def to_chunks(a):
        return jnp.moveaxis(a.reshape(bsz, nc, CHUNK, a.shape[2], a.shape[3]), 1, 0)

    causal = jnp.tril(jnp.ones((CHUNK, CHUNK), bool))[None, :, :, None, None]

    def step(S, inp):
        qc, kc, vc, gc = inp
        cum = jnp.cumsum(gc, axis=1)
        o_inter = jnp.einsum('bthd,bhde->bthe', qc * jnp.exp(cum), S)
        rel = cum[:, :, None] - cum[:, None, :]
        decay = jnp.where(causal, jnp.exp(jnp.where(causal, rel, 0.0)), 0.0)
        att = jnp.einsum('bthd,bshd,btshd->bhts', qc, kc, decay)
        o_intra = jnp.einsum('bhts,bshe->bthe', att, vc)
        last = cum[:, -1]
        S_new = jnp.exp(last)[..., None] * S + jnp.einsum(
            'bshd,bshe->bhde', kc * jnp.exp(last[:, None] - cum), vc)
        return S_new, o_inter + o_intra

    s_fin, o = lax.scan(step, s0, (to_chunks(q), to_chunks(k), to_chunks(v), to_chunks(logf)))
    o = jnp.moveaxis(o, 0, 1).reshape(bsz, nc * CHUNK, o.shape[-2], o.shape[-1])[:, :t_]
    return o, s_fin

def hgrn2_layer(x, s0, norm_g, w_in, lb, onorm_g, w_out):
    bsz, t_, _ = x.shape
    fd = H_A * DK_A
    z = rmsnorm(x, norm_g) @ w_in
    q, f, i, g = jnp.split(z, [fd, 2 * fd, 2 * fd + E_WIDTH], axis=-1)
    f = f.astype(jnp.float32)
    q = jax.nn.silu(q.astype(jnp.float32)) * (DK_A ** -0.5)
    base = jnp.log1p(-lb) + jax.nn.log_sigmoid(f)
    logf = jnp.where(lb > 0, jnp.logaddexp(jnp.log(jnp.maximum(lb, TINY)), base), base)
    k = (1.0 - lb) * jax.nn.sigmoid(-f)
    o, s_fin = gla_chunk_scan(q.reshape(bsz, t_, H_A, DK_A), k.reshape(bsz, t_, H_A, DK_A),
                              i.astype(jnp.float32).reshape(bsz, t_, H_A, DV_A),
                              logf.reshape(bsz, t_, H_A, DK_A), s0)
    o = rmsnorm(o, onorm_g).reshape(bsz, t_, E_WIDTH) * jax.nn.silu(g.astype(jnp.float32))
    return x + o.astype(x.dtype) @ w_out, s_fin

def alibi_slopes():
    h = jnp.arange(1, H_B + 1, dtype=jnp.float32)
    return (2.0 ** (-8.0 * h / H_B)).reshape(KV_B, G_B, 1, 1)

def sink_softmax_attention(q, k, v, dist, valid, sink):
    s = jnp.einsum('...ikgd,...jkd->...kgij', q.astype(jnp.float32), k.astype(jnp.float32)) * (HD_B ** -0.5)
    s = s - alibi_slopes() * dist.astype(jnp.float32)
    s = jnp.where(valid, s, NEG_BIG)
    m = jnp.maximum(jnp.max(s, axis=-1, keepdims=True), sink)
    p = jnp.where(valid, jnp.exp(s - m), 0.0)
    denom = jnp.sum(p, axis=-1, keepdims=True) + jnp.exp(sink - m)
    return jnp.einsum('...kgij,...jkd->...ikgd', p / denom, v.astype(jnp.float32))

def banded_attend(q, k, v, sink):
    bsz, t_ = q.shape[:2]
    nb = -(-t_ // WINDOW)
    pad = nb * WINDOW - t_
    qb = jnp.pad(q, ((0, 0), (0, pad), (0, 0), (0, 0), (0, 0))).reshape(bsz, nb, WINDOW, KV_B, G_B, HD_B)

    def band(a):
        a = jnp.pad(a, ((0, 0), (0, pad), (0, 0), (0, 0))).reshape(bsz, nb, WINDOW, KV_B, HD_B)
        prev = jnp.pad(a, ((0, 0), (1, 0), (0, 0), (0, 0), (0, 0)))[:, :-1]
        return jnp.concatenate([prev, a], axis=2)

    i = jnp.arange(WINDOW)[:, None]
    j = jnp.arange(2 * WINDOW)[None, :]
    dist = WINDOW + i - j
    valid = (dist >= 0) & (dist < WINDOW)
    valid = valid[None] & ((jnp.arange(nb)[:, None, None] > 0) | (j >= WINDOW)[None])
    o = sink_softmax_attention(qb, band(k), band(v), dist, valid[:, None, None], sink)
    return o.reshape(bsz, nb * WINDOW, KV_B, G_B, HD_B)[:, :t_]

def cached_attend(q, k, v, sink, past_k, past_v):
    wb = past_k.shape[1]
    t_ = q.shape[1]
    kf = jnp.concatenate([past_k.astype(k.dtype), k], axis=1)
    vf = jnp.concatenate([past_v.astype(v.dtype), v], axis=1)
    i = jnp.arange(t_)[:, None]
    j = jnp.arange(wb + t_)[None, :]
    dist = wb + i - j
    valid = (dist >= 0) & (dist < WINDOW)
    return sink_softmax_attention(q, kf, vf, dist, valid, sink)

def swa_layer(x, k_sh, v_sh, attend, norm_g, w_in, sink, w_out):
    bsz, t_, _ = x.shape
    z = rmsnorm(x, norm_g) @ w_in
    q, gate = jnp.split(z, 2, axis=-1)
    q = q.reshape(bsz, t_, KV_B, G_B, HD_B)
    o = attend(q, k_sh, v_sh, sink.astype(jnp.float32).reshape(KV_B, G_B, 1, 1))
    o = o.reshape(bsz, t_, E_WIDTH) * jax.nn.silu(gate.astype(jnp.float32))
    return x + o.astype(x.dtype) @ w_out

def trunk(x, s0, attend, norm_a, w_in_a, lb_a, onorm_a, w_out_a, norm_kv, w_kv,
          norm_b, w_in_b, sink_b, w_out_b, norm_f):
    bsz, t_, _ = x.shape
    lbs = lower_bounds(lb_a)
    states = []
    k_sh = v_sh = None
    for layer in range(DEPTH):
        if layer < N_A:
            x, s = hgrn2_layer(x, s0[layer], norm_a[layer], w_in_a[layer], lbs[layer],
                               onorm_a[layer], w_out_a[layer])
            states.append(s)
            if layer == N_A - 1:
                kv = rmsnorm(x, norm_kv) @ w_kv
                k_sh, v_sh = jnp.split(kv, 2, axis=-1)
                k_sh = k_sh.reshape(bsz, t_, KV_B, HD_B)
                v_sh = v_sh.reshape(bsz, t_, KV_B, HD_B)
        else:
            lb_i = layer - N_A
            x = swa_layer(x, k_sh, v_sh, attend, norm_b[lb_i], w_in_b[lb_i], sink_b[lb_i], w_out_b[lb_i])
    return rmsnorm(x, norm_f), jnp.stack(states), k_sh, v_sh

def setup_inputs(seed: int = 0) -> dict:
    key = jax.random.key(seed)
    ks = jax.random.split(key, 20)
    f32 = jnp.float32
    wb = min(WINDOW, PAST_LEN)
    za = 2 * H_A * DK_A + 2 * E_WIDTH

    def nrm(k, shape, s):
        return s * jax.random.normal(k, shape, f32)

    return {
        'x_prompt': nrm(ks[0], (BATCH, SEQ, D_MODEL), 1.0),
        'x_sample': nrm(ks[1], (DEC_BATCH, DEC_SEQ, D_MODEL), 1.0),
        'state_hgrn': nrm(ks[2], (N_A, DEC_BATCH, H_A, DK_A, DV_A), 0.3),
        'cache_k': nrm(ks[3], (DEC_BATCH, wb, KV_B, HD_B), 1.0),
        'cache_v': nrm(ks[4], (DEC_BATCH, wb, KV_B, HD_B), 1.0),
        'meta_tokens': nrm(ks[5], (N_META, D_MODEL), 1.0),
        'norm_a': 1.0 + nrm(ks[6], (N_A, D_MODEL), 0.02),
        'w_in_a': nrm(ks[7], (N_A, D_MODEL, za), D_MODEL ** -0.5),
        'lb_a': nrm(ks[8], (N_A, H_A * DK_A), 0.5),
        'onorm_a': 1.0 + nrm(ks[9], (N_A, DV_A), 0.02),
        'w_out_a': nrm(ks[10], (N_A, E_WIDTH, D_MODEL), E_WIDTH ** -0.5),
        'norm_kv': 1.0 + nrm(ks[11], (D_MODEL,), 0.02),
        'w_kv': nrm(ks[12], (D_MODEL, 2 * KV_B * HD_B), D_MODEL ** -0.5),
        'norm_b': 1.0 + nrm(ks[13], (N_B, D_MODEL), 0.02),
        'w_in_b': nrm(ks[14], (N_B, D_MODEL, 2 * E_WIDTH), D_MODEL ** -0.5),
        'sink_b': nrm(ks[15], (N_B, H_B), 0.5),
        'w_out_b': nrm(ks[16], (N_B, E_WIDTH, D_MODEL), E_WIDTH ** -0.5),
        'norm_f': 1.0 + nrm(ks[17], (D_MODEL,), 0.02),
    }

def reference(x_prompt, x_sample, state_hgrn, cache_k, cache_v, meta_tokens, norm_a, w_in_a, lb_a,
              onorm_a, w_out_a, norm_kv, w_kv, norm_b, w_in_b, sink_b, w_out_b, norm_f):
    weights = (norm_a, w_in_a, lb_a, onorm_a, w_out_a, norm_kv, w_kv, norm_b, w_in_b, sink_b, w_out_b, norm_f)
    bsz = x_prompt.shape[0]
    wb = cache_k.shape[1]
    meta = jnp.broadcast_to(meta_tokens.astype(x_prompt.dtype)[None], (bsz, N_META, D_MODEL))
    xp = jnp.concatenate([meta, x_prompt], axis=1)
    s0p = jnp.zeros((N_A, bsz, H_A, DK_A, DV_A), jnp.float32)
    yp, sp, kp, vp = trunk(xp, s0p, banded_attend, *weights)
    attend_s = functools.partial(cached_attend, past_k=cache_k, past_v=cache_v)
    ys, ss, k_new, v_new = trunk(x_sample, state_hgrn.astype(jnp.float32), attend_s, *weights)
    y_prompt = yp[:, N_META:]
    state_hgrn_prompt = sp.astype(state_hgrn.dtype)
    cache_k_prompt = kp[:, -wb:].astype(cache_k.dtype)
    cache_v_prompt = vp[:, -wb:].astype(cache_v.dtype)
    state_hgrn_sample = ss.astype(state_hgrn.dtype)
    cache_k_sample = jnp.concatenate([cache_k, k_new.astype(cache_k.dtype)], axis=1)[:, -wb:]
    cache_v_sample = jnp.concatenate([cache_v, v_new.astype(cache_v.dtype)], axis=1)[:, -wb:]
    return (y_prompt, ys, state_hgrn_prompt, cache_k_prompt, cache_v_prompt,
            state_hgrn_sample, cache_k_sample, cache_v_sample)


_drawn_inputs = setup_inputs


def setup_inputs(seed=0):
    import zlib

    import numpy as np

    out = dict(_drawn_inputs(seed))
    spreads = {}
    factors = {'state_hgrn': 3.06,
     'onorm_a': 5.207,
     'norm_kv': 2.914,
     'norm_b': 8.0,
     'sink_b': 26.523,
     'norm_f': 7.96}
    for name, (base, spread) in spreads.items():
        noise = np.random.default_rng([zlib.crc32(name.encode()), seed]).standard_normal(out[name].shape)
        drawn = base * np.exp(spread * noise) if base else spread * noise
        out[name] = __import__('jax').numpy.asarray(drawn.astype(out[name].dtype))
    for name, factor in factors.items():
        out[name] = (out[name] * factor).astype(out[name].dtype)
    return out
```

```python
import numpy as np
import concourse.bass as bass
from concourse import mybir
from contextlib import ExitStack

F32 = mybir.dt.float32
F32R = mybir.dt.float32r
ACT = mybir.ActivationFunctionType
ALU = mybir.AluOpType
AX = mybir.AxisListType

P = 128
D = 2048
META, SEQ, NB, TS = 16, 256, 8, 8
TP = META + SEQ
T = TP + NB * TS
TQ = T - META
KT = D // P
H = 16
DV = 256
ET = 2 * KT
KV, G, HD = 8, 8, 64
WIN = 128
EPS = 1e-6
BIG = 1e30

SLAB = 4
SLAB_W = SLAB * 256
RING = 4
SLABS_H = 3 * KT // SLAB
SLABS_OUT = ET // SLAB
SLABS_KV = 4 * KT // SLAB
SLABS_G = 4 * KT // SLAB
BASE_OUT_A = H * SLABS_H
BASE_KV = BASE_OUT_A + (D // 256) * SLABS_OUT
BASE_B = BASE_KV + SLABS_KV
BASE_OUT_B = BASE_B + KV * SLABS_G
N_SLABS = BASE_OUT_B + (D // 256) * SLABS_OUT

TAIL = T - 2 * P
TAILP = TP - 2 * P
LEVELS = 7
LV_TOKENS = [T, T, T, TP, 2 * P, 2 * P, 2 * P]
TOT_LEN = [T, T // 2, T // 4, T // 8, TP // 16, 2 * P // 32, 2 * P // 64, 2]
TOT_AT = [0] + [sum(TOT_LEN[1:l]) for l in range(1, LEVELS + 1)]
TOT_N = sum(TOT_LEN[1:])
QS_W = TAIL + TS
UNITS = G + 2
NKEYS = META + P
SC = NKEYS + 2 * P
SS = WIN + NB * TS

C_MASK = 0
C_MASK3 = C_MASK + (LEVELS + 1) * P
C_ROWS = C_MASK3 + 5 * TAIL
C_IDENT = C_ROWS + NB + 1
C_ONES = C_IDENT + P
C_ALL1 = C_ONES + P
C_DIST = 0
C_DIST_S = C_DIST + SC
C_SLOPE = C_DIST_S + 2 * SS
C_SLOPE_S = C_SLOPE + G
C_ALL2 = C_SLOPE_S + 2


def tables():
    t1 = np.zeros((P, C_ALL1), np.float32)
    s, t = np.arange(P)[:, None], np.arange(P)[None, :]
    for n, l in enumerate([6, 5, 4, 3, 2, 1, 0]):
        t1[:, C_MASK + n * P:C_MASK + (n + 1) * P] = ((s ^ t) >> l == 1) & (t > s)
    t1[:, C_MASK + LEVELS * P:C_MASK + (LEVELS + 1) * P] = s == t
    s, t = np.arange(TAIL)[:, None], np.arange(TAIL)[None, :]
    for n, l in enumerate([3, 2, 1, 0]):
        own = (s < TAILP) & (t < TAILP) if l == 3 else True
        t1[:TAIL, C_MASK3 + n * TAIL:C_MASK3 + (n + 1) * TAIL] = ((s ^ t) >> l == 1) & (t > s) & own
    t1[:TAIL, C_MASK3 + 4 * TAIL:C_MASK3 + 5 * TAIL] = s == t
    t1[:TAILP, C_ROWS] = 1.0
    for b in range(NB):
        t1[TAILP + b * TS:TAILP + (b + 1) * TS, C_ROWS + 1 + b] = 1.0
    t1[:, C_IDENT:C_IDENT + P] = np.eye(P)
    t1[:, C_ONES:C_ONES + P] = 1.0

    t2 = np.zeros((P, C_ALL2), np.float32)
    i = np.arange(P)[:, None]
    for at, q0, k0, n in ((C_DIST, META, 0, NKEYS), (C_DIST + NKEYS, META + P, META, 2 * P)):
        d = (q0 + i) - (k0 + np.arange(n)[None, :])
        t2[:, at:at + n] = np.where((d >= 0) & (d < WIN), -d, -BIG)
    row = np.arange(P)
    seq, u, tok = row // 32, row // 8 % 4, row % 8
    for half in range(2):
        at = C_DIST_S + half * SS
        d = WIN + tok[:, None] - np.arange(WIN)[None, :]
        t2[:, at:at + WIN] = np.where(d < WIN, -d, -BIG)
        new = np.arange(NB * TS)[None, :]
        d = tok[:, None] - new % TS
        own = (new // TS == 4 * half + seq[:, None]) & (d >= 0)
        t2[:, at + WIN:at + SS] = np.where(own, -d, -BIG)
    for g in range(G):
        t2[:, C_SLOPE + g] = 8.0 * 2.0 ** (-(g + 1) / 8.0)
    for par in range(2):
        t2[:, C_SLOPE_S + par] = 8.0 * 2.0 ** (-(2 * u + par + 1) / 8.0)
    return t1, t2


def trunk(nc, x_in, w_in, s0_in, cv_in, ckd_in, vec_in, sink_in, t1_in, t2_in, ckold_in, cvold_in,
          y_out, st_prompt, st_sample, k_out, v_out, ckold_out, cvold_out):
    stack = ExitStack()

    def sb(name, shape, dt=F32, scope=None):
        return (scope or stack).enter_context(nc.sbuf_tensor(name, shape, dt))

    def sem(name):
        return stack.enter_context(nc.semaphore(name))

    with stack:
        raw = sb("raw", [P, RING, SLAB, 256])
        split = sb("split", [P, RING, 2, SLAB, 256], F32R)
        t1 = sb("t1", [P, C_ALL1])
        vec = sb("vec", [P, 4 * KT + 2])
        rstd = sb("rstd", [P, T])
        xT = sb("xT", [P, KT, T])
        ogin = sb("ogin", [P, 4, 2, T])
        sqo = sb("sqo", [P, 2, T])
        VA, VKV, VB, VF, VO = 0, KT, 2 * KT, 3 * KT, 4 * KT
        ident, ones = t1[:, C_IDENT:C_IDENT + P], t1[:, C_ONES:C_ONES + P]

        s1 = stack.enter_context(ExitStack())
        xnH, xnL = sb("xnH", [P, KT, T], F32R, s1), sb("xnL", [P, KT, T], F32R, s1)
        xn, sq = sb("xn", [P, 2, T], F32, s1), sb("sq", [P, 2, T], F32, s1)
        qs, fs, ks, sigq = (sb(n, [P, T], F32, s1) for n in ("qs", "fs", "ks", "sigq"))
        qc = [sb(f"qc{l}", [P, T if l < 4 else TP], F32, s1) for l in range(LEVELS + 1)]
        kr = [ks] + [sb(f"kr{l}", [P, T if l < 4 else TP], F32, s1) for l in range(1, LEVELS + 1)]
        tot_all = sb("tot_all", [P, TOT_N], F32, s1)
        tot = [fs] + [tot_all[:, TOT_AT[l]:TOT_AT[l] + TOT_LEN[l]] for l in range(1, LEVELS + 1)]
        kx, kf = sb("kx", [P, P], F32, s1), sb("kf", [P, T], F32, s1)
        iT = sb("iT", [P, 2, T], F32, s1)
        V = sb("V", [P, 3, DV], F32, s1)
        masked = sb("masked", [P, 8 * P], F32, s1)
        att = sb("att", [P, 4, P], F32, s1)
        attX = sb("attX", [P, 2, TAIL], F32, s1)
        kt, kts = sb("kt", [P, 3, P], F32, s1), sb("kts", [P, NB + 1, P], F32, s1)
        Qs = sb("Qs", [P, TAILP + NB * QS_W], F32, s1)
        S0 = sb("S0", [P, NB, DV], F32, s1)
        Sp = sb("Sp", [P, DV], F32, s1)
        on = sb("on", [P, 3, DV], F32, s1)
        junk = sb("junk", [P, 3, DV], F32, s1)
        ssq, rs3 = sb("ssq", [P, 3], F32, s1), sb("rs3", [P, 3], F32, s1)
        ms3, norm_const = sb("ms3", [P, 2, 3], F32, s1), sb("norm_const", [P, 3, 3], F32, s1)
        sg, gs, og = (sb(n, [P, 2, T], F32, s1) for n in ("sg", "gs", "og"))
        s1.close()

        s2 = stack.enter_context(ExitStack())
        ogH, ogL = sb("ogH", [P, ET, T], F32R, s2), sb("ogL", [P, ET, T], F32R, s2)
        yst = sb("yst", [P, 4, TQ], F32, s2)
        s2.close()

        s3 = stack.enter_context(ExitStack())
        xkH, xkL = sb("xkH", [P, KT, T], F32R, s3), sb("xkL", [P, KT, T], F32R, s3)
        xk = sb("xk", [P, 2, T], F32, s3)
        kT = sb("kT", [P, KV, T], F32, s3)
        vT, ktmp = sb("vT", [P, 4, T], F32, s3), sb("ktmp", [P, 4, T], F32, s3)
        t2 = sb("t2", [P, C_ALL2], F32, s3)
        sinks = sb("sinks", [P, KV, G + 2], F32, s3)
        vtok = sb("vtok", [P, 4, 4 * P], F32, s3)
        ckT, cv = sb("ckT", [P, NB, WIN], F32, s3), sb("cv", [P, NB, HD], F32, s3)
        vg, kg, sinkg = sb("vg", [P, 4, HD], F32, s3), sb("kg", [P, T], F32, s3), sb("sinkg", [P, G + 2], F32, s3)
        qT, qsam = sb("qT", [P, 4, TQ], F32, s3), sb("qsam", [P, NB, 4, TS], F32, s3)
        sc, pT = sb("sc", [P, 2, SC], F32, s3), sb("pT", [P, 2, 4 * P], F32, s3)
        stat = sb("stat", [P, 2, 7, 2], F32, s3)
        gate, sgb, ob = (sb(n, [P, 4, TQ], F32, s3) for n in ("gate", "sgb", "ob"))
        s3.close()

        pz = stack.enter_context(nc.psum_tensor("pz", [P, 4, 512], F32))
        RA0, RA1, RO, RT = (stack.enter_context(nc.psum_tensor(n, [P, 512], F32))
                            for n in ("RA0", "RA1", "RO", "RT"))
        scratch = nc.dram_tensor("og_scratch", [ET, P, T], F32, kind="Internal").ap()

        w_loaded = [sem(f"w_loaded{i}") for i in range(RING)]
        (w_hi, w_lo, mm_done, x_loaded, t1_loaded, vec_loaded, s0_loaded, t2_loaded, sink_loaded,
         sq_ready, sq_used, ms_ready, root_ready, rstd_ready, xn_ready, xh_ready, xl_ready,
         sigq_ready, fk_ready, qs_ready, qc0_ready, lev_mul, lev_copied, kx_ready, kf_ready,
         kft_copied, Qs_ready, zeroed, i_copied, lev_done, masked_ready, att_ready, cross_done,
         cross_copied, kfT_done, kt_copied, kts_ready, vT_done, v_copied, o_done, ssq_ready,
         ms3_ready, rs3_ready, on_ready, s0_scaled, st_done, sp_copied, st_added, g_sig, g_ready,
         oT_done, og_ready, og_stored, st_stored, sp_stored) = (sem(n) for n in (
            "w_hi", "w_lo", "mm_done", "x_loaded", "t1_loaded", "vec_loaded", "s0_loaded", "t2_loaded",
            "sink_loaded", "sq_ready", "sq_used", "ms_ready", "root_ready", "rstd_ready", "xn_ready",
            "xh_ready", "xl_ready", "sigq_ready", "fk_ready", "qs_ready", "qc0_ready", "lev_mul",
            "lev_copied", "kx_ready", "kf_ready", "kft_copied", "Qs_ready", "zeroed", "i_copied",
            "lev_done", "masked_ready", "att_ready", "cross_done", "cross_copied", "kfT_done",
            "kt_copied", "kts_ready", "vT_done", "v_copied", "o_done", "ssq_ready", "ms3_ready",
            "rs3_ready", "on_ready", "s0_scaled", "st_done", "sp_copied", "st_added", "g_sig",
            "g_ready", "oT_done", "og_ready", "og_stored", "st_stored", "sp_stored"))
        og_loaded = [sem(f"og_loaded{i}") for i in range(4)]
        y_stored = [sem(f"y_stored{i}") for i in range(2)]
        (ogh_ready, ogl_ready, x_added, k_copied, k_spread, kv_stored, vtok_done, vtok_copied,
         sinks_ready, staged, ck_loaded, q_copied, qk_done, biased, max_ready, mm_ready, sm_ready,
         exp_ready, den_ready, rden_ready, p_ready, tr_done, pt_copied, pv_done, o_copied,
         g0_copied, gb_sig, gb_ready, ob_ready, slope_ready, y_ready, old_stored, vt_copied,
         obg_stored, qsam_ready) = (sem(n) for n in (
            "ogh_ready", "ogl_ready", "x_added", "k_copied", "k_spread", "kv_stored", "vtok_done",
            "vtok_copied", "sinks_ready", "staged", "ck_loaded", "q_copied", "qk_done", "biased",
            "max_ready", "mm_ready", "sm_ready", "exp_ready", "den_ready", "rden_ready", "p_ready",
            "tr_done", "pt_copied", "pv_done", "o_copied", "g0_copied", "gb_sig", "gb_ready",
            "ob_ready", "slope_ready", "y_ready", "old_stored", "vt_copied", "obg_stored",
            "qsam_ready"))

        def early(x, limit):
            return isinstance(x, int) and x < limit

        def load_slab(sp, g, s):
            if not early(g, RING):
                sp.wait_ge(w_lo, g - RING + 1)
            sp.dma_start(raw[:, s % RING], w_in[bass.ds(g, 1)].rearrange("a p n -> p (a n)")
                         ).then_inc(w_loaded[s % RING], 16)

        def split_hi(act, g, s, turn):
            act.wait_ge(w_loaded[s % RING], 16 * (turn + 1))
            if not early(g, RING):
                act.wait_ge(mm_done, g - RING + 1)
            nc.scalar.activation(split[:, s % RING, 0], raw[:, s % RING], ACT.Copy).then_inc(w_hi, 1)

        def split_lo(dve, g, s):
            dve.wait_ge(w_hi, g + 1)
            nc.vector.tensor_tensor(split[:, s % RING, 1], raw[:, s % RING],
                                    split[:, s % RING, 0].bitcast(F32), ALU.subtract).then_inc(w_lo, 1)

        def products(pe, g, s, kt0, bank, high, low, n, first, last):
            pe.wait_ge(w_lo, g + 1)
            for k in range(SLAB):
                for half in range(2):
                    cols = slice(half * P, half * P + P)
                    out = pz[:, bank + half, 0:n]
                    wh, wl = split[:, s % RING, 0, k, cols], split[:, s % RING, 1, k, cols]
                    begin, end = first and k == 0, last and k == SLAB - 1
                    nc.tensor.matmul(out, wh, high[:, kt0 + k, 0:n], start=begin, stop=False)
                    nc.tensor.matmul(out, wh, low[:, kt0 + k, 0:n], start=False, stop=False)
                    done = nc.tensor.matmul(out, wl, high[:, kt0 + k, 0:n], start=False, stop=end)
            done.then_inc(mm_done, 1)

        def root_dve(dve, c, n):
            dve.wait_ge(sq_used, KT * (c + 1))
            nc.vector.tensor_scalar(rstd[:, 0:n], RA0[:, 0:n], 1.0 / D, EPS, ALU.mult, ALU.add).then_inc(ms_ready, 1)
            dve.wait_ge(root_ready, c + 1)
            nc.vector.reciprocal(rstd[:, 0:n], rstd[:, 0:n]).then_inc(rstd_ready, 1)
            dve.wait_ge(rstd_ready, c + 1)

        def root_act(act, c, n):
            act.wait_ge(ms_ready, c + 1)
            nc.scalar.activation(rstd[:, 0:n], rstd[:, 0:n], ACT.Sqrt).then_inc(root_ready, 1)

        def sum_square(pe, sqr, at, count, slot, n, first, last):
            pe.wait_ge(sq_ready, at + 1)
            nc.tensor.matmul(RA0[:, 0:n], ones, sqr[:, slot, 0:n], start=first, stop=last).then_inc(sq_used, 1)

        def scaled(dve, ft, slot, done, buf, gcol, c0, n):
            if not early(done, 2):
                dve.wait_ge(xl_ready, done - 1)
            nc.vector.scalar_tensor_tensor(buf[:, slot, 0:n], xT[:, ft, c0:c0 + n], vec[:, gcol + ft:gcol + ft + 1],
                                           rstd[:, c0:c0 + n], ALU.mult, ALU.mult).then_inc(xn_ready, 1)

        def scaled_hi(act, ft, slot, done, buf, high, n):
            act.wait_ge(xn_ready, done + 1)
            nc.scalar.activation(high[:, ft, 0:n], buf[:, slot, 0:n], ACT.Copy).then_inc(xh_ready, 1)

        def scaled_lo(dve, ft, slot, done, buf, high, low, n):
            dve.wait_ge(xh_ready, done + 1)
            nc.vector.tensor_tensor(low[:, ft, 0:n], buf[:, slot, 0:n], high[:, ft, 0:n].bitcast(F32),
                                    ALU.subtract).then_inc(xl_ready, 1)

        def normalise_dve(dve, made, buf, gcol, high, low, c0, n, tiles):
            for ft in tiles:
                scaled(dve, ft, ft % 2, made + ft, buf, gcol, c0, n)
                if ft % 2:
                    scaled_lo(dve, ft - 1, 0, made + ft - 1, buf, high, low, n)
                    scaled_lo(dve, ft, 1, made + ft, buf, high, low, n)

        def normalise_act(act, made, buf, high, n, tiles):
            for ft in tiles:
                scaled_hi(act, ft, ft % 2, made + ft, buf, high, n)

        block = stack.enter_context(nc.Block())

        @block.sync
        def _(sp):
            def head_round(h):
                for s in range(SLABS_H):
                    load_slab(sp, SLABS_H * h + s, s)
                    if early(h, 1):
                        continue
                    if s == 10:
                        sp.wait_ge(st_added, 4 * h)
                        sp.dma_start(st_sample[bass.ds(h - 1, 1)].rearrange("a p n -> p (a n)"),
                                     S0[:].rearrange("p b e -> p (b e)")).then_inc(st_stored, 16)
                        sp.wait_ge(sp_copied, h)
                        sp.dma_start(st_prompt[bass.ds(h - 1, 1)].rearrange("a p n -> p (a n)"), Sp[:]
                                     ).then_inc(sp_stored, 16)
                    if s == 11:
                        sp.wait_ge(st_stored, 16 * h)
                        sp.dma_start(S0[:].rearrange("p b e -> p (b e)"),
                                     s0_in[bass.ds(h, 1)].rearrange("a p n -> p (a n)")).then_inc(s0_loaded, 16)
                        sp.wait_ge(og_ready, h)
                        sp.dma_start(scratch[bass.ds(2 * h - 2, 2)].rearrange("a p n -> p a n"), og[:]
                                     ).then_inc(og_stored, 16)

            head_round(0)
            with sp.Fori(1, H) as h:
                head_round(h)

            for s in range(RING):
                load_slab(sp, BASE_OUT_A + s, s)
            for c in range(ET // 2 - 1):
                if c >= 4:
                    sp.wait_ge(ogl_ready, c - 3)
                if c == 0:
                    sp.wait_ge(og_stored, 16 * (H - 1))
                sp.dma_start(ogin[:, c % 4], scratch[2 * c:2 * c + 2].rearrange("a p n -> p a n")
                             ).then_inc(og_loaded[c % 4], 16)
            sp.wait_ge(og_ready, H)
            sp.dma_start(scratch[ET - 2:ET].rearrange("a p n -> p a n"), og[:]).then_inc(og_stored, 16)
            sp.wait_ge(og_stored, 16 * H)
            sp.wait_ge(ogl_ready, ET // 2 - 4)
            sp.dma_start(ogin[:, (ET // 2 - 1) % 4], scratch[ET - 2:ET].rearrange("a p n -> p a n")
                         ).then_inc(og_loaded[(ET // 2 - 1) % 4], 16)
            sp.wait_ge(st_added, 4 * H)
            sp.dma_start(st_sample[H - 1], S0[:].rearrange("p b e -> p (b e)")).then_inc(st_stored, 16)
            sp.wait_ge(sp_copied, H)
            sp.dma_start(st_prompt[H - 1], Sp[:]).then_inc(sp_stored, 16)
            for s in range(RING, SLABS_OUT):
                load_slab(sp, BASE_OUT_A + s, s)
            with sp.Fori(1, D // 256) as j:
                for s in range(SLABS_OUT):
                    load_slab(sp, BASE_OUT_A + SLABS_OUT * j + s, s)

            for s in range(SLABS_KV):
                load_slab(sp, BASE_KV + s, s)
                if s == 4:
                    sp.wait_ge(mm_done, BASE_KV)
                    sp.dma_start(t2[:], t2_in).then_inc(t2_loaded, 16)
                    sp.dma_start(sinks[:].rearrange("p a b -> p (a b)"), sink_in).then_inc(sink_loaded, 16)
            for s in range(RING):
                load_slab(sp, BASE_B + s, s)
            sp.wait_ge(k_copied, 2)
            for src in range(2):
                for dst in range(2):
                    sp.dma_start(kT[64 * dst:64 * dst + 64].rearrange("p (j two) t -> p j two t", two=2)[:, :, src],
                                 ktmp[64 * src:64 * src + 64]).then_inc(k_spread, 16)
            sp.dma_start(k_out.rearrange("j p t -> p j t"), ktmp[:]).then_inc(kv_stored, 16)
            sp.wait_ge(vt_copied, 2)
            sp.dma_start(v_out.rearrange("j p t -> p j t"), vT[:]).then_inc(kv_stored, 16)
            sp.wait_ge(kv_stored, 32)

            def group_round(n):
                for s in range(SLABS_G):
                    if early(n, 1) and s < RING:
                        continue
                    load_slab(sp, BASE_B + SLABS_G * n + s, s)
                    if s == 10:
                        if not early(n, 1):
                            sp.wait_ge(pv_done, UNITS * n)
                        sp.dma_start(ckT[:].rearrange("p b j -> p (b j)"),
                                     ckd_in[bass.ds(n, 1)].rearrange("a p n -> p (a n)")).then_inc(ck_loaded, 16)
                        sp.dma_start(cv[:].rearrange("p b j -> p (b j)"),
                                     cv_in[bass.ds(n, 1)].rearrange("a p n -> p (a n)")).then_inc(ck_loaded, 16)
                    if s == 13 and not early(n, 1):
                        sp.wait_ge(ob_ready, n)
                        sp.dma_start(scratch[bass.ds(4 * n - 4, 4), :, 0:TQ].rearrange("a p n -> p a n"), gate[:]
                                     ).then_inc(obg_stored, 16)

            group_round(0)
            with sp.Fori(1, KV) as n:
                group_round(n)
            for s in range(RING):
                load_slab(sp, BASE_OUT_B + s, s)
            sp.wait_ge(obg_stored, 16 * (KV - 1))
            for c in range(ET // 2):
                sp.wait_ge(ogl_ready, ET // 2 + c - 3)
                if c == ET // 2 - 2:
                    sp.wait_ge(ob_ready, KV)
                    sp.dma_start(scratch[ET - 4:ET, :, 0:TQ].rearrange("a p n -> p a n"), gate[:]).then_inc(obg_stored, 16)
                    sp.wait_ge(obg_stored, 16 * KV)
                sp.dma_start(ogin[:, c % 4, :, 0:TQ], scratch[2 * c:2 * c + 2, :, 0:TQ].rearrange("a p n -> p a n")
                             ).then_inc(og_loaded[c % 4], 16)
            for s in range(RING, SLABS_OUT):
                load_slab(sp, BASE_OUT_B + s, s)
            with sp.Fori(1, D // 256) as j:
                for s in range(SLABS_OUT):
                    load_slab(sp, BASE_OUT_B + SLABS_OUT * j + s, s)
            for f in range(0, KT, 2):
                sp.wait_ge(y_ready, f + 2)
                i = f // 2 % 2
                sp.dma_start(y_out[f:f + 2].rearrange("a p n -> p a n"), yst[:, 2 * i:2 * i + 2]).then_inc(y_stored[i], 16)
            for i in range(2):
                sp.wait_ge(y_stored[i], 16 * KT // 4)
            sp.wait_ge(st_stored, 16 * H)
            sp.wait_ge(sp_stored, 16 * H)
            sp.wait_ge(kv_stored, 32)
            sp.wait_ge(obg_stored, 16 * KV)
            sp.wait_ge(old_stored, 32)

        @block.gpsimd
        def _(pool):
            nc.gpsimd.memset(Qs[:], 0.0)
            nc.gpsimd.memset(attX[:], 0.0)
            for i, value in enumerate((1.0 / DV, EPS, -0.5)):
                nc.gpsimd.memset(norm_const[:, i], value)
            nc.gpsimd.memset(ssq[:], 0.0).then_inc(zeroed, 1)
            pool.dma_start(ckold_out, ckold_in).then_inc(old_stored, 16)
            pool.dma_start(cvold_out, cvold_in).then_inc(old_stored, 16)
            pool.wait_ge(t1_loaded, 16)

            def keep(out, x):
                one = t1[0:x.shape[0], C_ONES:C_ONES + 1]
                for _ in range(len(x.shape) - 2):
                    one = one.unsqueeze(2)
                return nc.gpsimd.tensor_tensor(out, x, one.broadcast_to(list(x.shape)), ALU.mult)

            def tail(h):
                pool.wait_ge(ssq_ready, h + 1)
                nc.gpsimd.tensor_tensor(ms3[:, 0], ssq[:], norm_const[:, 0], ALU.mult).then_inc(ms3_ready, 1)
                pool.wait_ge(ms3_ready, 2 * h + 1)
                nc.gpsimd.tensor_tensor(ms3[:, 1], ms3[:, 0], norm_const[:, 1], ALU.add).then_inc(ms3_ready, 1)
                pool.wait_ge(ms3_ready, 2 * h + 2)
                nc.gpsimd.tensor_tensor(rs3[:], ms3[:, 1], norm_const[:, 2], ALU.pow).then_inc(rs3_ready, 1)

            def head(h):
                for l in range(LEVELS):
                    n, b = LV_TOKENS[l], 1 << l
                    if l == 0:
                        pool.wait_ge(qc0_ready, h + 1)
                    else:
                        pool.wait_ge(lev_mul, LEVELS * h + l)
                        pool.wait_ge(lev_copied, LEVELS * h + l)

                    def halves(x, which):
                        return x[:, 0:n].rearrange("p (b two h) -> p b two h", two=2, h=b)[:, :, which]
                    keep(halves(qc[l + 1], 0), halves(qc[l], 0))
                    nc.gpsimd.tensor_copy(halves(kr[l + 1], 1), halves(kr[l], 1)).then_inc(lev_copied, 1)
                pool.wait_ge(lev_copied, LEVELS * (h + 1))
                keep(kf[:, 2 * P:TP], kr[4][:, 2 * P:TP])
                nc.gpsimd.tensor_copy(kf[:, TP:T], kr[3][:, TP:T]).then_inc(kft_copied, 1)
                pool.wait_ge(kt_copied, h + 1)
                nc.gpsimd.tensor_tensor(kts[0:TAIL], kt[0:TAIL, 2:3].broadcast_to([TAIL, NB + 1, P]),
                                        t1[0:TAIL, C_ROWS:C_ROWS + NB + 1].unsqueeze(2).broadcast_to([TAIL, NB + 1, P]),
                                        ALU.mult).then_inc(kts_ready, 1)
                pool.wait_ge(o_done, 2 * (h + 1))
                nc.gpsimd.tensor_tensor(S0[:], S0[:], tot[3][:, TP // 8:TP // 8 + NB].unsqueeze(2).broadcast_to([P, NB, DV]),
                                        ALU.mult).then_inc(s0_scaled, 1)
                tail(h)

            head(0)
            with pool.Fori(1, H) as h:
                head(h)

            def stage(n):
                if not early(n, 1):
                    pool.wait_ge(pv_done, UNITS * n)
                    pool.wait_ge(sm_ready, UNITS * n)
                keep(kg[:].unsqueeze(1), kT[:, bass.ds(n, 1)])
                nc.gpsimd.tensor_copy(vg[:, 1:3], vtok[:, 1:3, bass.ds(n * HD, HD)])
                nc.gpsimd.tensor_copy(vg[0:META, 0:1], vtok[0:META, 0:1, bass.ds(n * HD, HD)])
                nc.gpsimd.tensor_copy(vg[0:NB * TS, 3:4], vtok[0:NB * TS, 3:4, bass.ds(n * HD, HD)])
                nc.gpsimd.tensor_copy(sinkg[:].unsqueeze(1), sinks[:, bass.ds(n, 1)]).then_inc(staged, 1)
                pool.wait_ge(q_copied, 2 * (n + 1))
                for w in range(4):
                    done = keep(qsam[:, :, w], qT[:, w, SEQ:TQ].rearrange("p (b t) -> p b t", t=TS))
                done.then_inc(qsam_ready, 1)

            pool.wait_ge(k_spread, 64)
            pool.wait_ge(vtok_copied, 4)
            pool.wait_ge(sinks_ready, 1)
            stage(0)
            with pool.Fori(1, KV) as n:
                stage(n)

        @block.scalar
        def _(act):
            act.dma_start(t1[:], t1_in).then_inc(t1_loaded, 16)
            act.dma_start(xT[:].rearrange("p a n -> p (a n)"), x_in).then_inc(x_loaded, 16)
            act.dma_start(vec[:], vec_in).then_inc(vec_loaded, 16)
            act.dma_start(S0[:].rearrange("p b e -> p (b e)"), s0_in[0]).then_inc(s0_loaded, 16)
            root_act(act, 0, T)
            for s in range(RING):
                split_hi(act, s, s, 0)
                normalise_act(act, 0, xn, xnH, T, range(4 * s, 4 * s + 4))

            def head_round(h, head=True):
                t = h - 1
                for s in range(SLABS_H if head else RING):
                    if not (early(h, 1) and s < RING):
                        split_hi(act, SLABS_H * h + s, s, SLABS_H // RING * h + s // RING)
                    if s == 1 and not early(h, 1):
                        act.wait_ge(cross_done, t + 1)
                        if not early(h, 2):
                            act.wait_ge(o_done, 2 * t)
                        nc.scalar.activation(att[:, 2], RO[:, 0:P], ACT.Copy)
                        nc.scalar.activation(attX[:, :, 0:TAILP], RO[:, P:P + 2 * TAILP].rearrange("p (a n) -> p a n", a=2),
                                             ACT.Copy).then_inc(cross_copied, 1)
                        act.wait_ge(kfT_done, t + 1)
                        nc.scalar.activation(kt[:, 0:2], RT[:, 0:2 * P].rearrange("p (a n) -> p a n", a=2), ACT.Copy)
                        nc.scalar.activation(kt[0:TAIL, 2], RT[0:TAIL, 2 * P:3 * P], ACT.Copy).then_inc(kt_copied, 1)
                    if s == 2 and not early(h, 1):
                        act.wait_ge(vT_done, 2 * (t + 1))
                        nc.scalar.activation(V[:, 0:2], RA0[:].rearrange("p (a n) -> p a n", a=2), ACT.Copy)
                        nc.scalar.activation(V[0:TAIL, 2], RA1[0:TAIL, 0:DV], ACT.Copy).then_inc(v_copied, 1)
                    if s == 3 and not early(h, 1):
                        act.wait_ge(mm_done, SLABS_H * h)
                        if not early(h, 2):
                            act.wait_ge(g_ready, t)
                        nc.scalar.activation(sg[:], pz[:, 0:2, 0:T], ACT.Sigmoid).then_inc(g_sig, 1)
                        act.wait_ge(o_done, 2 * (t + 1))
                        nc.scalar.activation(junk[:, 0], RO[:, 0:DV], ACT.Square, accum_out=ssq[:, 0:1])
                        nc.scalar.activation(junk[:, 1], RO[:, DV:2 * DV], ACT.Square, accum_out=ssq[:, 1:2])
                        nc.scalar.activation(junk[0:TAIL, 2], RA1[0:TAIL, 0:DV], ACT.Square, accum_out=ssq[0:TAIL, 2:3]
                                             ).then_inc(ssq_ready, 1)
                    if not head and s == 3:
                        outputs(t, h)
                        continue
                    if s == 4 and not early(h, 1):
                        outputs(t, h)
                    if s == 7 and head:
                        act.wait_ge(mm_done, SLABS_H * h + 4)
                        if not early(h, 1):
                            act.wait_ge(qs_ready, h)
                            act.wait_ge(kfT_done, h)
                            act.wait_ge(kf_ready, h)
                        nc.scalar.activation(sigq[:], pz[:, 0, 0:T], ACT.Sigmoid).then_inc(sigq_ready, 1)
                        nc.scalar.activation(fs[:], pz[:, 1, 0:T], ACT.Sigmoid)
                        nc.scalar.activation(ks[:], pz[:, 1, 0:T], ACT.Sigmoid, scale=-1.0).then_inc(fk_ready, 1)
                    if s == 11 and head:
                        act.wait_ge(mm_done, SLABS_H * h + 8)
                        if not early(h, 1):
                            act.wait_ge(vT_done, 2 * h)
                        nc.scalar.activation(iT[:], pz[:, 2:4, 0:T], ACT.Copy).then_inc(i_copied, 1)

            def outputs(t, h):
                act.wait_ge(st_done, 5 * t + 1)
                if not early(h, 2):
                    act.wait_ge(sp_stored, 16 * t)
                nc.scalar.activation(Sp[:], RT[:, 0:DV], ACT.Copy).then_inc(sp_copied, 1)
                act.wait_ge(rs3_ready, t + 1)
                if not early(h, 2):
                    act.wait_ge(oT_done, t)
                nc.scalar.activation(on[:, 0], RO[:, 0:DV], ACT.Copy, scale=rs3[:, 0:1])
                nc.scalar.activation(on[:, 1], RO[:, DV:2 * DV], ACT.Copy, scale=rs3[:, 1:2])
                nc.scalar.activation(on[0:TAIL, 2], RA1[0:TAIL, 0:DV], ACT.Copy, scale=rs3[0:TAIL, 2:3]
                                     ).then_inc(on_ready, 1)

            head_round(0)
            head_round(1)
            with act.Fori(2, H) as h:
                head_round(h)
            head_round(H, head=False)

            def gather(before, free, n):
                act.wait_ge(mm_done, free)
                for c in range(ET // 2):
                    act.wait_ge(og_loaded[c % 4], 16 * ((before + c) // 4 + 1))
                    nc.scalar.activation(ogH[:, 2 * c:2 * c + 2, 0:n], ogin[:, c % 4, :, 0:n], ACT.Copy).then_inc(ogh_ready, 1)

            def out_round(base, turn0, j):
                for s in range(SLABS_OUT):
                    if early(j, 1) and s < RING:
                        continue
                    split_hi(act, base + SLABS_OUT * j + s, s, turn0 + SLABS_OUT // RING * j + s // RING)

            def out_projection(base):
                out_round(base, base // RING, 0)
                with act.Fori(1, D // 256) as j:
                    out_round(base, base // RING, j)

            gather(0, BASE_OUT_A, T)
            out_projection(BASE_OUT_A)

            for s in range(RING):
                split_hi(act, BASE_KV + s, s, BASE_KV // RING)
            root_act(act, 1, T)
            normalise_act(act, KT, xk, xkH, T, range(KT))
            for s in range(RING, SLABS_KV):
                split_hi(act, BASE_KV + s, s, BASE_KV // RING + s // RING)
                if s in (7, 11):
                    j = s // 4 - 1
                    act.wait_ge(mm_done, BASE_KV + 4 * j + 4)
                    nc.scalar.activation(ktmp[:, 2 * j:2 * j + 2], pz[:, 2 * j:2 * j + 2, 0:T], ACT.Copy).then_inc(k_copied, 1)
                if s == 15:
                    act.wait_ge(mm_done, BASE_KV + 12)
                    nc.scalar.activation(vT[:, 0:2], pz[:, 0:2, 0:T], ACT.Copy).then_inc(vt_copied, 1)
            for s in range(RING):
                split_hi(act, BASE_B + s, s, BASE_B // RING)
                if s == 3:
                    act.wait_ge(mm_done, BASE_KV + SLABS_KV)
                    nc.scalar.activation(vT[:, 2:4], pz[:, 2:4, 0:T], ACT.Copy).then_inc(vt_copied, 1)
                normalise_act(act, 2 * KT, xk, xkH, TQ, range(4 * s, 4 * s + 4))
            act.wait_ge(vtok_done, 4)
            nc.scalar.activation(vtok[0:META, 0], RA0[0:META, :], ACT.Copy).then_inc(vtok_copied, 1)
            nc.scalar.activation(vtok[:, 1], RA1[:, :], ACT.Copy).then_inc(vtok_copied, 1)
            nc.scalar.activation(vtok[:, 2], RO[:, :], ACT.Copy).then_inc(vtok_copied, 1)
            nc.scalar.activation(vtok[0:NB * TS, 3], RT[0:NB * TS, :], ACT.Copy).then_inc(vtok_copied, 1)

            def exps(n, u):
                k, r = UNITS * n + u, u % 2
                act.wait_ge(sm_ready, k + 1)
                if u < G:
                    parts = [(sc[:, r, 0:NKEYS], 0), (sc[:, r, NKEYS:SC], 1)]
                else:
                    parts = [(sc[:, r, 0:SS], 0), (sc[:, r, SS:2 * SS], 1)]
                for part, i in parts:
                    nc.scalar.activation(part, part, ACT.Exp, bias=stat[:, r, 2, i:i + 1], scale=HD ** -0.5,
                                         accum_out=stat[:, r, 5, i:i + 1])
                nc.scalar.activation(stat[:, r, 4], stat[:, r, 3], ACT.Exp, scale=HD ** -0.5).then_inc(exp_ready, 1)

            def copy_p(n, u):
                k, r = UNITS * n + u, u % 2
                act.wait_ge(tr_done, k + 1)
                if not early(k, 2):
                    act.wait_ge(pv_done, k - 1)
                if u < G:
                    nc.scalar.activation(pT[:, r, P:4 * P], RT[:, P:4 * P], ACT.Copy)
                    nc.scalar.activation(pT[0:META, r, 0:P], RT[0:META, 0:P], ACT.Copy).then_inc(pt_copied, 1)
                else:
                    def fours(x):
                        return x.rearrange("p (two n) -> p two n", two=2)
                    nc.scalar.activation(fours(pT[:, r])[:, :, 0:P], fours(RT[:])[:, :, 0:P], ACT.Copy)
                    nc.scalar.activation(fours(pT[0:NB * TS, r])[:, :, P:2 * P], fours(RT[0:NB * TS])[:, :, P:2 * P],
                                         ACT.Copy).then_inc(pt_copied, 1)

            def copy_o(n, u):
                if u < G:
                    if u % 2:
                        act.wait_ge(pv_done, UNITS * n + u + 1)
                        if u == 1 and not early(n, 1):
                            act.wait_ge(ob_ready, n)
                        nc.scalar.activation(ob[:, u // 2, 0:SEQ], RO[:, 0:SEQ], ACT.Copy).then_inc(o_copied, 1)
                elif u == UNITS - 1:
                    act.wait_ge(pv_done, UNITS * (n + 1))
                    for w in range(4):
                        done = nc.scalar.activation(
                            ob[:, w, SEQ:TQ].rearrange("p (b t) -> p b t", t=TS),
                            RO[:, 0:SEQ].rearrange("p (b w t) -> p w b t", w=4, t=TS)[:, w], ACT.Copy)
                    done.then_inc(o_copied, 1)

            def group_round(n, own=True):
                for s in range(SLABS_G if own else 8):
                    if (own or s < RING) and not (early(n, 1) and s < RING):
                        split_hi(act, BASE_B + SLABS_G * n + s, s, BASE_B // RING + SLABS_G // RING * n + s // RING)
                    for u in range(UNITS):
                        for at, what in ((14 + u, copy_o), (12 + u, copy_p), (9 + u, exps)):
                            if at == s and own:
                                what(n, u)
                            if at == s + SLABS_G and not early(n, 1):
                                what(n - 1, u)
                    if s == 3 and not early(n, 1):
                        act.wait_ge(mm_done, BASE_B + SLABS_G * n)
                        act.wait_ge(g0_copied, n)
                        nc.scalar.activation(sgb[:, 0:2], gate[:, 0:2], ACT.Sigmoid)
                        nc.scalar.activation(sgb[:, 2:4], pz[:, 2:4, 0:TQ], ACT.Sigmoid).then_inc(gb_sig, 1)
                    if own and s in (7, 11):
                        j = s // 4 - 1
                        act.wait_ge(mm_done, BASE_B + SLABS_G * n + 4 * j + 4)
                        nc.scalar.activation(qT[:, 2 * j:2 * j + 2], pz[:, 2 * j:2 * j + 2, 0:TQ], ACT.Copy).then_inc(q_copied, 1)
                    if own and s == 15:
                        act.wait_ge(mm_done, BASE_B + SLABS_G * n + 12)
                        if not early(n, 1):
                            act.wait_ge(obg_stored, 16 * n)
                        nc.scalar.activation(gate[:, 0:2], pz[:, 0:2, 0:TQ], ACT.Copy).then_inc(g0_copied, 1)

            group_round(0)
            with act.Fori(1, KV) as n:
                group_round(n)
            group_round(KV, own=False)
            gather(ET // 2, BASE_OUT_B, TQ)
            out_projection(BASE_OUT_B)
            root_act(act, 2, TQ)

        @block.vector
        def _(dve):
            def squares(at, slot, buf, ft, c0, n):
                if not early(at, 2):
                    dve.wait_ge(sq_used, at - 1)
                nc.vector.tensor_tensor(buf[:, slot, 0:n], xT[:, ft, c0:c0 + n], xT[:, ft, c0:c0 + n], ALU.mult
                                        ).then_inc(sq_ready, 1)

            dve.wait_ge(x_loaded, 16)
            for ft in range(KT):
                squares(ft, ft % 2, sq, ft, 0, T)
            root_dve(dve, 0, T)
            dve.wait_ge(vec_loaded, 16)
            for s in range(RING):
                split_lo(dve, s, s)
                normalise_dve(dve, 0, xn, VA, xnH, xnL, 0, T, range(4 * s, 4 * s + 4))
            dve.wait_ge(t1_loaded, 16)
            dve.wait_ge(zeroed, 1)

            def doubling(h, l):
                n, b = LV_TOKENS[l], 1 << l
                dve.wait_ge(lev_copied, LEVELS * h + l)
                dve.wait_ge(lev_mul, LEVELS * h + l)

                def halves(x, which):
                    return x[:, 0:n].rearrange("p (b two h) -> p b two h", two=2, h=b)[:, :, which]
                blocks = tot[l][:, 0:n // b].rearrange("p (b two) -> p b two", two=2)
                shape = [P, n // (2 * b), b]
                nc.vector.tensor_tensor(halves(qc[l + 1], 1), halves(qc[l], 1), blocks[:, :, 0:1].broadcast_to(shape), ALU.mult)
                nc.vector.tensor_tensor(halves(kr[l + 1], 0), halves(kr[l], 0), blocks[:, :, 1:2].broadcast_to(shape), ALU.mult)
                nc.vector.tensor_tensor(tot[l + 1][:, 0:n // (2 * b)], blocks[:, :, 0], blocks[:, :, 1], ALU.mult
                                        ).then_inc(lev_mul, 1)

            def attention_tile(h, i):
                if i == 0:
                    dve.wait_ge(lev_done, 5 * h + 1)
                    if not early(h, 1):
                        dve.wait_ge(o_done, 2 * h)
                        dve.wait_ge(att_ready, 3 * h)
                    nc.vector.tensor_tensor(masked[0:TAIL, 0:5 * TAIL], RT[0:TAIL, 0:5 * TAIL],
                                            t1[0:TAIL, C_MASK3:C_MASK3 + 5 * TAIL], ALU.mult).then_inc(masked_ready, 1)
                    dve.wait_ge(masked_ready, 5 * h + 1)
                    nc.vector.tensor_reduce(out=att[0:TAIL, 3, 0:TAIL],
                                            in_=masked[0:TAIL, 0:5 * TAIL].rearrange("p (l t) -> p t l", t=TAIL),
                                            axis=AX.X, op=ALU.add).then_inc(att_ready, 1)
                else:
                    dve.wait_ge(att_ready, 3 * h + i)
                    for k, bank in ((0, RA0), (1, RA1)):
                        dve.wait_ge(lev_done, 5 * h + 2 * i + k)
                        nc.vector.tensor_tensor(masked[:, 512 * k:512 * k + 512], bank[:],
                                                t1[:, C_MASK + 512 * k:C_MASK + 512 * k + 512], ALU.mult
                                                ).then_inc(masked_ready, 1)
                    dve.wait_ge(masked_ready, 5 * h + 2 * i + 1)
                    nc.vector.tensor_reduce(out=att[:, i - 1], in_=masked[:].rearrange("p (l t) -> p t l", t=P),
                                            axis=AX.X, op=ALU.add).then_inc(att_ready, 1)

            def add_states(t, pair):
                bank = RA0 if pair % 2 == 0 else RT
                dve.wait_ge(st_done, 5 * t + pair + 2)
                dve.wait_ge(s0_scaled, t + 1)
                nc.vector.tensor_tensor(S0[:, 2 * pair:2 * pair + 2], bank[:].rearrange("p (a n) -> p a n", a=2),
                                        S0[:, 2 * pair:2 * pair + 2], ALU.add).then_inc(st_added, 1)

            def gate_a(t, h):
                dve.wait_ge(oT_done, t + 1)
                dve.wait_ge(g_ready, t + 1)
                if not early(h, 2):
                    dve.wait_ge(og_stored, 16 * t)
                nc.vector.scalar_tensor_tensor(og[:, 0], RO[:, 0:T], vec[:, VO:VO + 1], gs[:, 0], ALU.mult, ALU.mult)
                nc.vector.scalar_tensor_tensor(og[:, 1], RA1[:, 0:T], vec[:, VO + 1:VO + 2], gs[:, 1], ALU.mult, ALU.mult
                                               ).then_inc(og_ready, 1)

            def head_round(h, head=True):
                t = h - 1
                for s in range(SLABS_H if head else RING):
                    if not (early(h, 1) and s < RING):
                        split_lo(dve, SLABS_H * h + s, s)
                    if s == 0 and not early(h, 1):
                        attention_tile(t, 2)
                    if s == 3 and not early(h, 1):
                        dve.wait_ge(g_sig, t + 1)
                        nc.vector.tensor_tensor(gs[:], sg[:], pz[:, 0:2, 0:T], ALU.mult).then_inc(g_ready, 1)
                    if s == 3 and not head:
                        for pair in range(4):
                            add_states(t, pair)
                        gate_a(t, h)
                        continue
                    if s == 4 and not early(h, 1):
                        add_states(t, 0)
                    if s == 5 and not early(h, 1):
                        add_states(t, 1)
                        add_states(t, 2)
                    if s == 6 and not early(h, 1):
                        add_states(t, 3)
                    if s == 7:
                        if not early(h, 1):
                            gate_a(t, h)
                        dve.wait_ge(sigq_ready, h + 1)
                        nc.vector.scalar_tensor_tensor(qs[:], sigq[:], P ** -0.5, pz[:, 0, 0:T], ALU.mult, ALU.mult
                                                       ).then_inc(qs_ready, 1)
                        dve.wait_ge(fk_ready, h + 1)
                        dve.wait_ge(qs_ready, h + 1)
                        if not early(h, 1):
                            dve.wait_ge(s0_scaled, h)
                        nc.vector.tensor_tensor(qc[0][:], qs[:], fs[:], ALU.mult).then_inc(qc0_ready, 1)
                        dve.wait_ge(qc0_ready, h + 1)
                        for l in range(4):
                            doubling(h, l)
                    if s == 8:
                        for l in range(4, LEVELS):
                            doubling(h, l)
                        dve.wait_ge(lev_mul, LEVELS * (h + 1))
                        dve.wait_ge(lev_copied, LEVELS * (h + 1))
                        last, tail_decay = tot[7][:, 1:2], tot[4][:, TP // 16 - 1:TP // 16]
                        nc.vector.tensor_scalar(kx[:], kr[7][:, 0:P], last, None, ALU.mult).then_inc(kx_ready, 1)
                        nc.vector.tensor_scalar(kf[:, P:2 * P], kr[7][:, P:2 * P], tail_decay, None, ALU.mult)
                        dve.wait_ge(kx_ready, h + 1)
                        nc.vector.tensor_scalar(kf[:, 0:P], kx[:], tail_decay, None, ALU.mult).then_inc(kf_ready, 1)
                        nc.vector.tensor_copy(
                            Qs[:, TAILP:TAILP + NB * QS_W].rearrange("p (b c) -> p b c", c=QS_W)[:, :, 0:TS],
                            qc[3][:, TP:T].rearrange("p (b t) -> p b t", t=TS)).then_inc(Qs_ready, 1)
                    if s == 10:
                        attention_tile(h, 0)
                    if s == 11:
                        attention_tile(h, 1)

            head_round(0)
            head_round(1)
            with dve.Fori(2, H) as h:
                head_round(h)
            head_round(H, head=False)

            def gather(before, n):
                for c in range(ET // 2):
                    dve.wait_ge(ogh_ready, before + c + 1)
                    nc.vector.tensor_tensor(ogL[:, 2 * c:2 * c + 2, 0:n], ogin[:, c % 4, :, 0:n],
                                            ogH[:, 2 * c:2 * c + 2, 0:n].bitcast(F32), ALU.subtract).then_inc(ogl_ready, 1)

            def add_pair(base, before, j, bank, c0, n):
                dve.wait_ge(mm_done, base + SLABS_OUT * (j + 1))
                x = xT[:, bass.ds(2 * j, 2), c0:c0 + n]
                nc.vector.tensor_tensor(x, x, pz[:, bank:bank + 2, 0:n], ALU.add).then_inc(x_added, 1)
                dve.wait_ge(x_added, before // 2 + j + 1)
                dve.wait_ge(sq_used, before + KT + 2 * j)
                nc.vector.tensor_tensor(sqo[:, :, 0:n], x, x, ALU.mult).then_inc(sq_ready, 2)

            def out_projection(base, before, c0, n):
                def out_round(j, par):
                    for s in range(SLABS_OUT):
                        if not (early(j, 1) and s < RING):
                            split_lo(dve, base + SLABS_OUT * j + s, s)
                        if s == 3 and not early(j, 1):
                            add_pair(base, before, j - 1, 2 * (1 - par), c0, n)
                out_round(0, 0)
                out_round(1, 1)
                with dve.Fori(2, D // 256, 2) as j:
                    out_round(j, 0)
                    out_round(j + 1, 1)

            gather(0, T)
            out_projection(BASE_OUT_A, 0, 0, T)

            for s in range(RING):
                split_lo(dve, BASE_KV + s, s)
            add_pair(BASE_OUT_A, 0, D // 256 - 1, 2, 0, T)
            root_dve(dve, 1, T)
            normalise_dve(dve, KT, xk, VKV, xkH, xkL, 0, T, range(KT))
            for s in range(RING, SLABS_KV):
                split_lo(dve, BASE_KV + s, s)
                if s == 15:
                    dve.wait_ge(sink_loaded, 16)
                    dve.wait_ge(t2_loaded, 16)
                    nc.vector.tensor_scalar(sinks[:], sinks[:], HD ** 0.5, None, ALU.mult).then_inc(sinks_ready, 1)
            for s in range(RING):
                split_lo(dve, BASE_B + s, s)
                dve.wait_ge(mm_done, BASE_KV + 13 + s)
                normalise_dve(dve, 2 * KT, xk, VB, xkH, xkL, META, TQ, range(4 * s, 4 * s + 4))

            def scores(n, u):
                k, r = UNITS * n + u, u % 2
                bank = RA0 if r == 0 else RA1
                dve.wait_ge(qk_done, k + 1)
                dve.wait_ge(staged, n + 1)
                if not early(k, 2):
                    dve.wait_ge(tr_done, k - 1)
                if u < G:
                    nc.vector.scalar_tensor_tensor(sc[:, r, 0:SC], t2[:, C_DIST:C_DIST + SC],
                                                   t2[:, C_SLOPE + u:C_SLOPE + u + 1], bank[:, 0:SC],
                                                   ALU.mult, ALU.add).then_inc(biased, 1)
                    parts = [(0, NKEYS), (NKEYS, SC)]
                    sink = sinkg[:, u:u + 1].broadcast_to([P, 2])
                else:
                    slope = C_SLOPE_S + u - G
                    nc.vector.scalar_tensor_tensor(sc[:, r, 0:2 * SS], t2[:, C_DIST_S:C_DIST_S + 2 * SS],
                                                   t2[:, slope:slope + 1], bank[:, 0:2 * SS],
                                                   ALU.mult, ALU.add).then_inc(biased, 1)
                    parts = [(0, SS), (SS, 2 * SS)]
                    sink = sinkg[:, u:u + 1].broadcast_to([P, 2])
                dve.wait_ge(biased, k + 1)
                for i, (a, b) in enumerate(parts):
                    done = nc.vector.reduce_max(stat[:, r, 0, i:i + 1], sc[:, r, a:b], AX.X)
                done.then_inc(max_ready, 1)
                dve.wait_ge(max_ready, k + 1)
                nc.vector.tensor_tensor(stat[:, r, 1], stat[:, r, 0], sink, ALU.max).then_inc(mm_ready, 1)
                dve.wait_ge(mm_ready, k + 1)
                nc.vector.tensor_scalar(stat[:, r, 2], stat[:, r, 1], -HD ** -0.5, None, ALU.mult)
                nc.vector.tensor_tensor(stat[:, r, 3], sink, stat[:, r, 1], ALU.subtract).then_inc(sm_ready, 1)

            def divide(n, u):
                k, r = UNITS * n + u, u % 2
                dve.wait_ge(exp_ready, k + 1)
                nc.vector.tensor_tensor(stat[:, r, 5], stat[:, r, 5], stat[:, r, 4], ALU.add).then_inc(den_ready, 1)
                dve.wait_ge(den_ready, k + 1)
                nc.vector.reciprocal(stat[:, r, 6], stat[:, r, 5]).then_inc(rden_ready, 1)
                dve.wait_ge(rden_ready, k + 1)
                for i, (a, b) in enumerate([(0, NKEYS), (NKEYS, SC)] if u < G else [(0, SS), (SS, 2 * SS)]):
                    done = nc.vector.tensor_scalar(sc[:, r, a:b], sc[:, r, a:b], stat[:, r, 6, i:i + 1], None, ALU.mult)
                done.then_inc(p_ready, 1)

            def group_round(n, own=True):
                for s in range(SLABS_G if own else 9):
                    if (own or s < RING) and not (early(n, 1) and s < RING):
                        split_lo(dve, BASE_B + SLABS_G * n + s, s)
                    for u in range(UNITS):
                        for at, what in ((10 + u, divide), (9 + u, scores)):
                            if at == s and own:
                                what(n, u)
                            if at == s + SLABS_G and not early(n, 1):
                                what(n - 1, u)
                    if s == 4 and not early(n, 1):
                        dve.wait_ge(gb_sig, n)
                        nc.vector.tensor_tensor(gate[:, 0:2], gate[:, 0:2], sgb[:, 0:2], ALU.mult)
                        nc.vector.tensor_tensor(gate[:, 2:4], pz[:, 2:4, 0:TQ], sgb[:, 2:4], ALU.mult).then_inc(gb_ready, 1)
                    if s == 8 and not early(n, 1):
                        dve.wait_ge(o_copied, 5 * n)
                        dve.wait_ge(gb_ready, n)
                        nc.vector.tensor_tensor(gate[:], gate[:], ob[:], ALU.mult).then_inc(ob_ready, 1)
                        if own:
                            nc.vector.tensor_scalar(t2[:, C_SLOPE:C_ALL2], t2[:, C_SLOPE:C_ALL2], 0.5, None, ALU.mult
                                                    ).then_inc(slope_ready, 1)
                            dve.wait_ge(slope_ready, n)

            group_round(0)
            with dve.Fori(1, KV) as n:
                group_round(n)
            group_round(KV, own=False)
            gather(ET // 2, TQ)
            out_projection(BASE_OUT_B, KT, META, TQ)
            add_pair(BASE_OUT_B, KT, D // 256 - 1, 2, META, TQ)
            root_dve(dve, 2, TQ)
            for f in range(KT):
                if f >= 4 and f % 2 == 0:
                    dve.wait_ge(y_stored[f // 2 % 2], 16 * (f // 4))
                nc.vector.scalar_tensor_tensor(yst[:, f % 4], xT[:, f, META:T], vec[:, VF + f:VF + f + 1], rstd[:, 0:TQ],
                                               ALU.mult, ALU.mult).then_inc(y_ready, 1)

        @block.tensor
        def _(pe):
            pe.wait_ge(t1_loaded, 16)
            for ft in range(KT):
                sum_square(pe, sq, ft, 0, ft % 2, T, ft == 0, ft == KT - 1)

            def levels(h, i):
                if i == 0:
                    pe.wait_ge(lev_mul, LEVELS * h + 3)
                    pe.wait_ge(lev_copied, LEVELS * h + 3)
                    if not early(h, 1):
                        pe.wait_ge(st_added, 4 * h)
                        pe.wait_ge(sp_copied, h)
                    cols = slice(2 * P, T)
                    for k, l in enumerate([3, 2, 1, 0, None]):
                        lhs, rhs = (ks, qs) if l is None else (kr[l], qc[l])
                        done = nc.tensor.matmul(RT[0:TAIL, k * TAIL:k * TAIL + TAIL], lhs[:, cols], rhs[:, cols],
                                                start=True, stop=True)
                    done.then_inc(lev_done, 1)
                else:
                    pe.wait_ge(lev_mul, LEVELS * h + LEVELS - 1)
                    pe.wait_ge(lev_copied, LEVELS * h + LEVELS - 1)
                    cols = slice((i - 1) * P, i * P)
                    for b, bank in ((0, RA0), (1, RA1)):
                        if i == 1:
                            if not early(h, 1):
                                pe.wait_ge(og_ready, h)
                        else:
                            pe.wait_ge(masked_ready, 5 * h + 2 + b)
                        for k, l in enumerate([6, 5, 4, 3] if b == 0 else [2, 1, 0, None]):
                            lhs, rhs = (ks, qs) if l is None else (kr[l], qc[l])
                            done = nc.tensor.matmul(bank[:, k * P:k * P + P], lhs[:, cols], rhs[:, cols],
                                                    start=True, stop=True)
                        done.then_inc(lev_done, 1)

            def cross(h):
                pe.wait_ge(kx_ready, h + 1)
                pe.wait_ge(lev_mul, LEVELS * (h + 1))
                pe.wait_ge(lev_copied, LEVELS * (h + 1))
                if not early(h, 1):
                    pe.wait_ge(og_ready, h)
                nc.tensor.matmul(RO[:, 0:P], kr[7][:, 0:P], qc[7][:, P:2 * P], start=True, stop=True)
                nc.tensor.matmul(RO[:, P:P + TAILP], kx[:], qc[4][:, 2 * P:TP], start=True, stop=True)
                nc.tensor.matmul(RO[:, P + TAILP:P + 2 * TAILP], kr[7][:, P:2 * P], qc[4][:, 2 * P:TP],
                                 start=True, stop=True).then_inc(cross_done, 1)
                pe.wait_ge(kf_ready, h + 1)
                pe.wait_ge(kft_copied, h + 1)
                pe.wait_ge(masked_ready, 5 * h + 1)
                nc.tensor.transpose(RT[:, 0:P], kf[:, 0:P], ident)
                nc.tensor.transpose(RT[:, P:2 * P], kf[:, P:2 * P], ident)
                nc.tensor.transpose(RT[0:TAIL, 2 * P:3 * P], kf[:, 2 * P:T], ident).then_inc(kfT_done, 1)

            def values(h):
                pe.wait_ge(i_copied, h + 1)
                pe.wait_ge(masked_ready, 5 * h + 5)
                for i in range(2):
                    for e in range(2):
                        done = nc.tensor.transpose(RA0[:, i * DV + e * P:i * DV + e * P + P], iT[:, e, i * P:i * P + P], ident)
                done.then_inc(vT_done, 1)
                for e in range(2):
                    done = nc.tensor.transpose(RA1[0:TAIL, e * P:e * P + P], iT[:, e, 2 * P:T], ident)
                done.then_inc(vT_done, 1)

            def head_outputs(h):
                pe.wait_ge(v_copied, h + 1)
                pe.wait_ge(att_ready, 3 * (h + 1))
                pe.wait_ge(cross_copied, h + 1)
                nc.tensor.matmul(RO[:, 0:DV], att[:, 0], V[:, 0], start=True, stop=True)
                nc.tensor.matmul(RO[:, DV:2 * DV], att[:, 2], V[:, 0], start=True, stop=False)
                nc.tensor.matmul(RO[:, DV:2 * DV], att[:, 1], V[:, 1], start=False, stop=True).then_inc(o_done, 1)
                out = RA1[0:TAIL, 0:DV]
                nc.tensor.matmul(out, att[0:TAIL, 3, 0:TAIL], V[0:TAIL, 2], start=True, stop=False)
                nc.tensor.matmul(out, attX[:, 0], V[:, 0], start=False, stop=False)
                nc.tensor.matmul(out, attX[:, 1], V[:, 1], start=False, stop=False)
                pe.wait_ge(s0_loaded, 16 * (h + 1))
                pe.wait_ge(Qs_ready, h + 1)
                for b in range(NB):
                    done = nc.tensor.matmul(out, Qs[:, TAIL * b:TAIL * b + TAIL], S0[:, b], start=False, stop=b == NB - 1)
                done.then_inc(o_done, 1)

            def states(t, k):
                bank = RT if k % 2 == 0 else RA0
                if k == 0:
                    pe.wait_ge(kt_copied, t + 1)
                    pe.wait_ge(kts_ready, t + 1)
                    nc.tensor.matmul(bank[:, 0:DV], kt[:, 0], V[:, 0], start=True, stop=False)
                    nc.tensor.matmul(bank[:, 0:DV], kt[:, 1], V[:, 1], start=False, stop=False)
                    nc.tensor.matmul(bank[:, 0:DV], kts[0:TAIL, 0], V[0:TAIL, 2], start=False, stop=True).then_inc(st_done, 1)
                    return
                if k == 2:
                    pe.wait_ge(sp_copied, t + 1)
                if k > 2:
                    pe.wait_ge(st_added, 4 * t + k - 2)
                for i in range(2):
                    done = nc.tensor.matmul(bank[:, i * DV:i * DV + DV], kts[0:TAIL, 2 * k - 1 + i], V[0:TAIL, 2],
                                            start=True, stop=True)
                done.then_inc(st_done, 1)

            def turn_back(t):
                pe.wait_ge(on_ready, t + 1)
                for e, bank in ((0, RO), (1, RA1)):
                    for i, m in ((0, P), (1, P), (2, TAIL)):
                        done = nc.tensor.transpose(bank[:, i * P:i * P + m], on[0:m, i, e * P:e * P + P], ident[0:m, 0:m])
                done.then_inc(oT_done, 1)

            def head_round(h):
                t = h - 1
                for s in range(SLABS_H):
                    if s == 0 and not early(h, 1):
                        pe.wait_ge(g_ready, h)
                    if s == 4 and not early(h, 1):
                        pe.wait_ge(i_copied, h)
                    if s == 8:
                        pe.wait_ge(qs_ready, h + 1)
                        pe.wait_ge(fk_ready, h + 1)
                    if early(h, 1) and s < 4:
                        pe.wait_ge(xl_ready, 4 * s + 4)
                    products(pe, SLABS_H * h + s, s, 4 * (s % 4), 2 * (s // 4 % 2), xnH, xnL, T, s % 4 == 0, s % 4 == 3)
                    if not early(h, 1):
                        if s in (0, 1):
                            states(t, 2 * s)
                            states(t, 2 * s + 1)
                        if s == 2:
                            states(t, 4)
                        if s == 3:
                            turn_back(t)
                    if s in (6, 7, 8):
                        levels(h, s - 6)
                    if s == 9:
                        cross(h)
                    if s == 10:
                        values(h)
                    if s == 11:
                        head_outputs(h)

            head_round(0)
            with pe.Fori(1, H) as h:
                head_round(h)
            for k in range(5):
                states(H - 1, k)
            turn_back(H - 1)

            def out_projection(base, before, made, n):
                def sums(j, first):
                    for e in range(2):
                        at = before + KT + 2 * j + e
                        pe.wait_ge(sq_ready, at + 1)
                        nc.tensor.matmul(RA0[:, 0:n], ones, sqo[:, e, 0:n], start=first and e == 0, stop=False,
                                         skip_group_check=True).then_inc(sq_used, 1)

                def out_round(j, par):
                    for s in range(SLABS_OUT):
                        if early(j, 1):
                            pe.wait_ge(ogl_ready, made + 2 * s + 2)
                        if s == 0 and not early(j, 2):
                            pe.wait_ge(x_added, before // 2 + j - 1)
                        products(pe, base + SLABS_OUT * j + s, s, SLAB * s, 2 * par, ogH, ogL, n, s == 0, s == SLABS_OUT - 1)
                        if s == 3 and not early(j, 1):
                            sums(j - 1, early(j, 2))
                out_round(0, 0)
                out_round(1, 1)
                with pe.Fori(2, D // 256, 2) as j:
                    out_round(j, 0)
                    out_round(j + 1, 1)
                sums(D // 256 - 1, False)

            pe.wait_ge(g_ready, H)
            out_projection(BASE_OUT_A, 0, 0, T)

            for s in range(SLABS_KV):
                if s == 0:
                    pe.wait_ge(x_added, 7)
                if s == 4:
                    pe.wait_ge(x_added, 8)
                if s in (8, 12):
                    pe.wait_ge(k_copied, s // 4 - 1)
                if s < 4:
                    pe.wait_ge(xl_ready, KT + 4 * s + 4)
                products(pe, BASE_KV + s, s, 4 * (s % 4), 2 * (s // 4 % 2), xkH, xkL, T, s % 4 == 0, s % 4 == 3)
            pe.wait_ge(vt_copied, 2)
            pe.wait_ge(ms_ready, 2)
            for bank, a, b in ((RA0, 0, META), (RA1, META, META + P), (RO, META + P, TP), (RT, TP, T)):
                for j in range(4):
                    done = nc.tensor.transpose(bank[0:b - a, j * P:j * P + P], vT[:, j, a:b], ident)
                done.then_inc(vtok_done, 1)

            def score_products(n, u):
                k = UNITS * n + u
                bank = RA0 if u % 2 == 0 else RA1
                if u == 0:
                    pe.wait_ge(staged, n + 1)
                    pe.wait_ge(q_copied, 2 * n + 1)
                    if early(n, 1):
                        pe.wait_ge(vtok_copied, 4)
                if u == 4:
                    pe.wait_ge(q_copied, 2 * n + 2)
                if not early(k, 2):
                    pe.wait_ge(biased, k - 1)
                if u < G:
                    half = slice(64 * (u % 2), 64 * (u % 2) + 64)
                    nc.tensor.matmul(bank[:, 0:NKEYS], qT[half, u // 2, 0:P], kg[half, 0:NKEYS], start=True, stop=True)
                    nc.tensor.matmul(bank[:, NKEYS:SC], qT[half, u // 2, P:2 * P], kg[half, META:TP], start=True, stop=True
                                     ).then_inc(qk_done, 1)
                    return
                if u == G:
                    pe.wait_ge(ck_loaded, 32 * (n + 1))
                    pe.wait_ge(qsam_ready, n + 1)
                half = slice(64 * (u - G), 64 * (u - G) + 64)
                for four in range(2):
                    first = 4 * four
                    nc.tensor.matmul(bank[:, four * SS + WIN:four * SS + SS], qsam[half, first:first + 4].rearrange("p b w t -> p (b w t)"),
                                     kg[half, TP:T], start=True, stop=True)
                    for j in range(4):
                        done = nc.tensor.matmul(bank[32 * j:32 * j + 32, four * SS:four * SS + WIN],
                                                qsam[half, first + j].rearrange("p w t -> p (w t)"),
                                                ckT[half, first + j], start=True, stop=True)
                done.then_inc(qk_done, 1)

            def turn_p(n, u):
                k, r = UNITS * n + u, u % 2
                pe.wait_ge(p_ready, k + 1)
                if not early(k, 1):
                    pe.wait_ge(pt_copied, k)
                if u < G:
                    nc.tensor.transpose(RT[0:META, 0:P], sc[:, r, 0:META], ident)
                    for i in range(3):
                        a = META + i * P
                        done = nc.tensor.transpose(RT[:, P + i * P:2 * P + i * P], sc[:, r, a:a + P], ident)
                else:
                    for four in range(2):
                        nc.tensor.transpose(RT[:, four * 2 * P:four * 2 * P + P], sc[:, r, four * SS:four * SS + WIN], ident)
                        done = nc.tensor.transpose(RT[0:NB * TS, four * 2 * P + P:four * 2 * P + 2 * P],
                                                   sc[:, r, four * SS + WIN:four * SS + SS], ident)
                done.then_inc(tr_done, 1)

            def value_products(n, u):
                k, r = UNITS * n + u, u % 2
                pe.wait_ge(pt_copied, k + 1)
                if u == 0 and not early(n, 1):
                    pe.wait_ge(o_copied, 5 * n)
                if u in (2, 4, 6, 8):
                    pe.wait_ge(o_copied, 5 * n + u // 2)
                if u < G:
                    half = slice(64 * (u % 2), 64 * (u % 2) + 64)
                    nc.tensor.matmul(RO[half, 0:P], vg[0:META, 0], pT[0:META, r, 0:P], start=True, stop=False)
                    nc.tensor.matmul(RO[half, 0:P], vg[:, 1], pT[:, r, P:2 * P], start=False, stop=True)
                    nc.tensor.matmul(RO[half, P:2 * P], vg[:, 1], pT[:, r, 2 * P:3 * P], start=True, stop=False)
                    nc.tensor.matmul(RO[half, P:2 * P], vg[:, 2], pT[:, r, 3 * P:4 * P], start=False, stop=True
                                     ).then_inc(pv_done, 1)
                    return
                half = slice(64 * (u - G), 64 * (u - G) + 64)
                for four in range(2):
                    c0, p0 = four * P, four * 2 * P
                    for j in range(4):
                        out, p = RO[half, c0 + 32 * j:c0 + 32 * j + 32], p0 + 32 * j
                        nc.tensor.matmul(out, cv[:, 4 * four + j], pT[:, r, p:p + 32], start=True, stop=False)
                        done = nc.tensor.matmul(out, vg[0:NB * TS, 3], pT[0:NB * TS, r, p + P:p + P + 32],
                                                start=False, stop=True)
                done.then_inc(pv_done, 1)

            def group_round(n, own=True):
                for s in range(SLABS_G if own else 4):
                    if own:
                        if s in (0, 4) and not early(n, 1):
                            if s == 0:
                                pe.wait_ge(g0_copied, n)
                            else:
                                pe.wait_ge(gb_ready, n)
                        if s in (8, 12):
                            pe.wait_ge(q_copied, 2 * n + s // 4 - 1)
                        if early(n, 1) and s < 4:
                            pe.wait_ge(xl_ready, 2 * KT + 4 * s + 4)
                        products(pe, BASE_B + SLABS_G * n + s, s, 4 * (s % 4), 2 * (s // 4 % 2), xkH, xkL, TQ,
                                 s % 4 == 0, s % 4 == 3)
                    for u in range(UNITS):
                        for at, what in ((10 + u, value_products), (8 + u, turn_p), (5 + u, score_products)):
                            if at == s and own:
                                what(n, u)
                            if at == s + SLABS_G and not early(n, 1):
                                what(n - 1, u)

            group_round(0)
            with pe.Fori(1, KV) as n:
                group_round(n)
            group_round(KV, own=False)
            pe.wait_ge(g0_copied, KV)
            pe.wait_ge(gb_ready, KV)
            out_projection(BASE_OUT_B, KT, ET // 2, TQ)


_OUTS = [("y", (KT, P, TQ)), ("st_prompt", (H, P, DV)), ("st_sample", (H, P, NB * DV)), ("k", (4, P, T)),
         ("v", (4, P, T)), ("ck_old", (NB, WIN - TS, KV * HD)), ("cv_old", (NB, WIN - TS, KV * HD))]


def slabs(w):
    k, n = w.shape
    return w.reshape(k // (SLAB * P), SLAB, P, n // 256, 256).transpose(3, 0, 2, 1, 4).reshape(-1, P, SLAB_W)


def kernel(x_prompt, x_sample, state_hgrn, cache_k, cache_v, meta_tokens, norm_a, w_in_a, lb_a, onorm_a,
           w_out_a, norm_kv, w_kv, norm_b, w_in_b, sink_b, w_out_b, norm_f):
    import concourse.bacc as bacc
    from concourse.bass_utils import run_bass_kernel_spmd

    f32 = np.float32
    arr = [np.asarray(a) for a in (x_prompt, x_sample, state_hgrn, cache_k, cache_v, meta_tokens, norm_a, w_in_a,
                                   onorm_a, w_out_a, norm_kv, w_kv, norm_b, w_in_b, sink_b, w_out_b, norm_f)]
    xp, xs, st, ck, cv, meta, na, wa, on, woa, nkv, wkv, nb, wb, sink, wob, nf = arr
    x = np.concatenate([meta, xp[0], xs.reshape(NB * TS, D)], axis=0)
    x_in = x.T.reshape(KT, P, T).transpose(1, 0, 2).reshape(P, KT * T)
    q, f, i, g = np.split(wa[0], [D, 2 * D, 4 * D], axis=1)
    heads = []
    for h in range(H):
        qf = np.concatenate([q[:, h * P:h * P + P], f[:, h * P:h * P + P]], axis=1)
        heads += [qf, i[:, h * DV:h * DV + DV], g[:, h * DV:h * DV + DV]]
    qb, gb = np.split(wb[0], 2, axis=1)
    groups = []
    for n in range(KV):
        groups += [qb[:, n * 512:n * 512 + 512], gb[:, n * 512:n * 512 + 512]]
    w_in = np.concatenate([slabs(w) for w in heads + [woa[0], wkv] + groups + [wob[0]]], axis=0)
    assert w_in.shape[0] == N_SLABS
    s0_in = st[0].transpose(1, 2, 0, 3).reshape(H, P, NB * DV)
    ckd = ck.transpose(2, 3, 0, 1).reshape(KV, HD, NB * WIN)
    ckd = np.concatenate([ckd, ckd], axis=1)
    cvd = cv.transpose(2, 1, 0, 3).reshape(KV, WIN, NB * HD)
    vec = np.concatenate([a.reshape(-1, P).T for a in (na[0], nkv, nb[0], nf, on[0])], axis=1)
    row = np.arange(P) // 8 % 4
    by_head = np.broadcast_to(sink[0].reshape(1, KV, G), (P, KV, G))
    by_row = np.stack([sink[0].reshape(KV, G)[:, 2 * row + par] for par in range(2)], axis=-1).transpose(1, 0, 2)
    sinks = np.concatenate([by_head, by_row], axis=2).reshape(P, KV * (G + 2))
    t1, t2 = tables()

    nc = bacc.Bacc("TRN2", target_bir_lowering=False, num_devices=1)
    feeds, aps = {}, []
    for name, a in (("x", x_in), ("w", w_in), ("s0", s0_in), ("ck", ckd), ("cv", cvd), ("vec", vec), ("sinks", sinks),
                    ("t1", t1), ("t2", t2), ("ck_rest", ck[:, TS:].reshape(NB, WIN - TS, KV * HD)),
                    ("cv_rest", cv[:, TS:].reshape(NB, WIN - TS, KV * HD))):
        a = np.ascontiguousarray(a)
        feeds["in_" + name] = a
        aps.append(nc.dram_tensor("in_" + name, a.shape, mybir.dt.from_np(a.dtype), kind="ExternalInput").ap())
    outs = [nc.dram_tensor("out_" + name, shape, F32, kind="ExternalOutput").ap() for name, shape in _OUTS]
    x_d, w_d, s0_d, ck_d, cv_d, vec_d, sink_d, t1_d, t2_d, ckr_d, cvr_d = aps
    trunk(nc, x_d, w_d, s0_d, cv_d, ck_d, vec_d, sink_d, t1_d, t2_d, ckr_d, cvr_d, *outs)
    r = run_bass_kernel_spmd(nc, [feeds], core_ids=[0]).results[0]
    y, sp, ss, k, v, ck_old, cv_old = (np.asarray(r["out_" + name]) for name, _ in _OUTS)
    y = y.reshape(D, TQ).T
    k, v = (a.reshape(KV * HD, T).T for a in (k, v))

    def window(old, new):
        return np.concatenate([old.reshape(NB, WIN - TS, KV, HD), new[TP:].reshape(NB, TS, KV, HD)], axis=1)
    return (y[:SEQ].reshape(1, SEQ, D), y[SEQ:].reshape(NB, TS, D), sp.reshape(1, 1, H, P, DV),
            k[TP - WIN:TP].reshape(1, WIN, KV, HD), v[TP - WIN:TP].reshape(1, WIN, KV, HD),
            ss.reshape(H, P, NB, DV).transpose(2, 0, 1, 3)[None], window(ck_old, k), window(cv_old, v))
```

```python
import numpy as np
import concourse.bass as bass
from concourse import mybir
from contextlib import ExitStack

F32 = mybir.dt.float32
F32R = mybir.dt.float32r
ACT = mybir.ActivationFunctionType
ALU = mybir.AluOpType
AX = mybir.AxisListType

P = 128
D = 2048
META, SEQ, NB, TS = 16, 256, 8, 8
TP = META + SEQ
T = TP + NB * TS
TQ = T - META
KT = D // P
H = 16
DV = 256
ET = 2 * KT
KV, G, HD = 8, 8, 64
WIN = 128
EPS = 1e-6
BIG = 1e30

SLAB = 4
SLAB_W = SLAB * 256
RING = 4
SLABS_H = 3 * KT // SLAB
SLABS_OUT = ET // SLAB
SLABS_KV = 4 * KT // SLAB
SLABS_G = 4 * KT // SLAB
BASE_OUT_A = H * SLABS_H
BASE_KV = BASE_OUT_A + (D // 256) * SLABS_OUT
BASE_B = BASE_KV + SLABS_KV
BASE_OUT_B = BASE_B + KV * SLABS_G
N_SLABS = BASE_OUT_B + (D // 256) * SLABS_OUT

TAIL = T - 2 * P
TAILP = TP - 2 * P
LEVELS = 7
LV_TOKENS = [T, T, T, TP, 2 * P, 2 * P, 2 * P]
TOT_LEN = [T, T // 2, T // 4, T // 8, TP // 16, 2 * P // 32, 2 * P // 64, 2]
TOT_AT = [0] + [sum(TOT_LEN[1:l]) for l in range(1, LEVELS + 1)]
TOT_N = sum(TOT_LEN[1:])
QS_W = TAIL + TS
UNITS = G + 2
SCORES = 5
NKEYS = META + P
SC = NKEYS + 2 * P
SS = WIN + NB * TS

C_MASK = 0
C_MASK3 = C_MASK + (LEVELS + 1) * P
C_ROWS = C_MASK3 + 5 * TAIL
C_IDENT = C_ROWS + NB + 1
C_ONES = C_IDENT + P
C_ALL1 = C_ONES + P
C_DIST = 0
C_DIST_S = C_DIST + SC
C_SLOPE = C_DIST_S + 2 * SS
C_SLOPE_S = C_SLOPE + G
C_ALL2 = C_SLOPE_S + 2
UNUSED = 2 * KT * T - (2 * T + KV * T + C_ALL2 + KV * (G + 2) + 16 * P + NB * WIN + T + 4 * TQ + 4 * NB * TS + G + 2)


def tables():
    t1 = np.zeros((P, C_ALL1), np.float32)
    s, t = np.arange(P)[:, None], np.arange(P)[None, :]
    for n, l in enumerate([6, 5, 4, 3, 2, 1, 0]):
        t1[:, C_MASK + n * P:C_MASK + (n + 1) * P] = ((s ^ t) >> l == 1) & (t > s)
    t1[:, C_MASK + LEVELS * P:C_MASK + (LEVELS + 1) * P] = s == t
    s, t = np.arange(TAIL)[:, None], np.arange(TAIL)[None, :]
    for n, l in enumerate([3, 2, 1, 0]):
        own = (s < TAILP) & (t < TAILP) if l == 3 else True
        t1[:TAIL, C_MASK3 + n * TAIL:C_MASK3 + (n + 1) * TAIL] = ((s ^ t) >> l == 1) & (t > s) & own
    t1[:TAIL, C_MASK3 + 4 * TAIL:C_MASK3 + 5 * TAIL] = s == t
    t1[:TAILP, C_ROWS] = 1.0
    for b in range(NB):
        t1[TAILP + b * TS:TAILP + (b + 1) * TS, C_ROWS + 1 + b] = 1.0
    t1[:, C_IDENT:C_IDENT + P] = np.eye(P)
    t1[:, C_ONES:C_ONES + P] = 1.0

    t2 = np.zeros((P, C_ALL2), np.float32)
    i = np.arange(P)[:, None]
    for at, q0, k0, n in ((C_DIST, META, 0, NKEYS), (C_DIST + NKEYS, META + P, META, 2 * P)):
        d = (q0 + i) - (k0 + np.arange(n)[None, :])
        t2[:, at:at + n] = np.where((d >= 0) & (d < WIN), -d, -BIG)
    row = np.arange(P)
    seq, u, tok = row // 32, row // 8 % 4, row % 8
    for half in range(2):
        at = C_DIST_S + half * SS
        d = WIN + tok[:, None] - np.arange(WIN)[None, :]
        t2[:, at:at + WIN] = np.where(d < WIN, -d, -BIG)
        new = np.arange(NB * TS)[None, :]
        d = tok[:, None] - new % TS
        own = (new // TS == 4 * half + seq[:, None]) & (d >= 0)
        t2[:, at + WIN:at + SS] = np.where(own, -d, -BIG)
    for g in range(G):
        t2[:, C_SLOPE + g] = 8.0 * 2.0 ** (-(g + 1) / 8.0)
    for par in range(2):
        t2[:, C_SLOPE_S + par] = 8.0 * 2.0 ** (-(2 * u + par + 1) / 8.0)
    return t1, t2


def trunk(nc, x_in, w_in, s0_in, cv_in, ckd_in, vec_in, sink_in, t1_in, t2_in, ckold_in, cvold_in,
          y_out, st_prompt, st_sample, k_out, v_out, ckold_out, cvold_out):
    stack = ExitStack()

    def sb(name, shape, dt=F32, scope=None):
        return (scope or stack).enter_context(nc.sbuf_tensor(name, shape, dt))

    def sem(name):
        return stack.enter_context(nc.semaphore(name))

    with stack:
        raw = sb("raw", [P, RING, SLAB, 256])
        split = sb("split", [P, RING, 2, SLAB, 256], F32R)
        t1 = sb("t1", [P, C_ALL1])
        vec = sb("vec", [P, 4 * KT + 2])
        rstd = sb("rstd", [P, T])
        xT = sb("xT", [P, KT, T])
        ogin = sb("ogin", [P, 4, 2, T])
        sqo, sqsum = sb("sqo", [P, 2, T]), sb("sqsum", [P, 2, T])
        VA, VKV, VB, VF, VO = 0, KT, 2 * KT, 3 * KT, 4 * KT
        ident, ones = t1[:, C_IDENT:C_IDENT + P], t1[:, C_ONES:C_ONES + P]

        s1 = stack.enter_context(ExitStack())
        xnH, xnL = sb("xnH", [P, KT, T], F32R, s1), sb("xnL", [P, KT, T], F32R, s1)
        xn = sb("xn", [P, 2, T], F32, s1)
        qs, fs, ks, sigq = (sb(n, [P, T], F32, s1) for n in ("qs", "fs", "ks", "sigq"))
        qc = [sb(f"qc{l}", [P, T if l < 4 else TP], F32, s1) for l in range(LEVELS + 1)]
        kr = [ks] + [sb(f"kr{l}", [P, T if l < 4 else TP], F32, s1) for l in range(1, LEVELS + 1)]
        tot_all = sb("tot_all", [P, TOT_N], F32, s1)
        tot = [fs] + [tot_all[:, TOT_AT[l]:TOT_AT[l] + TOT_LEN[l]] for l in range(1, LEVELS + 1)]
        kx, kf = sb("kx", [P, P], F32, s1), sb("kf", [P, T], F32, s1)
        iT = sb("iT", [P, 2, T], F32, s1)
        V = sb("V", [P, 3, DV], F32, s1)
        masked = sb("masked", [P, 8 * P], F32, s1)
        att = sb("att", [P, 4, P], F32, s1)
        attX = sb("attX", [P, 2, TAIL], F32, s1)
        kt, kts = sb("kt", [P, 3, P], F32, s1), sb("kts", [P, NB + 1, P], F32, s1)
        Qs = sb("Qs", [P, TAILP + NB * QS_W], F32, s1)
        S0 = sb("S0", [P, NB, DV], F32, s1)
        Sp = sb("Sp", [P, DV], F32, s1)
        on = sb("on", [P, 3, DV], F32, s1)
        junk = sb("junk", [P, 3, DV], F32, s1)
        ssq, rs3 = sb("ssq", [P, 3], F32, s1), sb("rs3", [P, 3], F32, s1)
        ms3, norm_const = sb("ms3", [P, 2, 3], F32, s1), sb("norm_const", [P, 3, 3], F32, s1)
        sg, gs, og = (sb(n, [P, 2, T], F32, s1) for n in ("sg", "gs", "og"))
        sq_sum4, sq_new = ogin[:, 0:2].rearrange("p a b t -> p (a b) t"), ogin[:, 2:4].rearrange("p a b t -> p (a b) t")
        sq_new4 = [sq_new, S0[:].rearrange("p b e -> p (b e)")[:, 0:4 * T].rearrange("p (a t) -> p a t", a=4)]
        s1.close()

        s2 = stack.enter_context(ExitStack())
        ogH0, ogL0, ogH1, ogL1 = (sb(n, [P, KT, T], F32R, s2) for n in ("ogH0", "ogL0", "ogH1", "ogL1"))
        ogH, ogL = [ogH0, ogH1], [ogL0, ogL1]
        yst = sb("yst", [P, 4, TQ], F32, s2)
        s2.close()

        s3 = stack.enter_context(ExitStack())
        xkH, xkL = sb("xkH", [P, KT, T], F32R, s3), sb("xkL", [P, KT, T], F32R, s3)
        xk = sb("xk", [P, 2, T], F32, s3)
        kT = sb("kT", [P, KV, T], F32, s3)
        t2 = sb("t2", [P, C_ALL2], F32, s3)
        sinks = sb("sinks", [P, KV, G + 2], F32, s3)
        vtok = sb("vtok", [P, 4, 4 * P], F32, s3)
        ckT, kg = sb("ckT", [P, NB, WIN], F32, s3), sb("kg", [P, T], F32, s3)
        qT, qsam = sb("qT", [P, 4, TQ], F32, s3), sb("qsam", [P, NB, 4, TS], F32, s3)
        sinkg = sb("sinkg", [P, G + 2], F32, s3)
        sb("unused", [P, UNUSED], F32, s3)
        vT, ktmp = sb("vT", [P, 4, T], F32, s3), sb("ktmp", [P, 4, T], F32, s3)
        sgb, ob = vT[:, :, 0:TQ], ktmp[:, :, 0:TQ]
        cv, vg = sb("cv", [P, NB, HD], F32, s3), sb("vg", [P, 4, HD], F32, s3)
        sc, pT = sb("sc", [P, SCORES, SC], F32, s3), sb("pT", [P, 2, 4 * P], F32, s3)
        stat = sb("stat", [P, SCORES, 7, 2], F32, s3)
        gate = sb("gate", [P, 4, TQ], F32, s3)
        s3.close()

        pz = stack.enter_context(nc.psum_tensor("pz", [P, 4, 512], F32))
        RA0, RA1, RO, RT = (stack.enter_context(nc.psum_tensor(n, [P, 512], F32))
                            for n in ("RA0", "RA1", "RO", "RT"))
        scratch = nc.dram_tensor("og_scratch", [ET, P, T], F32, kind="Internal").ap()

        w_loaded = [sem(f"w_loaded{i}") for i in range(RING)]
        (w_hi, w_lo, mm_done, t1_loaded, vec_loaded, s0_loaded, t2_loaded, sink_loaded,
         sq_ready, sq_used, ms_ready, root_ready, rstd_ready, xn_ready, xh_ready, xl_ready,
         sigq_ready, fk_ready, qs_ready, qc0_ready, lev_mul, lev_copied, kx_ready, kf_ready,
         kft_copied, Qs_ready, zeroed, i_copied, lev_done, masked_ready, att_ready, cross_done,
         cross_copied, kfT_done, kt_copied, kts_ready, vT_done, v_copied, o_done, ssq_ready,
         ms3_ready, rs3_ready, on_ready, s0_scaled, st_done, sp_copied, st_added, g_sig, g_ready,
         oT_done, og_ready, og_stored, st_stored, sp_stored) = (sem(n) for n in (
            "w_hi", "w_lo", "mm_done", "t1_loaded", "vec_loaded", "s0_loaded", "t2_loaded",
            "sink_loaded", "sq_ready", "sq_used", "ms_ready", "root_ready", "rstd_ready", "xn_ready",
            "xh_ready", "xl_ready", "sigq_ready", "fk_ready", "qs_ready", "qc0_ready", "lev_mul",
            "lev_copied", "kx_ready", "kf_ready", "kft_copied", "Qs_ready", "zeroed", "i_copied",
            "lev_done", "masked_ready", "att_ready", "cross_done", "cross_copied", "kfT_done",
            "kt_copied", "kts_ready", "vT_done", "v_copied", "o_done", "ssq_ready", "ms3_ready",
            "rs3_ready", "on_ready", "s0_scaled", "st_done", "sp_copied", "st_added", "g_sig",
            "g_ready", "oT_done", "og_ready", "og_stored", "st_stored", "sp_stored"))
        x_loaded = [sem(f"x_loaded{i}") for i in range(4)]
        og_loaded = [sem(f"og_loaded{i}") for i in range(4)]
        y_stored = [sem(f"y_stored{i}") for i in range(2)]
        (ogh_ready, ogl_ready, x_added, k_copied, k_spread, kv_stored, vtok_done, vtok_copied,
         sinks_ready, staged, ck_loaded, q_copied, qk_done, biased, max_ready, mm_ready, sm_ready,
         exp_ready, den_ready, rden_ready, p_ready, tr_done, pt_copied, pv_done, o_copied,
         g0_copied, gb_sig, gb_ready, ob_ready, slope_ready, y_ready, old_stored, vt_copied,
         obg_stored, qsam_ready, v_staged, ones_loaded, sq_made, sq_added,
         sqo_ready, sqsum_ready) = (sem(n) for n in (
            "ogh_ready", "ogl_ready", "x_added", "k_copied", "k_spread", "kv_stored", "vtok_done",
            "vtok_copied", "sinks_ready", "staged", "ck_loaded", "q_copied", "qk_done", "biased",
            "max_ready", "mm_ready", "sm_ready", "exp_ready", "den_ready", "rden_ready", "p_ready",
            "tr_done", "pt_copied", "pv_done", "o_copied", "g0_copied", "gb_sig", "gb_ready",
            "ob_ready", "slope_ready", "y_ready", "old_stored", "vt_copied", "obg_stored",
            "qsam_ready", "v_staged", "ones_loaded", "sq_made", "sq_added",
            "sqo_ready", "sqsum_ready"))

        def early(x, limit):
            return isinstance(x, int) and x < limit

        def load_slab(sp, g, s):
            if not early(g, RING):
                sp.wait_ge(w_lo, g - RING + 1)
            sp.dma_start(raw[:, s % RING], w_in[bass.ds(g, 1)].rearrange("a p n -> p (a n)")
                         ).then_inc(w_loaded[s % RING], 16)

        def split_hi(act, g, s, turn):
            act.wait_ge(w_loaded[s % RING], 16 * (turn + 1))
            if not early(g, RING):
                act.wait_ge(mm_done, g - RING + 1)
            nc.scalar.activation(split[:, s % RING, 0], raw[:, s % RING], ACT.Copy).then_inc(w_hi, 1)

        def split_lo(dve, g, s):
            dve.wait_ge(w_hi, g + 1)
            nc.vector.tensor_tensor(split[:, s % RING, 1], raw[:, s % RING],
                                    split[:, s % RING, 0].bitcast(F32), ALU.subtract).then_inc(w_lo, 1)

        def products(pe, g, s, kt0, bank, high, low, n, first, last):
            pe.wait_ge(w_lo, g + 1)
            for k in range(SLAB):
                for half in range(2):
                    cols = slice(half * P, half * P + P)
                    out = pz[:, bank + half, 0:n]
                    wh, wl = split[:, s % RING, 0, k, cols], split[:, s % RING, 1, k, cols]
                    begin, end = first and k == 0, last and k == SLAB - 1
                    hi, lo = (x[(kt0 + k) // KT][:, (kt0 + k) % KT, 0:n] for x in (high, low))
                    nc.tensor.matmul(out, wh, hi, start=begin, stop=False)
                    nc.tensor.matmul(out, wh, lo, start=False, stop=False)
                    done = nc.tensor.matmul(out, wl, hi, start=False, stop=end)
            done.then_inc(mm_done, 1)

        def root_dve(dve, c, n):
            dve.wait_ge(sq_used, c + 1)
            nc.vector.tensor_scalar(rstd[:, 0:n], RA0[:, 0:n], 1.0 / D, EPS, ALU.mult, ALU.add).then_inc(ms_ready, 1)
            dve.wait_ge(root_ready, c + 1)
            nc.vector.reciprocal(rstd[:, 0:n], rstd[:, 0:n]).then_inc(rstd_ready, 1)
            dve.wait_ge(rstd_ready, c + 1)

        def root_act(act, c, n):
            act.wait_ge(ms_ready, c + 1)
            nc.scalar.activation(rstd[:, 0:n], rstd[:, 0:n], ACT.Sqrt).then_inc(root_ready, 1)

        def sums_before(c):
            return 1 + (D // 256 - 1) * (c - 1) if c else 0

        def sum_squares(pe, c, n):
            for buf in (sqsum, sqo) if c else (sqsum,):
                if buf is sqsum:
                    pe.wait_ge(sqsum_ready, sums_before(c + 1))
                else:
                    pe.wait_ge(sq_ready, c)
                for e in range(2):
                    done = nc.tensor.matmul(RA0[:, 0:n], ones, buf[:, e, 0:n], start=buf is sqsum and e == 0,
                                            stop=(buf is sqo or c == 0) and e == 1)
            done.then_inc(sq_used, 1)

        def scaled(dve, ft, slot, done, buf, gcol, c0, n):
            if not early(done, 2):
                dve.wait_ge(xl_ready, done - 1)
            nc.vector.scalar_tensor_tensor(buf[:, slot, 0:n], xT[:, ft, c0:c0 + n], vec[:, gcol + ft:gcol + ft + 1],
                                           rstd[:, c0:c0 + n], ALU.mult, ALU.mult).then_inc(xn_ready, 1)

        def scaled_hi(act, ft, slot, done, buf, high, n):
            act.wait_ge(xn_ready, done + 1)
            nc.scalar.activation(high[:, ft, 0:n], buf[:, slot, 0:n], ACT.Copy).then_inc(xh_ready, 1)

        def scaled_lo(dve, ft, slot, done, buf, high, low, n):
            dve.wait_ge(xh_ready, done + 1)
            nc.vector.tensor_tensor(low[:, ft, 0:n], buf[:, slot, 0:n], high[:, ft, 0:n].bitcast(F32),
                                    ALU.subtract).then_inc(xl_ready, 1)

        def normalise_dve(dve, made, buf, gcol, high, low, c0, n, tiles):
            for ft in tiles:
                scaled(dve, ft, ft % 2, made + ft, buf, gcol, c0, n)
                if ft % 2:
                    scaled_lo(dve, ft - 1, 0, made + ft - 1, buf, high, low, n)
                    scaled_lo(dve, ft, 1, made + ft, buf, high, low, n)

        def normalise_act(act, made, buf, high, n, tiles):
            for ft in tiles:
                scaled_hi(act, ft, ft % 2, made + ft, buf, high, n)

        def pair_source(held, c, n):
            return ogin[:, c % 4, :, 0:n] if c < ET // 2 - len(held) else held[c - ET // 2][:, :, 0:n]

        def pair(x, c, n):
            return x[2 * c // KT][:, 2 * c % KT:2 * c % KT + 2, 0:n]

        block = stack.enter_context(nc.Block())

        @block.sync
        def _(sp):
            for c in range(4):
                sp.dma_start(xT[:, 4 * c:4 * c + 4].rearrange("p a n -> p (a n)"), x_in[:, 4 * c * T:(4 * c + 4) * T]
                             ).then_inc(x_loaded[c], 16)

            def head_round(h):
                for s in range(SLABS_H):
                    load_slab(sp, SLABS_H * h + s, s)
                    if early(h, 1):
                        continue
                    if s == 10:
                        sp.wait_ge(st_added, 4 * h)
                        sp.dma_start(st_sample[bass.ds(h - 1, 1)].rearrange("a p n -> p (a n)"),
                                     S0[:].rearrange("p b e -> p (b e)")).then_inc(st_stored, 16)
                        sp.wait_ge(sp_copied, h)
                        sp.dma_start(st_prompt[bass.ds(h - 1, 1)].rearrange("a p n -> p (a n)"), Sp[:]
                                     ).then_inc(sp_stored, 16)
                    if s == 11:
                        sp.wait_ge(st_stored, 16 * h)
                        sp.dma_start(S0[:].rearrange("p b e -> p (b e)"),
                                     s0_in[bass.ds(h, 1)].rearrange("a p n -> p (a n)")).then_inc(s0_loaded, 16)
                        sp.wait_ge(og_ready, h)
                        sp.dma_start(scratch[bass.ds(2 * h - 2, 2)].rearrange("a p n -> p a n"), og[:]
                                     ).then_inc(og_stored, 16)

            head_round(0)
            with sp.Fori(1, H) as h:
                head_round(h)

            def load_pairs(before, pairs, n):
                for c in pairs:
                    if before + c >= 4:
                        sp.wait_ge(ogl_ready, before + c - 3)
                    sp.dma_start(ogin[:, c % 4, :, 0:n], scratch[2 * c:2 * c + 2, :, 0:n].rearrange("a p n -> p a n")
                                 ).then_inc(og_loaded[c % 4], 16)

            def first_out_rounds(base, before, held, n, finish):
                load_pairs(before, range(4), n)
                for s in range(2 * SLABS_OUT):
                    if s >= RING or base == BASE_OUT_A:
                        load_slab(sp, base + s, s)
                    if s >= 7:
                        load_pairs(before, range(min(2 * s - 10, ET // 2 - held), min(2 * s - 8, ET // 2 - held)), n)
                    if s == 10:
                        finish()

            def last_states():
                sp.wait_ge(st_added, 4 * H)
                sp.dma_start(st_sample[H - 1], S0[:].rearrange("p b e -> p (b e)")).then_inc(st_stored, 16)
                sp.wait_ge(sp_copied, H)
                sp.dma_start(st_prompt[H - 1], Sp[:]).then_inc(sp_stored, 16)

            sp.wait_ge(og_stored, 16 * (H - 1))
            first_out_rounds(BASE_OUT_A, 0, 1, T, last_states)
            with sp.Fori(2, D // 256) as j:
                for s in range(SLABS_OUT):
                    load_slab(sp, BASE_OUT_A + SLABS_OUT * j + s, s)

            for s in range(SLABS_KV):
                load_slab(sp, BASE_KV + s, s)
                if s == 4:
                    sp.wait_ge(mm_done, BASE_KV)
                    sp.dma_start(t2[:], t2_in).then_inc(t2_loaded, 16)
                    sp.dma_start(sinks[:].rearrange("p a b -> p (a b)"), sink_in).then_inc(sink_loaded, 16)
            for s in range(RING):
                load_slab(sp, BASE_B + s, s)
            sp.wait_ge(k_copied, 2)
            for src in range(2):
                for dst in range(2):
                    sp.dma_start(kT[64 * dst:64 * dst + 64].rearrange("p (j two) t -> p j two t", two=2)[:, :, src],
                                 ktmp[64 * src:64 * src + 64]).then_inc(k_spread, 16)
            sp.dma_start(k_out.rearrange("j p t -> p j t"), ktmp[:]).then_inc(kv_stored, 16)
            sp.wait_ge(vt_copied, 2)
            sp.dma_start(v_out.rearrange("j p t -> p j t"), vT[:]).then_inc(kv_stored, 16)
            sp.wait_ge(kv_stored, 32)

            def group_round(n):
                for s in range(SLABS_G):
                    if early(n, 1) and s < RING:
                        continue
                    load_slab(sp, BASE_B + SLABS_G * n + s, s)
                    if s == 10:
                        if not early(n, 1):
                            sp.wait_ge(pv_done, UNITS * n)
                        sp.dma_start(ckT[:].rearrange("p b j -> p (b j)"),
                                     ckd_in[bass.ds(n, 1)].rearrange("a p n -> p (a n)")).then_inc(ck_loaded, 16)
                        sp.dma_start(cv[:].rearrange("p b j -> p (b j)"),
                                     cv_in[bass.ds(n, 1)].rearrange("a p n -> p (a n)")).then_inc(ck_loaded, 16)
                    if s == 13 and not early(n, 1):
                        sp.wait_ge(ob_ready, n)
                        sp.dma_start(scratch[bass.ds(4 * n - 4, 4), :, 0:TQ].rearrange("a p n -> p a n"), gate[:]
                                     ).then_inc(obg_stored, 16)

            group_round(0)
            with sp.Fori(1, KV) as n:
                group_round(n)
            for s in range(RING):
                load_slab(sp, BASE_OUT_B + s, s)
            sp.wait_ge(obg_stored, 16 * (KV - 1))
            first_out_rounds(BASE_OUT_B, ET // 2, 2, TQ, lambda: None)
            with sp.Fori(2, D // 256) as j:
                for s in range(SLABS_OUT):
                    load_slab(sp, BASE_OUT_B + SLABS_OUT * j + s, s)
            for f in range(0, KT, 2):
                sp.wait_ge(y_ready, f + 2)
                i = f // 2 % 2
                sp.dma_start(y_out[f:f + 2].rearrange("a p n -> p a n"), yst[:, 2 * i:2 * i + 2]).then_inc(y_stored[i], 16)
            for i in range(2):
                sp.wait_ge(y_stored[i], 16 * KT // 4)
            sp.wait_ge(st_stored, 16 * H)
            sp.wait_ge(sp_stored, 16 * H)
            sp.wait_ge(kv_stored, 32)
            sp.wait_ge(obg_stored, 16 * (KV - 1))
            sp.wait_ge(old_stored, 32)

        @block.gpsimd
        def _(pool):
            nc.gpsimd.memset(Qs[:], 0.0)
            nc.gpsimd.memset(attX[:], 0.0)
            for i, value in enumerate((1.0 / DV, EPS, -0.5)):
                nc.gpsimd.memset(norm_const[:, i], value)
            nc.gpsimd.memset(ssq[:], 0.0).then_inc(zeroed, 1)
            pool.dma_start(ckold_out, ckold_in).then_inc(old_stored, 16)
            pool.dma_start(cvold_out, cvold_in).then_inc(old_stored, 16)
            pool.wait_ge(ones_loaded, 16)

            def keep(out, x):
                one = t1[0:x.shape[0], C_ONES:C_ONES + 1]
                for _ in range(len(x.shape) - 2):
                    one = one.unsqueeze(2)
                return nc.gpsimd.tensor_tensor(out, x, one.broadcast_to(list(x.shape)), ALU.mult)

            def tail(h):
                pool.wait_ge(ssq_ready, h + 1)
                nc.gpsimd.tensor_tensor(ms3[:, 0], ssq[:], norm_const[:, 0], ALU.mult).then_inc(ms3_ready, 1)
                pool.wait_ge(ms3_ready, 2 * h + 1)
                nc.gpsimd.tensor_tensor(ms3[:, 1], ms3[:, 0], norm_const[:, 1], ALU.add).then_inc(ms3_ready, 1)
                pool.wait_ge(ms3_ready, 2 * h + 2)
                nc.gpsimd.tensor_tensor(rs3[:], ms3[:, 1], norm_const[:, 2], ALU.pow).then_inc(rs3_ready, 1)

            def head(h):
                for l in range(LEVELS):
                    n, b = LV_TOKENS[l], 1 << l
                    if l == 0:
                        pool.wait_ge(qc0_ready, h + 1)
                    else:
                        pool.wait_ge(lev_mul, LEVELS * h + l)
                        pool.wait_ge(lev_copied, LEVELS * h + l)

                    def halves(x, which):
                        return x[:, 0:n].rearrange("p (b two h) -> p b two h", two=2, h=b)[:, :, which]
                    keep(halves(qc[l + 1], 0), halves(qc[l], 0))
                    nc.gpsimd.tensor_copy(halves(kr[l + 1], 1), halves(kr[l], 1)).then_inc(lev_copied, 1)
                pool.wait_ge(lev_copied, LEVELS * (h + 1))
                keep(kf[:, 2 * P:TP], kr[4][:, 2 * P:TP])
                nc.gpsimd.tensor_copy(kf[:, TP:T], kr[3][:, TP:T]).then_inc(kft_copied, 1)
                pool.wait_ge(kt_copied, h + 1)
                nc.gpsimd.tensor_tensor(kts[0:TAIL], kt[0:TAIL, 2:3].broadcast_to([TAIL, NB + 1, P]),
                                        t1[0:TAIL, C_ROWS:C_ROWS + NB + 1].unsqueeze(2).broadcast_to([TAIL, NB + 1, P]),
                                        ALU.mult).then_inc(kts_ready, 1)
                pool.wait_ge(o_done, 2 * (h + 1))
                nc.gpsimd.tensor_tensor(S0[:], S0[:], tot[3][:, TP // 8:TP // 8 + NB].unsqueeze(2).broadcast_to([P, NB, DV]),
                                        ALU.mult).then_inc(s0_scaled, 1)
                tail(h)

            head(0)
            with pool.Fori(1, H) as h:
                head(h)

            def stage(n):
                if not early(n, 1):
                    pool.wait_ge(qk_done, UNITS * n)
                    pool.wait_ge(sm_ready, UNITS * n)
                keep(kg[:].unsqueeze(1), kT[:, bass.ds(n, 1)])
                nc.gpsimd.tensor_copy(sinkg[:].unsqueeze(1), sinks[:, bass.ds(n, 1)]).then_inc(staged, 1)
                if not early(n, 1):
                    pool.wait_ge(pv_done, UNITS * n)
                keep(vg[:, 1:3], vtok[:, 1:3, bass.ds(n * HD, HD)])
                nc.gpsimd.tensor_copy(vg[0:META, 0:1], vtok[0:META, 0:1, bass.ds(n * HD, HD)])
                nc.gpsimd.tensor_copy(vg[0:NB * TS, 3:4], vtok[0:NB * TS, 3:4, bass.ds(n * HD, HD)]).then_inc(v_staged, 1)
                pool.wait_ge(q_copied, 2 * (n + 1))
                for w in range(4):
                    done = keep(qsam[:, :, w], qT[:, w, SEQ:TQ].rearrange("p (b t) -> p b t", t=TS))
                done.then_inc(qsam_ready, 1)

            pool.wait_ge(k_spread, 64)
            pool.wait_ge(vtok_copied, 4)
            pool.wait_ge(sinks_ready, 1)
            stage(0)
            with pool.Fori(1, KV) as n:
                stage(n)

        @block.scalar
        def _(act):
            act.dma_start(t1[:, C_ROWS:], t1_in[:, C_ROWS:]).then_inc(ones_loaded, 16)
            act.dma_start(vec[:], vec_in).then_inc(vec_loaded, 16)
            for c in range(1, 4):
                act.wait_ge(x_loaded[c], 16)
                if c == 3:
                    act.wait_ge(sq_added, 2)
                nc.scalar.activation(sq_new4[(c - 1) % 2], xT[:, 4 * c:4 * c + 4], ACT.Square).then_inc(sq_made, 1)
            act.dma_start(t1[:, 0:C_ROWS], t1_in[:, 0:C_ROWS]).then_inc(t1_loaded, 16)
            act.wait_ge(sq_added, 4)
            act.dma_start(S0[:].rearrange("p b e -> p (b e)"), s0_in[0]).then_inc(s0_loaded, 16)
            root_act(act, 0, T)
            for s in range(RING):
                split_hi(act, s, s, 0)
                normalise_act(act, 0, xn, xnH, T, range(4 * s, 4 * s + 4))

            def finish_head(h, s):
                t = h - 1
                if s == 1:
                    act.wait_ge(cross_done, t + 1)
                    if not early(h, 2):
                        act.wait_ge(o_done, 2 * t)
                    nc.scalar.activation(att[:, 2], RO[:, 0:P], ACT.Copy)
                    nc.scalar.activation(attX[:, :, 0:TAILP], RO[:, P:P + 2 * TAILP].rearrange("p (a n) -> p a n", a=2),
                                         ACT.Copy).then_inc(cross_copied, 1)
                    act.wait_ge(kfT_done, t + 1)
                    nc.scalar.activation(kt[:, 0:2], RT[:, 0:2 * P].rearrange("p (a n) -> p a n", a=2), ACT.Copy)
                    nc.scalar.activation(kt[0:TAIL, 2], RT[0:TAIL, 2 * P:3 * P], ACT.Copy).then_inc(kt_copied, 1)
                if s == 2:
                    act.wait_ge(vT_done, 2 * (t + 1))
                    nc.scalar.activation(V[:, 0:2], RA0[:].rearrange("p (a n) -> p a n", a=2), ACT.Copy)
                    nc.scalar.activation(V[0:TAIL, 2], RA1[0:TAIL, 0:DV], ACT.Copy).then_inc(v_copied, 1)
                if s == 3:
                    act.wait_ge(mm_done, SLABS_H * h)
                    if not early(h, 2):
                        act.wait_ge(g_ready, t)
                    nc.scalar.activation(sg[:], pz[:, 0:2, 0:T], ACT.Sigmoid).then_inc(g_sig, 1)
                    act.wait_ge(o_done, 2 * (t + 1))
                    nc.scalar.activation(junk[:, 0], RO[:, 0:DV], ACT.Square, accum_out=ssq[:, 0:1])
                    nc.scalar.activation(junk[:, 1], RO[:, DV:2 * DV], ACT.Square, accum_out=ssq[:, 1:2])
                    nc.scalar.activation(junk[0:TAIL, 2], RA1[0:TAIL, 0:DV], ACT.Square, accum_out=ssq[0:TAIL, 2:3]
                                         ).then_inc(ssq_ready, 1)
                if s == 4:
                    outputs(t, h)

            def head_round(h):
                for s in range(SLABS_H):
                    if not (early(h, 1) and s < RING):
                        split_hi(act, SLABS_H * h + s, s, SLABS_H // RING * h + s // RING)
                    if not early(h, 1):
                        finish_head(h, s)
                    if s == 7:
                        act.wait_ge(mm_done, SLABS_H * h + 4)
                        if not early(h, 1):
                            act.wait_ge(qs_ready, h)
                            act.wait_ge(kfT_done, h)
                            act.wait_ge(kf_ready, h)
                        nc.scalar.activation(sigq[:], pz[:, 0, 0:T], ACT.Sigmoid).then_inc(sigq_ready, 1)
                        nc.scalar.activation(fs[:], pz[:, 1, 0:T], ACT.Sigmoid)
                        nc.scalar.activation(ks[:], pz[:, 1, 0:T], ACT.Sigmoid, scale=-1.0).then_inc(fk_ready, 1)
                    if s == 11:
                        act.wait_ge(mm_done, SLABS_H * h + 8)
                        if not early(h, 1):
                            act.wait_ge(vT_done, 2 * h)
                        nc.scalar.activation(iT[:], pz[:, 2:4, 0:T], ACT.Copy).then_inc(i_copied, 1)

            def outputs(t, h):
                act.wait_ge(st_done, 5 * t + 1)
                if not early(h, 2):
                    act.wait_ge(sp_stored, 16 * t)
                nc.scalar.activation(Sp[:], RT[:, 0:DV], ACT.Copy).then_inc(sp_copied, 1)
                act.wait_ge(rs3_ready, t + 1)
                if not early(h, 2):
                    act.wait_ge(oT_done, t)
                nc.scalar.activation(on[:, 0], RO[:, 0:DV], ACT.Copy, scale=rs3[:, 0:1])
                nc.scalar.activation(on[:, 1], RO[:, DV:2 * DV], ACT.Copy, scale=rs3[:, 1:2])
                nc.scalar.activation(on[0:TAIL, 2], RA1[0:TAIL, 0:DV], ACT.Copy, scale=rs3[0:TAIL, 2:3]
                                     ).then_inc(on_ready, 1)

            head_round(0)
            head_round(1)
            with act.Fori(2, H) as h:
                head_round(h)

            def gather(before, pairs, held, ready, n):
                for c in pairs:
                    if c < ET // 2 - len(held):
                        turn = c // 4 + (before > 0) * (3 if c % 4 == 3 else 4)
                        act.wait_ge(og_loaded[c % 4], 16 * (turn + 1))
                    else:
                        act.wait_ge(*ready)
                    nc.scalar.activation(pair(ogH, c, n), pair_source(held, c, n), ACT.Copy).then_inc(ogh_ready, 1)

            def out_round(base, j, hooks=None):
                for s in range(SLABS_OUT):
                    split_hi(act, base + SLABS_OUT * j + s, s, base // RING + SLABS_OUT // RING * j + s // RING)
                    if hooks:
                        hooks(SLABS_OUT * j + s)

            def out_projection(base, before, held, ready, overlaid, finish, n):
                def hooks(s):
                    if s == 3:
                        act.wait_ge(mm_done, base)
                        gather(before, (0, 1), held, ready, n)
                    finish(s)
                    if s == 3:
                        gather(before, (2, 3), held, ready, n)
                    if s == 6:
                        for semaphore, value in overlaid:
                            act.wait_ge(semaphore, value)
                    if 4 <= s < 10:
                        gather(before, (2 * s - 4, 2 * s - 3), held, ready, n)
                out_round(base, 0, hooks)
                out_round(base, 1, hooks)
                with act.Fori(2, D // 256) as j:
                    out_round(base, j)

            out_projection(BASE_OUT_A, 0, [og[:]], (og_ready, H), [(st_done, 5 * H), (s0_scaled, H)],
                           lambda s: finish_head(H, s), T)

            for s in range(RING):
                split_hi(act, BASE_KV + s, s, BASE_KV // RING)
            root_act(act, 1, T)
            normalise_act(act, KT, xk, xkH, T, range(KT))
            for s in range(RING, SLABS_KV):
                split_hi(act, BASE_KV + s, s, BASE_KV // RING + s // RING)
                if s in (7, 11):
                    j = s // 4 - 1
                    act.wait_ge(mm_done, BASE_KV + 4 * j + 4)
                    nc.scalar.activation(ktmp[:, 2 * j:2 * j + 2], pz[:, 2 * j:2 * j + 2, 0:T], ACT.Copy).then_inc(k_copied, 1)
                if s == 15:
                    act.wait_ge(mm_done, BASE_KV + 12)
                    nc.scalar.activation(vT[:, 0:2], pz[:, 0:2, 0:T], ACT.Copy).then_inc(vt_copied, 1)
            for s in range(RING):
                split_hi(act, BASE_B + s, s, BASE_B // RING)
                if s == 3:
                    act.wait_ge(mm_done, BASE_KV + SLABS_KV)
                    nc.scalar.activation(vT[:, 2:4], pz[:, 2:4, 0:T], ACT.Copy).then_inc(vt_copied, 1)
                normalise_act(act, 2 * KT, xk, xkH, TQ, range(4 * s, 4 * s + 4))
            act.wait_ge(vtok_done, 4)
            nc.scalar.activation(vtok[0:META, 0], RA0[0:META, :], ACT.Copy).then_inc(vtok_copied, 1)
            nc.scalar.activation(vtok[:, 1], RA1[:, :], ACT.Copy).then_inc(vtok_copied, 1)
            nc.scalar.activation(vtok[:, 2], RO[:, :], ACT.Copy).then_inc(vtok_copied, 1)
            nc.scalar.activation(vtok[0:NB * TS, 3], RT[0:NB * TS, :], ACT.Copy).then_inc(vtok_copied, 1)

            def exps(n, u):
                k, r = UNITS * n + u, u % SCORES
                act.wait_ge(sm_ready, k + 1)
                if u < G:
                    parts = [(sc[:, r, 0:NKEYS], 0), (sc[:, r, NKEYS:SC], 1)]
                else:
                    parts = [(sc[:, r, 0:SS], 0), (sc[:, r, SS:2 * SS], 1)]
                for part, i in parts:
                    nc.scalar.activation(part, part, ACT.Exp, bias=stat[:, r, 2, i:i + 1], scale=HD ** -0.5,
                                         accum_out=stat[:, r, 5, i:i + 1])
                nc.scalar.activation(stat[:, r, 4], stat[:, r, 3], ACT.Exp, scale=HD ** -0.5).then_inc(exp_ready, 1)

            def copy_p(n, u):
                k, r = UNITS * n + u, u % 2
                act.wait_ge(tr_done, k + 1)
                if not early(k, 2):
                    act.wait_ge(pv_done, k - 1)
                if u < G:
                    nc.scalar.activation(pT[:, r, P:4 * P], RT[:, P:4 * P], ACT.Copy)
                    nc.scalar.activation(pT[0:META, r, 0:P], RT[0:META, 0:P], ACT.Copy).then_inc(pt_copied, 1)
                else:
                    def fours(x):
                        return x.rearrange("p (two n) -> p two n", two=2)
                    nc.scalar.activation(fours(pT[:, r])[:, :, 0:P], fours(RT[:])[:, :, 0:P], ACT.Copy)
                    nc.scalar.activation(fours(pT[0:NB * TS, r])[:, :, P:2 * P], fours(RT[0:NB * TS])[:, :, P:2 * P],
                                         ACT.Copy).then_inc(pt_copied, 1)

            def copy_o(n, u):
                if u < G:
                    if u % 2:
                        act.wait_ge(pv_done, UNITS * n + u + 1)
                        nc.scalar.activation(ob[:, u // 2, 0:SEQ], RO[:, 0:SEQ], ACT.Copy).then_inc(o_copied, 1)
                elif u == UNITS - 1:
                    act.wait_ge(pv_done, UNITS * (n + 1))
                    for w in range(4):
                        done = nc.scalar.activation(
                            ob[:, w, SEQ:TQ].rearrange("p (b t) -> p b t", t=TS),
                            RO[:, 0:SEQ].rearrange("p (b w t) -> p w b t", w=4, t=TS)[:, w], ACT.Copy)
                    done.then_inc(o_copied, 1)

            def finish_group(n, s):
                for u in range(UNITS):
                    for at, what in ((15 + u, copy_o), (13 + u, copy_p), (10 + u, exps)):
                        if at == s + SLABS_G:
                            what(n - 1, u)
                if s == 3:
                    act.wait_ge(mm_done, BASE_B + SLABS_G * n)
                    act.wait_ge(g0_copied, n)
                    nc.scalar.activation(sgb[:, 0:2], gate[:, 0:2], ACT.Sigmoid)
                    nc.scalar.activation(sgb[:, 2:4], pz[:, 2:4, 0:TQ], ACT.Sigmoid).then_inc(gb_sig, 1)

            def group_round(n):
                for s in range(SLABS_G):
                    if not (early(n, 1) and s < RING):
                        split_hi(act, BASE_B + SLABS_G * n + s, s, BASE_B // RING + SLABS_G // RING * n + s // RING)
                    if not early(n, 1):
                        finish_group(n, s)
                    for u in range(UNITS):
                        for at, what in ((15 + u, copy_o), (13 + u, copy_p), (10 + u, exps)):
                            if at == s:
                                what(n, u)
                    if s in (7, 11):
                        j = s // 4 - 1
                        act.wait_ge(mm_done, BASE_B + SLABS_G * n + 4 * j + 4)
                        nc.scalar.activation(qT[:, 2 * j:2 * j + 2], pz[:, 2 * j:2 * j + 2, 0:TQ], ACT.Copy).then_inc(q_copied, 1)
                    if s == 15:
                        act.wait_ge(mm_done, BASE_B + SLABS_G * n + 12)
                        if not early(n, 1):
                            act.wait_ge(obg_stored, 16 * n)
                        nc.scalar.activation(gate[:, 0:2], pz[:, 0:2, 0:TQ], ACT.Copy).then_inc(g0_copied, 1)

            act.wait_ge(kv_stored, 32)
            group_round(0)
            with act.Fori(1, KV) as n:
                group_round(n)
            out_projection(BASE_OUT_B, ET // 2, [gate[:, 0:2], gate[:, 2:4]], (ob_ready, KV),
                           [(sm_ready, UNITS * KV), (v_staged, KV), (qsam_ready, KV)],
                           lambda s: finish_group(KV, s), TQ)
            root_act(act, 2, TQ)

        @block.vector
        def _(dve):
            quarters = [xT[:, 4 * c:4 * c + 4] for c in range(4)]
            dve.wait_ge(x_loaded[0], 16)
            nc.vector.tensor_tensor(sq_sum4, quarters[0], quarters[0], ALU.mult).then_inc(sq_added, 1)
            for c in range(1, 4):
                dve.wait_ge(sq_made, c)
                dve.wait_ge(sq_added, c)
                nc.vector.tensor_tensor(sq_sum4, sq_sum4, sq_new4[(c - 1) % 2], ALU.add).then_inc(sq_added, 1)
            dve.wait_ge(sq_added, 4)
            nc.vector.tensor_tensor(sqsum[:], sq_sum4[:, 0:2], sq_sum4[:, 2:4], ALU.add).then_inc(sqsum_ready, 1)
            root_dve(dve, 0, T)
            dve.wait_ge(vec_loaded, 16)
            for s in range(RING):
                split_lo(dve, s, s)
                normalise_dve(dve, 0, xn, VA, xnH, xnL, 0, T, range(4 * s, 4 * s + 4))
            dve.wait_ge(t1_loaded, 16)
            dve.wait_ge(zeroed, 1)

            def doubling(h, l):
                n, b = LV_TOKENS[l], 1 << l
                dve.wait_ge(lev_copied, LEVELS * h + l)
                dve.wait_ge(lev_mul, LEVELS * h + l)

                def halves(x, which):
                    return x[:, 0:n].rearrange("p (b two h) -> p b two h", two=2, h=b)[:, :, which]
                blocks = tot[l][:, 0:n // b].rearrange("p (b two) -> p b two", two=2)
                shape = [P, n // (2 * b), b]
                nc.vector.tensor_tensor(halves(qc[l + 1], 1), halves(qc[l], 1), blocks[:, :, 0:1].broadcast_to(shape), ALU.mult)
                nc.vector.tensor_tensor(halves(kr[l + 1], 0), halves(kr[l], 0), blocks[:, :, 1:2].broadcast_to(shape), ALU.mult)
                nc.vector.tensor_tensor(tot[l + 1][:, 0:n // (2 * b)], blocks[:, :, 0], blocks[:, :, 1], ALU.mult
                                        ).then_inc(lev_mul, 1)

            def attention_tile(h, i):
                if i == 0:
                    dve.wait_ge(lev_done, 5 * h + 1)
                    if not early(h, 1):
                        dve.wait_ge(o_done, 2 * h)
                        dve.wait_ge(att_ready, 3 * h)
                    nc.vector.tensor_tensor(masked[0:TAIL, 0:5 * TAIL], RT[0:TAIL, 0:5 * TAIL],
                                            t1[0:TAIL, C_MASK3:C_MASK3 + 5 * TAIL], ALU.mult).then_inc(masked_ready, 1)
                    dve.wait_ge(masked_ready, 5 * h + 1)
                    nc.vector.tensor_reduce(out=att[0:TAIL, 3, 0:TAIL],
                                            in_=masked[0:TAIL, 0:5 * TAIL].rearrange("p (l t) -> p t l", t=TAIL),
                                            axis=AX.X, op=ALU.add).then_inc(att_ready, 1)
                else:
                    dve.wait_ge(att_ready, 3 * h + i)
                    for k, bank in ((0, RA0), (1, RA1)):
                        dve.wait_ge(lev_done, 5 * h + 2 * i + k)
                        nc.vector.tensor_tensor(masked[:, 512 * k:512 * k + 512], bank[:],
                                                t1[:, C_MASK + 512 * k:C_MASK + 512 * k + 512], ALU.mult
                                                ).then_inc(masked_ready, 1)
                    dve.wait_ge(masked_ready, 5 * h + 2 * i + 1)
                    nc.vector.tensor_reduce(out=att[:, i - 1], in_=masked[:].rearrange("p (l t) -> p t l", t=P),
                                            axis=AX.X, op=ALU.add).then_inc(att_ready, 1)

            def add_states(t, pair):
                bank = RA0 if pair % 2 == 0 else RT
                dve.wait_ge(st_done, 5 * t + pair + 2)
                dve.wait_ge(s0_scaled, t + 1)
                nc.vector.tensor_tensor(S0[:, 2 * pair:2 * pair + 2], bank[:].rearrange("p (a n) -> p a n", a=2),
                                        S0[:, 2 * pair:2 * pair + 2], ALU.add).then_inc(st_added, 1)

            def gate_a(t, h):
                dve.wait_ge(oT_done, t + 1)
                dve.wait_ge(g_ready, t + 1)
                if not early(h, 2):
                    dve.wait_ge(og_stored, 16 * t)
                nc.vector.scalar_tensor_tensor(og[:, 0], RO[:, 0:T], vec[:, VO:VO + 1], gs[:, 0], ALU.mult, ALU.mult)
                nc.vector.scalar_tensor_tensor(og[:, 1], RA1[:, 0:T], vec[:, VO + 1:VO + 2], gs[:, 1], ALU.mult, ALU.mult
                                               ).then_inc(og_ready, 1)

            def finish_head(h, s):
                t = h - 1
                if s == 0:
                    attention_tile(t, 2)
                if s == 3:
                    dve.wait_ge(g_sig, t + 1)
                    nc.vector.tensor_tensor(gs[:], sg[:], pz[:, 0:2, 0:T], ALU.mult).then_inc(g_ready, 1)
                if s == 4:
                    add_states(t, 0)
                if s == 5:
                    add_states(t, 1)
                    add_states(t, 2)
                if s == 6:
                    add_states(t, 3)
                if s == 7:
                    gate_a(t, h)

            def head_round(h):
                for s in range(SLABS_H):
                    if not (early(h, 1) and s < RING):
                        split_lo(dve, SLABS_H * h + s, s)
                    if not early(h, 1):
                        finish_head(h, s)
                    if s == 7:
                        dve.wait_ge(sigq_ready, h + 1)
                        nc.vector.scalar_tensor_tensor(qs[:], sigq[:], P ** -0.5, pz[:, 0, 0:T], ALU.mult, ALU.mult
                                                       ).then_inc(qs_ready, 1)
                        dve.wait_ge(fk_ready, h + 1)
                        dve.wait_ge(qs_ready, h + 1)
                        if not early(h, 1):
                            dve.wait_ge(s0_scaled, h)
                        nc.vector.tensor_tensor(qc[0][:], qs[:], fs[:], ALU.mult).then_inc(qc0_ready, 1)
                        dve.wait_ge(qc0_ready, h + 1)
                        for l in range(4):
                            doubling(h, l)
                    if s == 8:
                        for l in range(4, LEVELS):
                            doubling(h, l)
                        dve.wait_ge(lev_mul, LEVELS * (h + 1))
                        dve.wait_ge(lev_copied, LEVELS * (h + 1))
                        last, tail_decay = tot[7][:, 1:2], tot[4][:, TP // 16 - 1:TP // 16]
                        nc.vector.tensor_scalar(kx[:], kr[7][:, 0:P], last, None, ALU.mult).then_inc(kx_ready, 1)
                        nc.vector.tensor_scalar(kf[:, P:2 * P], kr[7][:, P:2 * P], tail_decay, None, ALU.mult)
                        dve.wait_ge(kx_ready, h + 1)
                        nc.vector.tensor_scalar(kf[:, 0:P], kx[:], tail_decay, None, ALU.mult).then_inc(kf_ready, 1)
                        nc.vector.tensor_copy(
                            Qs[:, TAILP:TAILP + NB * QS_W].rearrange("p (b c) -> p b c", c=QS_W)[:, :, 0:TS],
                            qc[3][:, TP:T].rearrange("p (b t) -> p b t", t=TS)).then_inc(Qs_ready, 1)
                    if s == 10:
                        attention_tile(h, 0)
                    if s == 11:
                        attention_tile(h, 1)

            head_round(0)
            head_round(1)
            with dve.Fori(2, H) as h:
                head_round(h)

            def gather(before, pairs, held, n):
                for c in pairs:
                    dve.wait_ge(ogh_ready, before + c + 1)
                    nc.vector.tensor_tensor(pair(ogL, c, n), pair_source(held, c, n), pair(ogH, c, n).bitcast(F32),
                                            ALU.subtract).then_inc(ogl_ready, 1)

            def add_pair(base, c, j, bank, c0, n):
                at = (D // 256) * (c - 1) + j
                dve.wait_ge(mm_done, base + SLABS_OUT * (j + 1))
                x = xT[:, bass.ds(2 * j, 2), c0:c0 + n]
                nc.vector.tensor_tensor(x, x, pz[:, bank:bank + 2, 0:n], ALU.add).then_inc(x_added, 1)
                dve.wait_ge(x_added, at + 1)
                if early(j, 1):
                    nc.vector.tensor_tensor(sqsum[:, :, 0:n], x, x, ALU.mult).then_inc(sqsum_ready, 1)
                elif isinstance(j, int) and j == D // 256 - 1:
                    nc.vector.tensor_tensor(sqo[:, :, 0:n], x, x, ALU.mult).then_inc(sq_ready, 1)
                    return
                else:
                    nc.vector.tensor_tensor(sqo[:, :, 0:n], x, x, ALU.mult).then_inc(sqo_ready, 1)
                    dve.wait_ge(sqo_ready, (D // 256 - 2) * (c - 1) + j)
                    nc.vector.tensor_tensor(sqsum[:, :, 0:n], sqsum[:, :, 0:n], sqo[:, :, 0:n], ALU.add).then_inc(sqsum_ready, 1)
                dve.wait_ge(sqsum_ready, sums_before(c) + j + 1)

            def out_projection(base, c, held, finish, c0, n):
                def out_round(j, par, hooks=None):
                    for s in range(SLABS_OUT):
                        split_lo(dve, base + SLABS_OUT * j + s, s)
                        if hooks:
                            hooks(SLABS_OUT * j + s)
                        if s == 3 and not early(j, 1):
                            add_pair(base, c, j - 1, 2 * (1 - par), c0, n)

                def hooks(s):
                    before = ET // 2 * (c - 1)
                    if s == 3:
                        gather(before, (0, 1), held, n)
                    finish(s)
                    if s == 3:
                        gather(before, (2, 3), held, n)
                    if 4 <= s < 10:
                        gather(before, (2 * s - 4, 2 * s - 3), held, n)
                out_round(0, 0, hooks)
                out_round(1, 1, hooks)
                with dve.Fori(2, D // 256, 2) as j:
                    out_round(j, 0)
                    out_round(j + 1, 1)

            out_projection(BASE_OUT_A, 1, [og[:]], lambda s: finish_head(H, s), 0, T)

            for s in range(RING):
                split_lo(dve, BASE_KV + s, s)
            add_pair(BASE_OUT_A, 1, D // 256 - 1, 2, 0, T)
            root_dve(dve, 1, T)
            normalise_dve(dve, KT, xk, VKV, xkH, xkL, 0, T, range(KT))
            for s in range(RING, SLABS_KV):
                split_lo(dve, BASE_KV + s, s)
                if s == 15:
                    dve.wait_ge(sink_loaded, 16)
                    dve.wait_ge(t2_loaded, 16)
                    nc.vector.tensor_scalar(sinks[:], sinks[:], HD ** 0.5, None, ALU.mult).then_inc(sinks_ready, 1)
            for s in range(RING):
                split_lo(dve, BASE_B + s, s)
                dve.wait_ge(mm_done, BASE_KV + 13 + s)
                normalise_dve(dve, 2 * KT, xk, VB, xkH, xkL, META, TQ, range(4 * s, 4 * s + 4))

            def scores(n, u):
                k, r = UNITS * n + u, u % SCORES
                bank = RA0 if u % 2 == 0 else RA1
                dve.wait_ge(qk_done, k + 1)
                dve.wait_ge(staged, n + 1)
                if not early(k, SCORES):
                    dve.wait_ge(tr_done, k - SCORES + 1)
                if u < G:
                    nc.vector.scalar_tensor_tensor(sc[:, r, 0:SC], t2[:, C_DIST:C_DIST + SC],
                                                   t2[:, C_SLOPE + u:C_SLOPE + u + 1], bank[:, 0:SC],
                                                   ALU.mult, ALU.add).then_inc(biased, 1)
                    parts = [(0, NKEYS), (NKEYS, SC)]
                    sink = sinkg[:, u:u + 1].broadcast_to([P, 2])
                else:
                    slope = C_SLOPE_S + u - G
                    nc.vector.scalar_tensor_tensor(sc[:, r, 0:2 * SS], t2[:, C_DIST_S:C_DIST_S + 2 * SS],
                                                   t2[:, slope:slope + 1], bank[:, 0:2 * SS],
                                                   ALU.mult, ALU.add).then_inc(biased, 1)
                    parts = [(0, SS), (SS, 2 * SS)]
                    sink = sinkg[:, u:u + 1].broadcast_to([P, 2])
                dve.wait_ge(biased, k + 1)
                for i, (a, b) in enumerate(parts):
                    done = nc.vector.reduce_max(stat[:, r, 0, i:i + 1], sc[:, r, a:b], AX.X)
                done.then_inc(max_ready, 1)
                dve.wait_ge(max_ready, k + 1)
                nc.vector.tensor_tensor(stat[:, r, 1], stat[:, r, 0], sink, ALU.max).then_inc(mm_ready, 1)
                dve.wait_ge(mm_ready, k + 1)
                nc.vector.tensor_scalar(stat[:, r, 2], stat[:, r, 1], -HD ** -0.5, None, ALU.mult)
                nc.vector.tensor_tensor(stat[:, r, 3], sink, stat[:, r, 1], ALU.subtract).then_inc(sm_ready, 1)

            def divide(n, u):
                k, r = UNITS * n + u, u % SCORES
                dve.wait_ge(exp_ready, k + 1)
                nc.vector.tensor_tensor(stat[:, r, 5], stat[:, r, 5], stat[:, r, 4], ALU.add).then_inc(den_ready, 1)
                dve.wait_ge(den_ready, k + 1)
                nc.vector.reciprocal(stat[:, r, 6], stat[:, r, 5]).then_inc(rden_ready, 1)
                dve.wait_ge(rden_ready, k + 1)
                for i, (a, b) in enumerate([(0, NKEYS), (NKEYS, SC)] if u < G else [(0, SS), (SS, 2 * SS)]):
                    done = nc.vector.tensor_scalar(sc[:, r, a:b], sc[:, r, a:b], stat[:, r, 6, i:i + 1], None, ALU.mult)
                done.then_inc(p_ready, 1)

            def finish_group(n, s):
                for u in range(UNITS):
                    for at, what in ((11 + u, divide), (9 + u, scores)):
                        if at == s + SLABS_G:
                            what(n - 1, u)
                if s == 4:
                    dve.wait_ge(gb_sig, n)
                    nc.vector.tensor_tensor(gate[:, 0:2], gate[:, 0:2], sgb[:, 0:2], ALU.mult)
                    nc.vector.tensor_tensor(gate[:, 2:4], pz[:, 2:4, 0:TQ], sgb[:, 2:4], ALU.mult).then_inc(gb_ready, 1)
                if s == 8:
                    dve.wait_ge(o_copied, 5 * n)
                    dve.wait_ge(gb_ready, n)
                    nc.vector.tensor_tensor(gate[:], gate[:], ob[:], ALU.mult).then_inc(ob_ready, 1)

            def group_round(n):
                for s in range(SLABS_G):
                    if not (early(n, 1) and s < RING):
                        split_lo(dve, BASE_B + SLABS_G * n + s, s)
                    if not early(n, 1):
                        finish_group(n, s)
                    for u in range(UNITS):
                        for at, what in ((11 + u, divide), (9 + u, scores)):
                            if at == s:
                                what(n, u)
                    if s == 8 and not early(n, 1):
                        nc.vector.tensor_scalar(t2[:, C_SLOPE:C_ALL2], t2[:, C_SLOPE:C_ALL2], 0.5, None, ALU.mult
                                                ).then_inc(slope_ready, 1)
                        dve.wait_ge(slope_ready, n)

            group_round(0)
            with dve.Fori(1, KV) as n:
                group_round(n)
            out_projection(BASE_OUT_B, 2, [gate[:, 0:2], gate[:, 2:4]], lambda s: finish_group(KV, s), META, TQ)
            add_pair(BASE_OUT_B, 2, D // 256 - 1, 2, META, TQ)
            root_dve(dve, 2, TQ)
            for f in range(KT):
                if f >= 4 and f % 2 == 0:
                    dve.wait_ge(y_stored[f // 2 % 2], 16 * (f // 4))
                nc.vector.scalar_tensor_tensor(yst[:, f % 4], xT[:, f, META:T], vec[:, VF + f:VF + f + 1], rstd[:, 0:TQ],
                                               ALU.mult, ALU.mult).then_inc(y_ready, 1)

        @block.tensor
        def _(pe):
            pe.wait_ge(ones_loaded, 16)
            sum_squares(pe, 0, T)

            def levels(h, i):
                if i == 0:
                    pe.wait_ge(lev_mul, LEVELS * h + 3)
                    pe.wait_ge(lev_copied, LEVELS * h + 3)
                    if not early(h, 1):
                        pe.wait_ge(st_added, 4 * h)
                        pe.wait_ge(sp_copied, h)
                    cols = slice(2 * P, T)
                    for k, l in enumerate([3, 2, 1, 0, None]):
                        lhs, rhs = (ks, qs) if l is None else (kr[l], qc[l])
                        done = nc.tensor.matmul(RT[0:TAIL, k * TAIL:k * TAIL + TAIL], lhs[:, cols], rhs[:, cols],
                                                start=True, stop=True)
                    done.then_inc(lev_done, 1)
                else:
                    pe.wait_ge(lev_mul, LEVELS * h + LEVELS - 1)
                    pe.wait_ge(lev_copied, LEVELS * h + LEVELS - 1)
                    cols = slice((i - 1) * P, i * P)
                    for b, bank in ((0, RA0), (1, RA1)):
                        if i == 1:
                            if not early(h, 1):
                                pe.wait_ge(og_ready, h)
                        else:
                            pe.wait_ge(masked_ready, 5 * h + 2 + b)
                        for k, l in enumerate([6, 5, 4, 3] if b == 0 else [2, 1, 0, None]):
                            lhs, rhs = (ks, qs) if l is None else (kr[l], qc[l])
                            done = nc.tensor.matmul(bank[:, k * P:k * P + P], lhs[:, cols], rhs[:, cols],
                                                    start=True, stop=True)
                        done.then_inc(lev_done, 1)

            def cross(h):
                pe.wait_ge(kx_ready, h + 1)
                pe.wait_ge(lev_mul, LEVELS * (h + 1))
                pe.wait_ge(lev_copied, LEVELS * (h + 1))
                if not early(h, 1):
                    pe.wait_ge(og_ready, h)
                nc.tensor.matmul(RO[:, 0:P], kr[7][:, 0:P], qc[7][:, P:2 * P], start=True, stop=True)
                nc.tensor.matmul(RO[:, P:P + TAILP], kx[:], qc[4][:, 2 * P:TP], start=True, stop=True)
                nc.tensor.matmul(RO[:, P + TAILP:P + 2 * TAILP], kr[7][:, P:2 * P], qc[4][:, 2 * P:TP],
                                 start=True, stop=True).then_inc(cross_done, 1)
                pe.wait_ge(kf_ready, h + 1)
                pe.wait_ge(kft_copied, h + 1)
                pe.wait_ge(masked_ready, 5 * h + 1)
                nc.tensor.transpose(RT[:, 0:P], kf[:, 0:P], ident)
                nc.tensor.transpose(RT[:, P:2 * P], kf[:, P:2 * P], ident)
                nc.tensor.transpose(RT[0:TAIL, 2 * P:3 * P], kf[:, 2 * P:T], ident).then_inc(kfT_done, 1)

            def values(h):
                pe.wait_ge(i_copied, h + 1)
                pe.wait_ge(masked_ready, 5 * h + 5)
                for i in range(2):
                    for e in range(2):
                        done = nc.tensor.transpose(RA0[:, i * DV + e * P:i * DV + e * P + P], iT[:, e, i * P:i * P + P], ident)
                done.then_inc(vT_done, 1)
                for e in range(2):
                    done = nc.tensor.transpose(RA1[0:TAIL, e * P:e * P + P], iT[:, e, 2 * P:T], ident)
                done.then_inc(vT_done, 1)

            def head_outputs(h):
                pe.wait_ge(v_copied, h + 1)
                pe.wait_ge(att_ready, 3 * (h + 1))
                pe.wait_ge(cross_copied, h + 1)
                nc.tensor.matmul(RO[:, 0:DV], att[:, 0], V[:, 0], start=True, stop=True)
                nc.tensor.matmul(RO[:, DV:2 * DV], att[:, 2], V[:, 0], start=True, stop=False)
                nc.tensor.matmul(RO[:, DV:2 * DV], att[:, 1], V[:, 1], start=False, stop=True).then_inc(o_done, 1)
                out = RA1[0:TAIL, 0:DV]
                nc.tensor.matmul(out, att[0:TAIL, 3, 0:TAIL], V[0:TAIL, 2], start=True, stop=False)
                nc.tensor.matmul(out, attX[:, 0], V[:, 0], start=False, stop=False)
                nc.tensor.matmul(out, attX[:, 1], V[:, 1], start=False, stop=False)
                pe.wait_ge(s0_loaded, 16 * (h + 1))
                pe.wait_ge(Qs_ready, h + 1)
                for b in range(NB):
                    done = nc.tensor.matmul(out, Qs[:, TAIL * b:TAIL * b + TAIL], S0[:, b], start=False, stop=b == NB - 1)
                done.then_inc(o_done, 1)

            def states(t, k):
                bank = RT if k % 2 == 0 else RA0
                if k == 0:
                    pe.wait_ge(kt_copied, t + 1)
                    pe.wait_ge(kts_ready, t + 1)
                    nc.tensor.matmul(bank[:, 0:DV], kt[:, 0], V[:, 0], start=True, stop=False)
                    nc.tensor.matmul(bank[:, 0:DV], kt[:, 1], V[:, 1], start=False, stop=False)
                    nc.tensor.matmul(bank[:, 0:DV], kts[0:TAIL, 0], V[0:TAIL, 2], start=False, stop=True).then_inc(st_done, 1)
                    return
                if k == 2:
                    pe.wait_ge(sp_copied, t + 1)
                if k > 2:
                    pe.wait_ge(st_added, 4 * t + k - 2)
                for i in range(2):
                    done = nc.tensor.matmul(bank[:, i * DV:i * DV + DV], kts[0:TAIL, 2 * k - 1 + i], V[0:TAIL, 2],
                                            start=True, stop=True)
                done.then_inc(st_done, 1)

            def turn_back(t):
                pe.wait_ge(on_ready, t + 1)
                for e, bank in ((0, RO), (1, RA1)):
                    for i, m in ((0, P), (1, P), (2, TAIL)):
                        done = nc.tensor.transpose(bank[:, i * P:i * P + m], on[0:m, i, e * P:e * P + P], ident[0:m, 0:m])
                done.then_inc(oT_done, 1)

            def finish_head(h, s):
                if s in (0, 1):
                    states(h - 1, 2 * s)
                    states(h - 1, 2 * s + 1)
                if s == 2:
                    states(h - 1, 4)
                if s == 3:
                    turn_back(h - 1)

            def head_round(h):
                for s in range(SLABS_H):
                    if s == 0 and not early(h, 1):
                        pe.wait_ge(g_ready, h)
                    if s == 4 and not early(h, 1):
                        pe.wait_ge(i_copied, h)
                    if s == 8:
                        pe.wait_ge(qs_ready, h + 1)
                        pe.wait_ge(fk_ready, h + 1)
                    if early(h, 1) and s < 4:
                        pe.wait_ge(xl_ready, 4 * s + 4)
                    products(pe, SLABS_H * h + s, s, 4 * (s % 4), 2 * (s // 4 % 2), [xnH], [xnL], T, s % 4 == 0, s % 4 == 3)
                    if not early(h, 1):
                        finish_head(h, s)
                    if s in (6, 7, 8):
                        levels(h, s - 6)
                    if s == 9:
                        cross(h)
                    if s == 10:
                        values(h)
                    if s == 11:
                        head_outputs(h)

            head_round(0)
            with pe.Fori(1, H) as h:
                head_round(h)

            def out_projection(base, c, free, free_next, before_first, finish, n):
                def out_round(j, par):
                    for s in range(SLABS_OUT):
                        if early(j, 1):
                            if s == 0:
                                before_first()
                                pe.wait_ge(*free)
                            pe.wait_ge(ogl_ready, ET // 2 * (c - 1) + 2 * s + 2)
                        if s == 0 and isinstance(j, int) and j == 1:
                            pe.wait_ge(*free_next)
                        if s == 0 and not early(j, 2):
                            pe.wait_ge(x_added, (D // 256) * (c - 1) + j - 1)
                        products(pe, base + SLABS_OUT * j + s, s, SLAB * s, 2 * par, ogH, ogL, n, s == 0, s == SLABS_OUT - 1)
                        if early(j, 1):
                            finish(s)
                out_round(0, 0)
                out_round(1, 1)
                with pe.Fori(2, D // 256, 2) as j:
                    out_round(j, 0)
                    out_round(j + 1, 1)

            out_projection(BASE_OUT_A, 1, (g_ready, H), (i_copied, H), lambda: finish_head(H, 0),
                           lambda s: s and finish_head(H, s), T)
            pe.wait_ge(st_added, 4 * H)
            sum_squares(pe, 1, T)

            for s in range(SLABS_KV):
                if s == 0:
                    pe.wait_ge(x_added, 7)
                if s == 4:
                    pe.wait_ge(x_added, 8)
                if s in (8, 12):
                    pe.wait_ge(k_copied, s // 4 - 1)
                if s < 4:
                    pe.wait_ge(xl_ready, KT + 4 * s + 4)
                products(pe, BASE_KV + s, s, 4 * (s % 4), 2 * (s // 4 % 2), [xkH], [xkL], T, s % 4 == 0, s % 4 == 3)
            def values_by_token():
                pe.wait_ge(vt_copied, 2)
                pe.wait_ge(ms_ready, 2)
                for bank, a, b in ((RA0, 0, META), (RA1, META, META + P), (RO, META + P, TP), (RT, TP, T)):
                    for j in range(4):
                        done = nc.tensor.transpose(bank[0:b - a, j * P:j * P + P], vT[:, j, a:b], ident)
                    done.then_inc(vtok_done, 1)

            def score_products(n, u):
                k = UNITS * n + u
                bank = RA0 if u % 2 == 0 else RA1
                if u == 0:
                    pe.wait_ge(staged, n + 1)
                    pe.wait_ge(q_copied, 2 * n + 1)
                    if early(n, 1):
                        pe.wait_ge(vtok_copied, 4)
                if u == 4:
                    pe.wait_ge(q_copied, 2 * n + 2)
                if not early(k, 2):
                    pe.wait_ge(biased, k - 1)
                if u < G:
                    half = slice(64 * (u % 2), 64 * (u % 2) + 64)
                    nc.tensor.matmul(bank[:, 0:NKEYS], qT[half, u // 2, 0:P], kg[half, 0:NKEYS], start=True, stop=True)
                    nc.tensor.matmul(bank[:, NKEYS:SC], qT[half, u // 2, P:2 * P], kg[half, META:TP], start=True, stop=True
                                     ).then_inc(qk_done, 1)
                    return
                if u == G:
                    pe.wait_ge(ck_loaded, 32 * (n + 1))
                    pe.wait_ge(qsam_ready, n + 1)
                half = slice(64 * (u - G), 64 * (u - G) + 64)
                for four in range(2):
                    first = 4 * four
                    nc.tensor.matmul(bank[:, four * SS + WIN:four * SS + SS], qsam[half, first:first + 4].rearrange("p b w t -> p (b w t)"),
                                     kg[half, TP:T], start=True, stop=True)
                    for j in range(4):
                        done = nc.tensor.matmul(bank[32 * j:32 * j + 32, four * SS:four * SS + WIN],
                                                qsam[half, first + j].rearrange("p w t -> p (w t)"),
                                                ckT[half, first + j], start=True, stop=True)
                done.then_inc(qk_done, 1)

            def turn_p(n, u):
                k, r = UNITS * n + u, u % SCORES
                pe.wait_ge(p_ready, k + 1)
                if not early(k, 1):
                    pe.wait_ge(pt_copied, k)
                if u < G:
                    nc.tensor.transpose(RT[0:META, 0:P], sc[:, r, 0:META], ident)
                    for i in range(3):
                        a = META + i * P
                        done = nc.tensor.transpose(RT[:, P + i * P:2 * P + i * P], sc[:, r, a:a + P], ident)
                else:
                    for four in range(2):
                        nc.tensor.transpose(RT[:, four * 2 * P:four * 2 * P + P], sc[:, r, four * SS:four * SS + WIN], ident)
                        done = nc.tensor.transpose(RT[0:NB * TS, four * 2 * P + P:four * 2 * P + 2 * P],
                                                   sc[:, r, four * SS + WIN:four * SS + SS], ident)
                done.then_inc(tr_done, 1)

            def value_products(n, u):
                k, r = UNITS * n + u, u % 2
                pe.wait_ge(pt_copied, k + 1)
                if u == 0:
                    pe.wait_ge(v_staged, n + 1)
                    if early(n, 1):
                        pe.wait_ge(vtok_copied, 4)
                    else:
                        pe.wait_ge(o_copied, 5 * n)
                if u in (2, 4, 6, 8):
                    pe.wait_ge(o_copied, 5 * n + u // 2)
                if u < G:
                    half = slice(64 * (u % 2), 64 * (u % 2) + 64)
                    nc.tensor.matmul(RO[half, 0:P], vg[0:META, 0], pT[0:META, r, 0:P], start=True, stop=False)
                    nc.tensor.matmul(RO[half, 0:P], vg[:, 1], pT[:, r, P:2 * P], start=False, stop=True)
                    nc.tensor.matmul(RO[half, P:2 * P], vg[:, 1], pT[:, r, 2 * P:3 * P], start=True, stop=False)
                    nc.tensor.matmul(RO[half, P:2 * P], vg[:, 2], pT[:, r, 3 * P:4 * P], start=False, stop=True
                                     ).then_inc(pv_done, 1)
                    return
                half = slice(64 * (u - G), 64 * (u - G) + 64)
                for four in range(2):
                    c0, p0 = four * P, four * 2 * P
                    for j in range(4):
                        out, p = RO[half, c0 + 32 * j:c0 + 32 * j + 32], p0 + 32 * j
                        nc.tensor.matmul(out, cv[:, 4 * four + j], pT[:, r, p:p + 32], start=True, stop=False)
                        done = nc.tensor.matmul(out, vg[0:NB * TS, 3], pT[0:NB * TS, r, p + P:p + P + 32],
                                                start=False, stop=True)
                done.then_inc(pv_done, 1)

            def finish_group(n, s):
                for u in range(UNITS):
                    for at, what in ((11 + u, value_products), (9 + u, turn_p), (5 + u, score_products)):
                        if at == s + SLABS_G:
                            what(n - 1, u)

            def group_round(n):
                for s in range(SLABS_G):
                    if s == 0 and not early(n, 1):
                        pe.wait_ge(g0_copied, n)
                    if s == 4 and not early(n, 1):
                        pe.wait_ge(gb_ready, n)
                    if s == 4 and early(n, 1):
                        pe.wait_ge(vt_copied, 2)
                    if s in (8, 12):
                        pe.wait_ge(q_copied, 2 * n + s // 4 - 1)
                    if early(n, 1) and s < 4:
                        pe.wait_ge(xl_ready, 2 * KT + 4 * s + 4)
                    products(pe, BASE_B + SLABS_G * n + s, s, 4 * (s % 4), 2 * (s // 4 % 2), [xkH], [xkL], TQ,
                             s % 4 == 0, s % 4 == 3)
                    if early(n, 1) and s == 1:
                        values_by_token()
                    if not early(n, 1):
                        finish_group(n, s)
                    for u in range(UNITS):
                        for at, what in ((11 + u, value_products), (9 + u, turn_p), (5 + u, score_products)):
                            if at == s:
                                what(n, u)

            group_round(0)
            with pe.Fori(1, KV) as n:
                group_round(n)
            out_projection(BASE_OUT_B, 2, (g0_copied, KV), (gb_ready, KV), lambda: None, lambda s: finish_group(KV, s), TQ)
            sum_squares(pe, 2, TQ)


_OUTS = [("y", (KT, P, TQ)), ("st_prompt", (H, P, DV)), ("st_sample", (H, P, NB * DV)), ("k", (4, P, T)),
         ("v", (4, P, T)), ("ck_old", (NB, WIN - TS, KV * HD)), ("cv_old", (NB, WIN - TS, KV * HD))]


def slabs(w):
    k, n = w.shape
    return w.reshape(k // (SLAB * P), SLAB, P, n // 256, 256).transpose(3, 0, 2, 1, 4).reshape(-1, P, SLAB_W)


def kernel(x_prompt, x_sample, state_hgrn, cache_k, cache_v, meta_tokens, norm_a, w_in_a, lb_a, onorm_a,
           w_out_a, norm_kv, w_kv, norm_b, w_in_b, sink_b, w_out_b, norm_f):
    import concourse.bacc as bacc
    from concourse.bass_utils import run_bass_kernel_spmd

    f32 = np.float32
    arr = [np.asarray(a) for a in (x_prompt, x_sample, state_hgrn, cache_k, cache_v, meta_tokens, norm_a, w_in_a,
                                   onorm_a, w_out_a, norm_kv, w_kv, norm_b, w_in_b, sink_b, w_out_b, norm_f)]
    xp, xs, st, ck, cv, meta, na, wa, on, woa, nkv, wkv, nb, wb, sink, wob, nf = arr
    x = np.concatenate([meta, xp[0], xs.reshape(NB * TS, D)], axis=0)
    x_in = x.T.reshape(KT, P, T).transpose(1, 0, 2).reshape(P, KT * T)
    q, f, i, g = np.split(wa[0], [D, 2 * D, 4 * D], axis=1)
    heads = []
    for h in range(H):
        qf = np.concatenate([q[:, h * P:h * P + P], f[:, h * P:h * P + P]], axis=1)
        heads += [qf, i[:, h * DV:h * DV + DV], g[:, h * DV:h * DV + DV]]
    qb, gb = np.split(wb[0], 2, axis=1)
    groups = []
    for n in range(KV):
        groups += [qb[:, n * 512:n * 512 + 512], gb[:, n * 512:n * 512 + 512]]
    w_in = np.concatenate([slabs(w) for w in heads + [woa[0], wkv] + groups + [wob[0]]], axis=0)
    assert w_in.shape[0] == N_SLABS
    s0_in = st[0].transpose(1, 2, 0, 3).reshape(H, P, NB * DV)
    ckd = ck.transpose(2, 3, 0, 1).reshape(KV, HD, NB * WIN)
    ckd = np.concatenate([ckd, ckd], axis=1)
    cvd = cv.transpose(2, 1, 0, 3).reshape(KV, WIN, NB * HD)
    vec = np.concatenate([a.reshape(-1, P).T for a in (na[0], nkv, nb[0], nf, on[0])], axis=1)
    row = np.arange(P) // 8 % 4
    by_head = np.broadcast_to(sink[0].reshape(1, KV, G), (P, KV, G))
    by_row = np.stack([sink[0].reshape(KV, G)[:, 2 * row + par] for par in range(2)], axis=-1).transpose(1, 0, 2)
    sinks = np.concatenate([by_head, by_row], axis=2).reshape(P, KV * (G + 2))
    t1, t2 = tables()

    nc = bacc.Bacc("TRN2", target_bir_lowering=False, num_devices=1)
    feeds, aps = {}, []
    for name, a in (("x", x_in), ("w", w_in), ("s0", s0_in), ("ck", ckd), ("cv", cvd), ("vec", vec), ("sinks", sinks),
                    ("t1", t1), ("t2", t2), ("ck_rest", ck[:, TS:].reshape(NB, WIN - TS, KV * HD)),
                    ("cv_rest", cv[:, TS:].reshape(NB, WIN - TS, KV * HD))):
        a = np.ascontiguousarray(a)
        feeds["in_" + name] = a
        aps.append(nc.dram_tensor("in_" + name, a.shape, mybir.dt.from_np(a.dtype), kind="ExternalInput").ap())
    outs = [nc.dram_tensor("out_" + name, shape, F32, kind="ExternalOutput").ap() for name, shape in _OUTS]
    x_d, w_d, s0_d, ck_d, cv_d, vec_d, sink_d, t1_d, t2_d, ckr_d, cvr_d = aps
    trunk(nc, x_d, w_d, s0_d, cv_d, ck_d, vec_d, sink_d, t1_d, t2_d, ckr_d, cvr_d, *outs)
    r = run_bass_kernel_spmd(nc, [feeds], core_ids=[0]).results[0]
    y, sp, ss, k, v, ck_old, cv_old = (np.asarray(r["out_" + name]) for name, _ in _OUTS)
    y = y.reshape(D, TQ).T
    k, v = (a.reshape(KV * HD, T).T for a in (k, v))

    def window(old, new):
        return np.concatenate([old.reshape(NB, WIN - TS, KV, HD), new[TP:].reshape(NB, TS, KV, HD)], axis=1)
    return (y[:SEQ].reshape(1, SEQ, D), y[SEQ:].reshape(NB, TS, D), sp.reshape(1, 1, H, P, DV),
            k[TP - WIN:TP].reshape(1, WIN, KV, HD), v[TP - WIN:TP].reshape(1, WIN, KV, HD),
            ss.reshape(H, P, NB, DV).transpose(2, 0, 1, 3)[None], window(ck_old, k), window(cv_old, v))
```

```python
import numpy as np
import concourse.bass as bass
from concourse import mybir
from contextlib import ExitStack

F32 = mybir.dt.float32
F32R = mybir.dt.float32r
ACT = mybir.ActivationFunctionType
ALU = mybir.AluOpType
AX = mybir.AxisListType

P = 128
D = 2048
META, SEQ, NB, TS = 16, 256, 8, 8
TP = META + SEQ
T = TP + NB * TS
TQ = T - META
KT = D // P
H = 16
DV = 256
ET = 2 * KT
KV, G, HD = 8, 8, 64
WIN = 128
EPS = 1e-6
BIG = 1e30

SLAB = 4
SLAB_W = SLAB * 256
RING = 4
SLABS_H = 3 * KT // SLAB
SLABS_OUT = ET // SLAB
SLABS_KV = 4 * KT // SLAB
SLABS_G = 4 * KT // SLAB
BASE_OUT_A = H * SLABS_H
BASE_KV = BASE_OUT_A + (D // 256) * SLABS_OUT
BASE_B = BASE_KV + SLABS_KV
BASE_OUT_B = BASE_B + KV * SLABS_G
N_SLABS = BASE_OUT_B + (D // 256) * SLABS_OUT

TAIL = T - 2 * P
TAILP = TP - 2 * P
LEVELS = 7
LV_TOKENS = [T, T, T, TP, 2 * P, 2 * P, 2 * P]
TOT_LEN = [T, T // 2, T // 4, T // 8, TP // 16, 2 * P // 32, 2 * P // 64, 2]
TOT_AT = [0] + [sum(TOT_LEN[1:l]) for l in range(1, LEVELS + 1)]
TOT_N = sum(TOT_LEN[1:])
QS_W = TAIL + TS
S4 = 4 * TS
STACK = 3 * S4
UNITS = G + 2
SCORES = 5
NKEYS = META + P
SC = NKEYS + 2 * P
SS = WIN + NB * TS

C_MASK = 0
C_MASK3 = C_MASK + (LEVELS + 1) * P
C_ROWS = C_MASK3 + 5 * TAIL
C_ROWS4 = C_ROWS + 1
C_IDENT = C_ROWS4 + 4
C_ONES = C_IDENT + P
C_ALL1 = C_ONES + P
C_DIST = 0
C_DIST_S = C_DIST + SC
C_SLOPE = C_DIST_S + 2 * SS
C_SLOPE_S = C_SLOPE + G
C_ALL2 = C_SLOPE_S + 2
UNUSED = 2 * KT * T - (KV * T + C_ALL2 + KV * (G + 2) + 16 * P + NB * WIN + T + 4 * TQ + 4 * NB * TS + G + 2)


def tables():
    t1 = np.zeros((P, C_ALL1), np.float32)
    s, t = np.arange(P)[:, None], np.arange(P)[None, :]
    for n, l in enumerate([6, 5, 4, 3, 2, 1, 0]):
        t1[:, C_MASK + n * P:C_MASK + (n + 1) * P] = ((s ^ t) >> l == 1) & (t > s)
    t1[:, C_MASK + LEVELS * P:C_MASK + (LEVELS + 1) * P] = s == t
    s, t = np.arange(TAIL)[:, None], np.arange(TAIL)[None, :]
    for n, l in enumerate([3, 2, 1, 0]):
        own = (s < TAILP) & (t < TAILP) if l == 3 else True
        t1[:TAIL, C_MASK3 + n * TAIL:C_MASK3 + (n + 1) * TAIL] = ((s ^ t) >> l == 1) & (t > s) & own
    t1[:TAIL, C_MASK3 + 4 * TAIL:C_MASK3 + 5 * TAIL] = s == t
    t1[:TAILP, C_ROWS] = 1.0
    for j in range(4):
        t1[:STACK, C_ROWS4 + j] = np.arange(STACK) % S4 // TS == j
    t1[:, C_IDENT:C_IDENT + P] = np.eye(P)
    t1[:, C_ONES:C_ONES + P] = 1.0

    t2 = np.zeros((P, C_ALL2), np.float32)
    i = np.arange(P)[:, None]
    for at, q0, k0, n in ((C_DIST, META, 0, NKEYS), (C_DIST + NKEYS, META + P, META, 2 * P)):
        d = (q0 + i) - (k0 + np.arange(n)[None, :])
        t2[:, at:at + n] = np.where((d >= 0) & (d < WIN), -d, -BIG)
    row = np.arange(P)
    seq, u, tok = row // 32, row // 8 % 4, row % 8
    for half in range(2):
        at = C_DIST_S + half * SS
        d = WIN + tok[:, None] - np.arange(WIN)[None, :]
        t2[:, at:at + WIN] = np.where(d < WIN, -d, -BIG)
        new = np.arange(NB * TS)[None, :]
        d = tok[:, None] - new % TS
        own = (new // TS == 4 * half + seq[:, None]) & (d >= 0)
        t2[:, at + WIN:at + SS] = np.where(own, -d, -BIG)
    for g in range(G):
        t2[:, C_SLOPE + g] = 8.0 * 2.0 ** (-(g + 1) / 8.0)
    for par in range(2):
        t2[:, C_SLOPE_S + par] = 8.0 * 2.0 ** (-(2 * u + par + 1) / 8.0)
    return t1, t2


def trunk(nc, x_in, w_in, s0_in, cv_in, ckd_in, vec_in, sink_in, t1_in, t2_in, ckold_in, cvold_in,
          y_out, st_prompt, st_sample, k_out, v_out, ckold_out, cvold_out):
    stack = ExitStack()

    def sb(name, shape, dt=F32, scope=None):
        return (scope or stack).enter_context(nc.sbuf_tensor(name, shape, dt))

    def sem(name):
        return stack.enter_context(nc.semaphore(name))

    with stack:
        raw = sb("raw", [P, RING, SLAB, 256])
        split = sb("split", [P, RING, 2, SLAB, 256], F32R)
        t1 = sb("t1", [P, C_ALL1])
        vec = sb("vec", [P, 4 * KT + 2])
        rstd = sb("rstd", [P, T])
        xT = sb("xT", [P, KT, T])
        ogin = sb("ogin", [P, 4, 2, T])
        xn = ogin[:].rearrange("p a b t -> p (a b) t")
        sqo, sqsum = sb("sqo", [P, 2, T]), sb("sqsum", [P, 2, T])
        VA, VKV, VB, VF, VO = 0, KT, 2 * KT, 3 * KT, 4 * KT
        ident, ones = t1[:, C_IDENT:C_IDENT + P], t1[:, C_ONES:C_ONES + P]

        s1 = stack.enter_context(ExitStack())
        xnH, xnL = sb("xnH", [P, KT, T], F32R, s1), sb("xnL", [P, KT, T], F32R, s1)
        qs, fs, ks, sigq = (sb(n, [P, T], F32, s1) for n in ("qs", "fs", "ks", "sigq"))
        qc = [sb(f"qc{l}", [P, T if l < 4 else TP], F32, s1) for l in range(LEVELS + 1)]
        kr = [ks] + [sb(f"kr{l}", [P, T if l < 4 else TP], F32, s1) for l in range(1, LEVELS + 1)]
        tot_all = sb("tot_all", [P, TOT_N], F32, s1)
        tot = [fs] + [tot_all[:, TOT_AT[l]:TOT_AT[l] + TOT_LEN[l]] for l in range(1, LEVELS + 1)]
        kx, kf = sb("kx", [P, P], F32, s1), sb("kf", [P, T], F32, s1)
        iT = sb("iT", [P, 2, T], F32, s1)
        V = sb("V", [P, 3, DV], F32, s1)
        masked = sb("masked", [P, 8 * P], F32, s1)
        att = sb("att", [P, 4, P], F32, s1)
        attX = sb("attX", [P, 2, TAIL], F32, s1)
        kt, kts = sb("kt", [P, 3, P], F32, s1), sb("kts", [P, P], F32, s1)
        k3, v3 = sb("k3", [P, 2, 3, S4], F32R, s1), sb("v3", [P, 2, 2, 3, S4], F32R, s1)
        k3t, k3s = sb("k3t", [P, 2, P], F32, s1), sb("k3s", [P, NB, P], F32R, s1)
        v3t = sb("v3t", [P, 2, DV], F32R, s1)
        Qs = sb("Qs", [P, TAILP + NB * QS_W], F32, s1)
        S0 = sb("S0", [P, NB, DV], F32, s1)
        Sp = sb("Sp", [P, DV], F32, s1)
        on = sb("on", [P, 3, DV], F32, s1)
        ssq, rs3 = sb("ssq", [P, 3], F32, s1), sb("rs3", [P, 3], F32, s1)
        ms3, norm_const = sb("ms3", [P, 2, 3], F32, s1), sb("norm_const", [P, 3, 3], F32, s1)
        sg, gs, og = (sb(n, [P, 2, T], F32, s1) for n in ("sg", "gs", "og"))
        sq_sum4, sq_new = ogin[:, 0:2].rearrange("p a b t -> p (a b) t"), ogin[:, 2:4].rearrange("p a b t -> p (a b) t")
        sq_new4 = [sq_new, S0[:].rearrange("p b e -> p (b e)")[:, 0:4 * T].rearrange("p (a t) -> p a t", a=4)]
        s1.close()

        s2 = stack.enter_context(ExitStack())
        ogH0, ogL0, ogH1, ogL1 = (sb(n, [P, KT, T], F32R, s2) for n in ("ogH0", "ogL0", "ogH1", "ogL1"))
        ogH, ogL = [ogH0, ogH1], [ogL0, ogL1]
        y = sb("y", [P, KT, TQ], F32, s2)
        s2.close()

        s3 = stack.enter_context(ExitStack())
        xkH, xkL = sb("xkH", [P, KT, T], F32R, s3), sb("xkL", [P, KT, T], F32R, s3)
        kT = sb("kT", [P, KV, T], F32, s3)
        t2 = sb("t2", [P, C_ALL2], F32, s3)
        sinks = sb("sinks", [P, KV, G + 2], F32, s3)
        vtok = sb("vtok", [P, 4, 4 * P], F32, s3)
        ckT, kg = sb("ckT", [P, NB, WIN], F32, s3), sb("kg", [P, T], F32, s3)
        qT, qsam = sb("qT", [P, 4, TQ], F32, s3), sb("qsam", [P, NB, 4, TS], F32, s3)
        sinkg = sb("sinkg", [P, G + 2], F32, s3)
        sb("unused", [P, UNUSED], F32, s3)
        vT, ktmp = sb("vT", [P, 4, T], F32, s3), sb("ktmp", [P, 4, T], F32, s3)
        sgb, ob = vT[:, :, 0:TQ], ktmp[:, :, 0:TQ]
        cv, vg = sb("cv", [P, NB, HD], F32, s3), sb("vg", [P, 4, HD], F32, s3)
        sc, pT = sb("sc", [P, SCORES, SC], F32, s3), sb("pT", [P, 2, 4 * P], F32, s3)
        stat = sb("stat", [P, SCORES, 7, 2], F32, s3)
        gate = sb("gate", [P, 4, TQ], F32, s3)
        s3.close()

        pz = stack.enter_context(nc.psum_tensor("pz", [P, 4, 512], F32))
        RA0, RA1, RO, RT = (stack.enter_context(nc.psum_tensor(n, [P, 512], F32))
                            for n in ("RA0", "RA1", "RO", "RT"))
        scratch = nc.dram_tensor("og_scratch", [ET, P, T], F32, kind="Internal").ap()

        w_loaded = [sem(f"w_loaded{i}") for i in range(RING)]
        (w_hi, w_lo, mm_done, t1_loaded, vec_loaded, s0_loaded, t2_loaded, sink_loaded,
         sq_ready, sq_used, ms_ready, root_ready, rstd_ready, xn_ready, xh_ready, xl_ready,
         sigq_ready, fk_ready, qs_ready, qc0_ready, lev_mul, lev_copied, kx_ready, kf_ready,
         kft_copied, Qs_ready, zeroed, i_copied, lev_done, masked_ready, att_ready,
         cross_copied, kfT_done, kt_copied, kts_ready, vT_done, v_copied, o_done, ssq_ready,
         ms3_ready, rs3_ready, on_ready, s0_scaled, st_done, sp_copied, st_added, g_sig, g_ready,
         oT_done, og_ready, og_stored, st_stored, sp_stored) = (sem(n) for n in (
            "w_hi", "w_lo", "mm_done", "t1_loaded", "vec_loaded", "s0_loaded", "t2_loaded",
            "sink_loaded", "sq_ready", "sq_used", "ms_ready", "root_ready", "rstd_ready", "xn_ready",
            "xh_ready", "xl_ready", "sigq_ready", "fk_ready", "qs_ready", "qc0_ready", "lev_mul",
            "lev_copied", "kx_ready", "kf_ready", "kft_copied", "Qs_ready", "zeroed", "i_copied",
            "lev_done", "masked_ready", "att_ready", "cross_copied", "kfT_done",
            "kt_copied", "kts_ready", "vT_done", "v_copied", "o_done", "ssq_ready", "ms3_ready",
            "rs3_ready", "on_ready", "s0_scaled", "st_done", "sp_copied", "st_added", "g_sig",
            "g_ready", "oT_done", "og_ready", "og_stored", "st_stored", "sp_stored"))
        x_loaded = [sem(f"x_loaded{i}") for i in range(4)]
        og_loaded = [sem(f"og_loaded{i}") for i in range(4)]
        y_ready = [sem(f"y_ready{i}") for i in range(4)]
        (ogh_ready, ogl_ready, x_added, k_copied, k_spread, kv_stored, vtok_done, vtok_copied,
         sinks_ready, staged, ck_loaded, q_copied, qk_done, biased, max_ready, mm_ready, sm_ready,
         exp_ready, den_ready, rden_ready, p_ready, tr_done, pt_copied, pv_done, o_copied,
         g0_copied, gb_sig, gb_ready, ob_ready, slope_ready, y_stored, old_stored, vt_copied,
         obg_stored, qsam_ready, v_staged, ones_loaded, sq_made, sq_added,
         sqo_ready, sqsum_ready, xg_ready, k3h_ready, k3_ready, v3h_ready, v3_ready,
         k3_turned, v3_turned, k3_copied, v3_copied) = (sem(n) for n in (
            "ogh_ready", "ogl_ready", "x_added", "k_copied", "k_spread", "kv_stored", "vtok_done",
            "vtok_copied", "sinks_ready", "staged", "ck_loaded", "q_copied", "qk_done", "biased",
            "max_ready", "mm_ready", "sm_ready", "exp_ready", "den_ready", "rden_ready", "p_ready",
            "tr_done", "pt_copied", "pv_done", "o_copied", "g0_copied", "gb_sig", "gb_ready",
            "ob_ready", "slope_ready", "y_stored", "old_stored", "vt_copied", "obg_stored",
            "qsam_ready", "v_staged", "ones_loaded", "sq_made", "sq_added",
            "sqo_ready", "sqsum_ready", "xg_ready", "k3h_ready", "k3_ready", "v3h_ready", "v3_ready",
            "k3_turned", "v3_turned", "k3_copied", "v3_copied"))

        def early(x, limit):
            return isinstance(x, int) and x < limit

        def load_slab(sp, g, s):
            if not early(g, RING):
                sp.wait_ge(w_lo, g - RING + 1)
            sp.dma_start(raw[:, s % RING], w_in[bass.ds(g, 1)].rearrange("a p n -> p (a n)")
                         ).then_inc(w_loaded[s % RING], 16)

        def split_hi(act, g, s, turn):
            act.wait_ge(w_loaded[s % RING], 16 * (turn + 1))
            if not early(g, RING):
                act.wait_ge(mm_done, g - RING + 1)
            nc.scalar.activation(split[:, s % RING, 0], raw[:, s % RING], ACT.Copy).then_inc(w_hi, 1)

        def split_lo(dve, g, s):
            dve.wait_ge(w_hi, g + 1)
            nc.vector.tensor_tensor(split[:, s % RING, 1], raw[:, s % RING],
                                    split[:, s % RING, 0].bitcast(F32), ALU.subtract).then_inc(w_lo, 1)

        def products(pe, g, s, kt0, bank, high, low, n, first, last, made=None):
            pe.wait_ge(w_lo, g + 1)
            for k in range(SLAB):
                if made:
                    pe.wait_ge(*made(kt0 + k))
                for half in range(2):
                    cols = slice(half * P, half * P + P)
                    out = pz[:, bank + half, 0:n]
                    wh, wl = split[:, s % RING, 0, k, cols], split[:, s % RING, 1, k, cols]
                    begin, end = first and k == 0, last and k == SLAB - 1
                    hi, lo = (x[(kt0 + k) // KT][:, (kt0 + k) % KT, 0:n] for x in (high, low))
                    nc.tensor.matmul(out, wh, hi, start=begin, stop=False)
                    nc.tensor.matmul(out, wh, lo, start=False, stop=False)
                    done = nc.tensor.matmul(out, wl, hi, start=False, stop=end)
            done.then_inc(mm_done, 1)

        def root_dve(dve, c, n):
            dve.wait_ge(sq_used, c + 1)
            nc.vector.tensor_scalar(rstd[:, 0:n], RA0[:, 0:n], 1.0 / D, EPS, ALU.mult, ALU.add).then_inc(ms_ready, 1)
            dve.wait_ge(root_ready, c + 1)
            nc.vector.reciprocal(rstd[:, 0:n], rstd[:, 0:n]).then_inc(rstd_ready, 1)
            dve.wait_ge(rstd_ready, c + 1)

        def root_act(act, c, n):
            act.wait_ge(ms_ready, c + 1)
            nc.scalar.activation(rstd[:, 0:n], rstd[:, 0:n], ACT.Sqrt).then_inc(root_ready, 1)

        def sums_before(c):
            return 1 + (D // 256 - 1) * (c - 1) if c else 0

        def sum_squares(pe, c, n):
            for buf in (sqsum, sqo) if c else (sqsum,):
                if buf is sqsum:
                    pe.wait_ge(sqsum_ready, sums_before(c + 1))
                else:
                    pe.wait_ge(sq_ready, c)
                for e in range(2):
                    done = nc.tensor.matmul(RA0[:, 0:n], ones, buf[:, e, 0:n], start=buf is sqsum and e == 0,
                                            stop=(buf is sqo or c == 0) and e == 1)
            done.then_inc(sq_used, 1)

        def normalise_dve(dve, split_before, gcol, c0, n, tiles):
            for ft in tiles:
                if split_before + ft >= 4:
                    dve.wait_ge(xl_ready, split_before + ft - 3)
                nc.vector.scalar_tensor_tensor(xn[:, ft % 4, 0:n], xT[:, ft, c0:c0 + n], vec[:, gcol + ft:gcol + ft + 1],
                                               rstd[:, c0:c0 + n], ALU.mult, ALU.mult).then_inc(xn_ready, 1)

        def normalise_act(act, made, high, n, tiles):
            for ft in tiles:
                act.wait_ge(xn_ready, made + ft + 1)
                nc.scalar.activation(high[:, ft, 0:n], xn[:, ft % 4, 0:n], ACT.Copy).then_inc(xh_ready, 1)

        def result(engine, c):
            engine.tensor_tensor(y[:, 4 * c:4 * c + 4], xT[:, 4 * c:4 * c + 4, META:T],
                                 rstd[:, 0:TQ].unsqueeze(1).broadcast_to([P, 4, TQ]), ALU.mult).then_inc(y_ready[c], 1)

        def weighted_act(act, tiles):
            for ft in tiles:
                if ft == 0:
                    act.wait_ge(mm_done, BASE_KV - SLABS_OUT // 2)
                    act.wait_ge(x_added, D // 256 - 1)
                if ft == KT - 2:
                    act.wait_ge(x_added, D // 256)
                nc.scalar.activation(xkH[:, ft], xT[:, ft], ACT.Copy, scale=vec[:, VKV + ft:VKV + ft + 1]).then_inc(xh_ready, 1)

        def weighted_dve(dve, tiles):
            for ft in tiles:
                dve.wait_ge(xh_ready, KT + ft + 1)
                nc.vector.scalar_tensor_tensor(xkL[:, ft], xT[:, ft], vec[:, VKV + ft:VKV + ft + 1],
                                               xkH[:, ft].bitcast(F32), ALU.mult, ALU.subtract).then_inc(xl_ready, 1)

        def normalise_pool(pool, made, high, low, n):
            for ft in range(KT):
                pool.wait_ge(xh_ready, made + ft + 1)
                nc.gpsimd.tensor_tensor(low[:, ft, 0:n], xn[:, ft % 4, 0:n], high[:, ft, 0:n].bitcast(F32),
                                        ALU.subtract).then_inc(xl_ready, 1)

        def pair_source(held, c, n):
            return ogin[:, c % 4, :, 0:n] if c < ET // 2 - len(held) else held[c - ET // 2][:, :, 0:n]

        def pair(x, c, n):
            return x[2 * c // KT][:, 2 * c % KT:2 * c % KT + 2, 0:n]

        block = stack.enter_context(nc.Block())

        @block.sync
        def _(sp):
            for c in range(4):
                sp.dma_start(xT[:, 4 * c:4 * c + 4].rearrange("p a n -> p (a n)"), x_in[:, 4 * c * T:(4 * c + 4) * T]
                             ).then_inc(x_loaded[c], 16)

            def head_round(h):
                for s in range(SLABS_H):
                    load_slab(sp, SLABS_H * h + s, s)
                    if early(h, 1):
                        continue
                    if s == 10:
                        sp.wait_ge(st_added, 4 * h)
                        sp.dma_start(st_sample[bass.ds(h - 1, 1)].rearrange("a p n -> p (a n)"),
                                     S0[:].rearrange("p b e -> p (b e)")).then_inc(st_stored, 16)
                        sp.wait_ge(sp_copied, h)
                        sp.dma_start(st_prompt[bass.ds(h - 1, 1)].rearrange("a p n -> p (a n)"), Sp[:]
                                     ).then_inc(sp_stored, 16)
                    if s == 11:
                        sp.wait_ge(st_stored, 16 * h)
                        sp.dma_start(S0[:].rearrange("p b e -> p (b e)"),
                                     s0_in[bass.ds(h, 1)].rearrange("a p n -> p (a n)")).then_inc(s0_loaded, 16)
                        sp.wait_ge(og_ready, h)
                        sp.dma_start(scratch[bass.ds(2 * h - 2, 2)].rearrange("a p n -> p a n"), og[:]
                                     ).then_inc(og_stored, 16)

            head_round(0)
            with sp.Fori(1, H) as h:
                head_round(h)

            def load_pairs(before, pairs, n):
                for c in pairs:
                    if before + c >= 4:
                        sp.wait_ge(ogl_ready, before + c - 3)
                    sp.dma_start(ogin[:, c % 4, :, 0:n], scratch[2 * c:2 * c + 2, :, 0:n].rearrange("a p n -> p a n")
                                 ).then_inc(og_loaded[c % 4], 16)

            def first_out_rounds(base, before, held, n, finish):
                load_pairs(before, range(4), n)
                for s in range(2 * SLABS_OUT):
                    if s >= RING or base == BASE_OUT_A:
                        load_slab(sp, base + s, s)
                    if s >= 7:
                        first = 4 if s == 7 else 2 * s - 8
                        load_pairs(before, range(min(first, ET // 2 - held), min(2 * s - 6, ET // 2 - held)), n)
                    if s == 10:
                        finish()

            def last_states():
                sp.wait_ge(st_added, 4 * H)
                sp.dma_start(st_sample[H - 1], S0[:].rearrange("p b e -> p (b e)")).then_inc(st_stored, 16)
                sp.wait_ge(sp_copied, H)
                sp.dma_start(st_prompt[H - 1], Sp[:]).then_inc(sp_stored, 16)

            sp.wait_ge(og_stored, 16 * (H - 1))
            first_out_rounds(BASE_OUT_A, 0, 1, T, last_states)
            with sp.Fori(2, D // 256) as j:
                for s in range(SLABS_OUT):
                    load_slab(sp, BASE_OUT_A + SLABS_OUT * j + s, s)

            for s in range(SLABS_KV):
                load_slab(sp, BASE_KV + s, s)
                if s == 4:
                    sp.wait_ge(mm_done, BASE_KV)
                    sp.dma_start(t2[:], t2_in).then_inc(t2_loaded, 16)
                    sp.dma_start(sinks[:].rearrange("p a b -> p (a b)"), sink_in).then_inc(sink_loaded, 16)
            for s in range(RING):
                load_slab(sp, BASE_B + s, s)
            sp.wait_ge(k_copied, 2)
            for src in range(2):
                for dst in range(2):
                    sp.dma_start(kT[64 * dst:64 * dst + 64].rearrange("p (j two) t -> p j two t", two=2)[:, :, src],
                                 ktmp[64 * src:64 * src + 64]).then_inc(k_spread, 16)
            sp.dma_start(k_out.rearrange("j p t -> p j t"), ktmp[:]).then_inc(kv_stored, 16)
            sp.wait_ge(vt_copied, 2)
            sp.dma_start(v_out.rearrange("j p t -> p j t"), vT[:]).then_inc(kv_stored, 16)
            sp.wait_ge(kv_stored, 32)

            def group_round(n):
                for s in range(SLABS_G):
                    if early(n, 1) and s < RING:
                        continue
                    load_slab(sp, BASE_B + SLABS_G * n + s, s)
                    if s == 10:
                        if not early(n, 1):
                            sp.wait_ge(pv_done, UNITS * n)
                        sp.dma_start(ckT[:].rearrange("p b j -> p (b j)"),
                                     ckd_in[bass.ds(n, 1)].rearrange("a p n -> p (a n)")).then_inc(ck_loaded, 16)
                        sp.dma_start(cv[:].rearrange("p b j -> p (b j)"),
                                     cv_in[bass.ds(n, 1)].rearrange("a p n -> p (a n)")).then_inc(ck_loaded, 16)
                    if s == 13 and not early(n, 1):
                        sp.wait_ge(ob_ready, n)
                        sp.dma_start(scratch[bass.ds(4 * n - 4, 4), :, 0:TQ].rearrange("a p n -> p a n"), gate[:]
                                     ).then_inc(obg_stored, 16)

            group_round(0)
            with sp.Fori(1, KV) as n:
                group_round(n)
            for s in range(RING):
                load_slab(sp, BASE_OUT_B + s, s)
            sp.wait_ge(obg_stored, 16 * (KV - 1))
            first_out_rounds(BASE_OUT_B, ET // 2, 2, TQ, lambda: None)
            with sp.Fori(2, D // 256) as j:
                for s in range(SLABS_OUT):
                    load_slab(sp, BASE_OUT_B + SLABS_OUT * j + s, s)
            for c in (0, 1, 3, 2):
                sp.wait_ge(y_ready[c], 1)
                sp.dma_start(y_out[4 * c:4 * c + 4].rearrange("a p n -> p a n"), y[:, 4 * c:4 * c + 4]).then_inc(y_stored, 16)
            sp.wait_ge(y_stored, 64)
            sp.wait_ge(st_stored, 16 * H)
            sp.wait_ge(sp_stored, 16 * H)
            sp.wait_ge(kv_stored, 32)
            sp.wait_ge(obg_stored, 16 * (KV - 1))
            sp.wait_ge(old_stored, 32)

        @block.gpsimd
        def _(pool):
            nc.gpsimd.memset(Qs[:], 0.0)
            nc.gpsimd.memset(attX[:], 0.0)
            for i, value in enumerate((1.0 / DV, EPS, -0.5)):
                nc.gpsimd.memset(norm_const[:, i], value)
            nc.gpsimd.memset(ssq[:], 0.0).then_inc(zeroed, 1)
            normalise_pool(pool, 0, xnH, xnL, T)
            pool.dma_start(ckold_out, ckold_in).then_inc(old_stored, 16)
            pool.dma_start(cvold_out, cvold_in).then_inc(old_stored, 16)
            pool.wait_ge(ones_loaded, 16)

            def keep(out, x):
                one = t1[0:x.shape[0], C_ONES:C_ONES + 1]
                for _ in range(len(x.shape) - 2):
                    one = one.unsqueeze(2)
                return nc.gpsimd.tensor_tensor(out, x, one.broadcast_to(list(x.shape)), ALU.mult)

            def tail(h):
                pool.wait_ge(ssq_ready, h + 1)
                nc.gpsimd.tensor_tensor(ms3[:, 0], ssq[:], norm_const[:, 0], ALU.mult).then_inc(ms3_ready, 1)
                pool.wait_ge(ms3_ready, 2 * h + 1)
                nc.gpsimd.tensor_tensor(ms3[:, 1], ms3[:, 0], norm_const[:, 1], ALU.add).then_inc(ms3_ready, 1)
                pool.wait_ge(ms3_ready, 2 * h + 2)
                nc.gpsimd.tensor_tensor(rs3[:], ms3[:, 1], norm_const[:, 2], ALU.pow).then_inc(rs3_ready, 1)

            def head(h):
                for l in range(LEVELS):
                    n, b = LV_TOKENS[l], 1 << l
                    if l == 0:
                        pool.wait_ge(qc0_ready, h + 1)
                    else:
                        pool.wait_ge(lev_mul, LEVELS * h + l)
                        pool.wait_ge(lev_copied, LEVELS * h + l)

                    def halves(x, which):
                        return x[:, 0:n].rearrange("p (b two h) -> p b two h", two=2, h=b)[:, :, which]
                    keep(halves(qc[l + 1], 0), halves(qc[l], 0))
                    nc.gpsimd.tensor_copy(halves(kr[l + 1], 1), halves(kr[l], 1)).then_inc(lev_copied, 1)
                pool.wait_ge(lev_copied, LEVELS * (h + 1))
                keep(kf[:, 2 * P:TP], kr[4][:, 2 * P:TP])
                nc.gpsimd.tensor_copy(kf[:, TP:T], kr[3][:, TP:T]).then_inc(kft_copied, 1)
                pool.wait_ge(kt_copied, h + 1)
                nc.gpsimd.tensor_tensor(kts[0:TAIL], kt[0:TAIL, 2], t1[0:TAIL, C_ROWS:C_ROWS + 1].broadcast_to([TAIL, P]), ALU.mult)
                pool.wait_ge(k3_copied, h + 1)
                for g in range(2):
                    done = nc.gpsimd.tensor_tensor(
                        k3s[0:STACK, 4 * g:4 * g + 4], k3t[0:STACK, g:g + 1].broadcast_to([STACK, 4, P]),
                        t1[0:STACK, C_ROWS4:C_ROWS4 + 4].unsqueeze(2).broadcast_to([STACK, 4, P]), ALU.mult)
                done.then_inc(kts_ready, 1)
                pool.wait_ge(o_done, 2 * (h + 1))
                nc.gpsimd.tensor_tensor(S0[:], S0[:], tot[3][:, TP // 8:TP // 8 + NB].unsqueeze(2).broadcast_to([P, NB, DV]),
                                        ALU.mult).then_inc(s0_scaled, 1)
                tail(h)

            head(0)
            with pool.Fori(1, H) as h:
                head(h)

            normalise_pool(pool, 2 * KT, xkH, xkL, TQ)

            def stage(n):
                if not early(n, 1):
                    pool.wait_ge(qk_done, UNITS * n)
                    pool.wait_ge(sm_ready, UNITS * n)
                keep(kg[:].unsqueeze(1), kT[:, bass.ds(n, 1)])
                nc.gpsimd.tensor_copy(sinkg[:].unsqueeze(1), sinks[:, bass.ds(n, 1)]).then_inc(staged, 1)
                if not early(n, 1):
                    pool.wait_ge(pv_done, UNITS * n)
                keep(vg[:, 1:3], vtok[:, 1:3, bass.ds(n * HD, HD)])
                nc.gpsimd.tensor_copy(vg[0:META, 0:1], vtok[0:META, 0:1, bass.ds(n * HD, HD)])
                nc.gpsimd.tensor_copy(vg[0:NB * TS, 3:4], vtok[0:NB * TS, 3:4, bass.ds(n * HD, HD)]).then_inc(v_staged, 1)
                pool.wait_ge(q_copied, 2 * (n + 1))
                for w in range(4):
                    done = keep(qsam[:, :, w], qT[:, w, SEQ:TQ].rearrange("p (b t) -> p b t", t=TS))
                done.then_inc(qsam_ready, 1)

            nc.gpsimd.memset(vg[:, 3], 0.0).then_inc(zeroed, 1)
            pool.wait_ge(zeroed, 2)
            pool.wait_ge(k_spread, 64)
            pool.wait_ge(vtok_copied, 4)
            pool.wait_ge(sinks_ready, 1)
            stage(0)
            with pool.Fori(1, KV) as n:
                stage(n)
            pool.wait_ge(xg_ready, KT)
            pool.wait_ge(rstd_ready, 3)
            result(nc.gpsimd, 3)

        @block.scalar
        def _(act):
            act.dma_start(t1[:, C_ROWS:], t1_in[:, C_ROWS:]).then_inc(ones_loaded, 16)
            act.dma_start(vec[:], vec_in).then_inc(vec_loaded, 16)
            for c in range(1, 4):
                act.wait_ge(x_loaded[c], 16)
                if c == 3:
                    act.wait_ge(sq_added, 2)
                nc.scalar.activation(sq_new4[(c - 1) % 2], xT[:, 4 * c:4 * c + 4], ACT.Square).then_inc(sq_made, 1)
            act.dma_start(t1[:, 0:C_ROWS], t1_in[:, 0:C_ROWS]).then_inc(t1_loaded, 16)
            act.wait_ge(sq_added, 4)
            act.dma_start(S0[:].rearrange("p b e -> p (b e)"), s0_in[0]).then_inc(s0_loaded, 16)
            for s in range(2):
                split_hi(act, s, s, 0)
            root_act(act, 0, T)
            for s in range(RING):
                if s < 2:
                    split_hi(act, s + 2, s + 2, 0)
                normalise_act(act, 0, xnH, T, range(4 * s, 4 * s + 4))

            def finish_head(h, s):
                t = h - 1
                if s == 1:
                    act.wait_ge(k3_turned, t + 1)
                    if not early(h, 2):
                        act.wait_ge(o_done, 2 * t)
                    nc.scalar.activation(att[:, 2], RO[:, 0:P], ACT.Copy)
                    nc.scalar.activation(attX[:, :, 0:TAILP], RO[:, P:P + 2 * TAILP].rearrange("p (a n) -> p a n", a=2),
                                         ACT.Copy).then_inc(cross_copied, 1)
                    act.wait_ge(kfT_done, t + 1)
                    nc.scalar.activation(kt[:, 0:2], RT[:, 0:2 * P].rearrange("p (a n) -> p a n", a=2), ACT.Copy)
                    nc.scalar.activation(kt[0:TAIL, 2], RT[0:TAIL, 2 * P:3 * P], ACT.Copy).then_inc(kt_copied, 1)
                    nc.scalar.activation(k3t[0:STACK], RO[0:STACK, 2 * P:4 * P].rearrange("p (g n) -> p g n", g=2),
                                         ACT.Copy).then_inc(k3_copied, 1)
                if s == 2:
                    act.wait_ge(vT_done, 2 * (t + 1))
                    nc.scalar.activation(V[:, 0:2], RA0[:].rearrange("p (a n) -> p a n", a=2), ACT.Copy)
                    nc.scalar.activation(V[0:TAIL, 2], RA1[0:TAIL, 0:DV], ACT.Copy).then_inc(v_copied, 1)
                    act.wait_ge(v3_turned, t + 1)
                    nc.scalar.activation(v3t[0:STACK], pz[0:STACK, 2].rearrange("p (g n) -> p g n", g=2),
                                         ACT.Copy).then_inc(v3_copied, 1)
                if s == 3:
                    act.wait_ge(mm_done, SLABS_H * h)
                    if not early(h, 2):
                        act.wait_ge(g_ready, t)
                    nc.scalar.activation(sg[:], pz[:, 0:2, 0:T], ACT.Sigmoid).then_inc(g_sig, 1)
                    act.wait_ge(o_done, 2 * (t + 1))
                    nc.scalar.activation(on[:, 0], RO[:, 0:DV], ACT.Square, accum_out=ssq[:, 0:1])
                    nc.scalar.activation(on[:, 1], RO[:, DV:2 * DV], ACT.Square, accum_out=ssq[:, 1:2])
                    nc.scalar.activation(on[0:TAIL, 2], RA1[0:TAIL, 0:DV], ACT.Square, accum_out=ssq[0:TAIL, 2:3]
                                         ).then_inc(ssq_ready, 1)
                if s == 4:
                    outputs(t, h)

            def head_round(h):
                for s in range(SLABS_H):
                    if not (early(h, 1) and s < RING):
                        split_hi(act, SLABS_H * h + s, s, SLABS_H // RING * h + s // RING)
                    if not early(h, 1):
                        finish_head(h, s)
                    if s == 7:
                        act.wait_ge(mm_done, SLABS_H * h + 4)
                        if not early(h, 1):
                            act.wait_ge(qs_ready, h)
                            act.wait_ge(kfT_done, h)
                            act.wait_ge(kf_ready, h)
                        nc.scalar.activation(sigq[:], pz[:, 0, 0:T], ACT.Sigmoid).then_inc(sigq_ready, 1)
                        nc.scalar.activation(fs[:], pz[:, 1, 0:T], ACT.Sigmoid)
                        nc.scalar.activation(ks[:], pz[:, 1, 0:T], ACT.Sigmoid, scale=-1.0).then_inc(fk_ready, 1)
                    if s == 9:
                        act.wait_ge(lev_mul, LEVELS * h + 3)
                        act.wait_ge(lev_copied, LEVELS * h + 3)
                        if not early(h, 1):
                            act.wait_ge(k3_turned, h)
                        nc.scalar.activation(k3[:, :, 0:2], kr[3][:, TP:T].rearrange("p (g t) -> p g t", g=2).unsqueeze(2)
                                             .broadcast_to([P, 2, 2, S4]), ACT.Copy).then_inc(k3h_ready, 1)
                    if s == 11:
                        act.wait_ge(mm_done, SLABS_H * h + 8)
                        if not early(h, 1):
                            act.wait_ge(v3_turned, h)
                        for e in range(2):
                            done = nc.scalar.activation(
                                v3[:, e, :, 0::2], pz[:, 2 + e, TP:T].rearrange("p (g t) -> p g t", g=2).unsqueeze(2)
                                .broadcast_to([P, 2, 2, S4]), ACT.Copy)
                        done.then_inc(v3h_ready, 1)
                        if not early(h, 1):
                            act.wait_ge(vT_done, 2 * h)
                        nc.scalar.activation(iT[:], pz[:, 2:4, 0:T], ACT.Copy).then_inc(i_copied, 1)

            def outputs(t, h):
                act.wait_ge(st_done, 5 * t + 1)
                if not early(h, 2):
                    act.wait_ge(sp_stored, 16 * t)
                nc.scalar.activation(Sp[:], RT[:, 0:DV], ACT.Copy).then_inc(sp_copied, 1)
                act.wait_ge(rs3_ready, t + 1)
                if not early(h, 2):
                    act.wait_ge(oT_done, t)
                nc.scalar.activation(on[:, 0], RO[:, 0:DV], ACT.Copy, scale=rs3[:, 0:1])
                nc.scalar.activation(on[:, 1], RO[:, DV:2 * DV], ACT.Copy, scale=rs3[:, 1:2])
                nc.scalar.activation(on[0:TAIL, 2], RA1[0:TAIL, 0:DV], ACT.Copy, scale=rs3[0:TAIL, 2:3]
                                     ).then_inc(on_ready, 1)

            head_round(0)
            head_round(1)
            with act.Fori(2, H) as h:
                head_round(h)

            def gather(before, pairs, held, ready, n):
                for c in pairs:
                    if c < ET // 2 - len(held):
                        turn = c // 4 + (before > 0) * (3 if c % 4 == 3 else 4)
                        act.wait_ge(og_loaded[c % 4], 16 * (turn + 1))
                    else:
                        act.wait_ge(*ready)
                    nc.scalar.activation(pair(ogH, c, n), pair_source(held, c, n), ACT.Copy).then_inc(ogh_ready, 1)

            def out_round(base, j, hooks=None):
                for s in range(SLABS_OUT):
                    split_hi(act, base + SLABS_OUT * j + s, s, base // RING + SLABS_OUT // RING * j + s // RING)
                    if hooks:
                        hooks(SLABS_OUT * j + s)

            def out_projection(base, before, held, ready, overlaid, finish, n, last=None):
                def hooks(s):
                    if s == 3:
                        act.wait_ge(mm_done, base)
                        gather(before, (0, 1), held, ready, n)
                    finish(s)
                    if s == 3:
                        gather(before, (2, 3), held, ready, n)
                    if s == 6:
                        for semaphore, value in overlaid:
                            act.wait_ge(semaphore, value)
                    if 4 <= s < 10:
                        gather(before, (2 * s - 4, 2 * s - 3), held, ready, n)
                out_round(base, 0, hooks)
                out_round(base, 1, hooks)
                with act.Fori(2, D // 256 - 1) as j:
                    out_round(base, j)
                out_round(base, D // 256 - 1, last)

            out_projection(BASE_OUT_A, 0, [og[:]], (og_ready, H), [(st_done, 5 * H), (s0_scaled, H)],
                           lambda s: finish_head(H, s), T,
                           lambda s: weighted_act(act, range(4)) if s == BASE_KV - BASE_OUT_A - 1 else None)

            for s in range(SLABS_KV):
                split_hi(act, BASE_KV + s, s, BASE_KV // RING + s // RING)
                if s < 3:
                    weighted_act(act, range(4 * s + 4, min(4 * s + 8, KT - 2)))
                if s == 3:
                    weighted_act(act, range(KT - 2, KT))
                if s == 4:
                    root_act(act, 1, T)
            for s in range(RING):
                split_hi(act, BASE_B + s, s, BASE_B // RING)
                normalise_act(act, KT, xkH, TQ, range(4 * s, 4 * s + 4))
            act.wait_ge(vtok_done, 4)
            nc.scalar.activation(vtok[0:META, 0], RA0[0:META, :], ACT.Copy).then_inc(vtok_copied, 1)
            nc.scalar.activation(vtok[:, 1], RA1[:, :], ACT.Copy).then_inc(vtok_copied, 1)
            nc.scalar.activation(vtok[:, 2], RO[:, :], ACT.Copy).then_inc(vtok_copied, 1)
            nc.scalar.activation(vtok[0:NB * TS, 3], RT[0:NB * TS, :], ACT.Copy).then_inc(vtok_copied, 1)

            def exps(n, u):
                k, r = UNITS * n + u, u % SCORES
                act.wait_ge(sm_ready, k + 1)
                if u < G:
                    parts = [(sc[:, r, 0:NKEYS], 0), (sc[:, r, NKEYS:SC], 1)]
                else:
                    parts = [(sc[:, r, 0:SS], 0), (sc[:, r, SS:2 * SS], 1)]
                for part, i in parts:
                    nc.scalar.activation(part, part, ACT.Exp, bias=stat[:, r, 2, i:i + 1], scale=HD ** -0.5,
                                         accum_out=stat[:, r, 5, i:i + 1])
                nc.scalar.activation(stat[:, r, 4], stat[:, r, 3], ACT.Exp, scale=HD ** -0.5).then_inc(exp_ready, 1)

            def copy_p(n, u):
                k, r = UNITS * n + u, u % 2
                act.wait_ge(tr_done, k + 1)
                if not early(k, 2):
                    act.wait_ge(pv_done, k - 1)
                if u < G:
                    nc.scalar.activation(pT[:, r, P:4 * P], RT[:, P:4 * P], ACT.Copy)
                    nc.scalar.activation(pT[0:META, r, 0:P], RT[0:META, 0:P], ACT.Copy).then_inc(pt_copied, 1)
                else:
                    def fours(x):
                        return x.rearrange("p (two n) -> p two n", two=2)
                    nc.scalar.activation(fours(pT[:, r])[:, :, 0:P], fours(RT[:])[:, :, 0:P], ACT.Copy)
                    nc.scalar.activation(fours(pT[0:NB * TS, r])[:, :, P:2 * P], fours(RT[0:NB * TS])[:, :, P:2 * P],
                                         ACT.Copy).then_inc(pt_copied, 1)

            def copy_o(n, u):
                if u < G:
                    if u % 2:
                        act.wait_ge(pv_done, UNITS * n + u + 1)
                        nc.scalar.activation(ob[:, u // 2, 0:SEQ], RO[:, 0:SEQ], ACT.Copy).then_inc(o_copied, 1)
                elif u == UNITS - 1:
                    act.wait_ge(pv_done, UNITS * (n + 1))
                    for w in range(4):
                        done = nc.scalar.activation(
                            ob[:, w, SEQ:TQ].rearrange("p (b t) -> p b t", t=TS),
                            RO[:, 0:SEQ].rearrange("p (b w t) -> p w b t", w=4, t=TS)[:, w], ACT.Copy)
                    done.then_inc(o_copied, 1)

            def finish_group(n, s):
                for u in range(UNITS):
                    for at, what in ((15 + u, copy_o), (13 + u, copy_p), (10 + u, exps)):
                        if at == s + SLABS_G:
                            what(n - 1, u)
                if s == 3:
                    act.wait_ge(mm_done, BASE_B + SLABS_G * n)
                    act.wait_ge(g0_copied, n)
                    nc.scalar.activation(sgb[:, 0:2], gate[:, 0:2], ACT.Sigmoid)
                    nc.scalar.activation(sgb[:, 2:4], pz[:, 2:4, 0:TQ], ACT.Sigmoid).then_inc(gb_sig, 1)

            def group_round(n):
                for s in range(SLABS_G):
                    if not (early(n, 1) and s < RING):
                        split_hi(act, BASE_B + SLABS_G * n + s, s, BASE_B // RING + SLABS_G // RING * n + s // RING)
                    if not early(n, 1):
                        finish_group(n, s)
                    for u in range(UNITS):
                        for at, what in ((15 + u, copy_o), (13 + u, copy_p), (10 + u, exps)):
                            if at == s:
                                what(n, u)
                    if s in (7, 11):
                        j = s // 4 - 1
                        act.wait_ge(mm_done, BASE_B + SLABS_G * n + 4 * j + 4)
                        nc.scalar.activation(qT[:, 2 * j:2 * j + 2], pz[:, 2 * j:2 * j + 2, 0:TQ], ACT.Copy).then_inc(q_copied, 1)
                    if s == 15:
                        act.wait_ge(mm_done, BASE_B + SLABS_G * n + 12)
                        if not early(n, 1):
                            act.wait_ge(obg_stored, 16 * n)
                        nc.scalar.activation(gate[:, 0:2], pz[:, 0:2, 0:TQ], ACT.Copy).then_inc(g0_copied, 1)

            act.wait_ge(kv_stored, 32)
            group_round(0)
            with act.Fori(1, KV) as n:
                group_round(n)
            out_projection(BASE_OUT_B, ET // 2, [gate[:, 0:2], gate[:, 2:4]], (ob_ready, KV),
                           [(sm_ready, UNITS * KV), (v_staged, KV), (qsam_ready, KV)],
                           lambda s: finish_group(KV, s), TQ)
            for f in range(KT):
                if f == 0:
                    act.wait_ge(sqsum_ready, sums_before(3))
                if f == KT - 2:
                    root_act(act, 2, TQ)
                    act.wait_ge(sq_ready, 2)
                nc.scalar.activation(xT[:, f, META:T], xT[:, f, META:T], ACT.Copy, scale=vec[:, VF + f:VF + f + 1]
                                     ).then_inc(xg_ready, 1)

        @block.vector
        def _(dve):
            quarters = [xT[:, 4 * c:4 * c + 4] for c in range(4)]
            dve.wait_ge(x_loaded[0], 16)
            nc.vector.tensor_tensor(sq_sum4, quarters[0], quarters[0], ALU.mult).then_inc(sq_added, 1)
            for c in range(1, 4):
                dve.wait_ge(sq_made, c)
                dve.wait_ge(sq_added, c)
                nc.vector.tensor_tensor(sq_sum4, sq_sum4, sq_new4[(c - 1) % 2], ALU.add).then_inc(sq_added, 1)
            dve.wait_ge(sq_added, 4)
            nc.vector.tensor_tensor(sqsum[:], sq_sum4[:, 0:2], sq_sum4[:, 2:4], ALU.add).then_inc(sqsum_ready, 1)
            for s in range(2):
                split_lo(dve, s, s)
            root_dve(dve, 0, T)
            dve.wait_ge(vec_loaded, 16)
            for s in range(RING):
                if s >= 2:
                    split_lo(dve, s, s)
                normalise_dve(dve, 0, VA, 0, T, range(4 * s, 4 * s + 4))
            dve.wait_ge(t1_loaded, 16)
            dve.wait_ge(zeroed, 1)

            def doubling(h, l):
                n, b = LV_TOKENS[l], 1 << l
                dve.wait_ge(lev_copied, LEVELS * h + l)
                dve.wait_ge(lev_mul, LEVELS * h + l)

                def halves(x, which):
                    return x[:, 0:n].rearrange("p (b two h) -> p b two h", two=2, h=b)[:, :, which]
                blocks = tot[l][:, 0:n // b].rearrange("p (b two) -> p b two", two=2)
                shape = [P, n // (2 * b), b]
                nc.vector.tensor_tensor(halves(qc[l + 1], 1), halves(qc[l], 1), blocks[:, :, 0:1].broadcast_to(shape), ALU.mult)
                nc.vector.tensor_tensor(halves(kr[l + 1], 0), halves(kr[l], 0), blocks[:, :, 1:2].broadcast_to(shape), ALU.mult)
                nc.vector.tensor_tensor(tot[l + 1][:, 0:n // (2 * b)], blocks[:, :, 0], blocks[:, :, 1], ALU.mult
                                        ).then_inc(lev_mul, 1)

            def attention_tile(h, i):
                if i == 0:
                    dve.wait_ge(lev_done, 5 * h + 1)
                    if not early(h, 1):
                        dve.wait_ge(o_done, 2 * h)
                        dve.wait_ge(att_ready, 3 * h)
                    nc.vector.tensor_tensor(masked[0:TAIL, 0:5 * TAIL], RT[0:TAIL, 0:5 * TAIL],
                                            t1[0:TAIL, C_MASK3:C_MASK3 + 5 * TAIL], ALU.mult).then_inc(masked_ready, 1)
                    dve.wait_ge(masked_ready, 5 * h + 1)
                    nc.vector.tensor_reduce(out=att[0:TAIL, 3, 0:TAIL],
                                            in_=masked[0:TAIL, 0:5 * TAIL].rearrange("p (l t) -> p t l", t=TAIL),
                                            axis=AX.X, op=ALU.add).then_inc(att_ready, 1)
                else:
                    dve.wait_ge(att_ready, 3 * h + i)
                    for k, bank in ((0, RA0), (1, RA1)):
                        dve.wait_ge(lev_done, 5 * h + 2 * i + k)
                        nc.vector.tensor_tensor(masked[:, 512 * k:512 * k + 512], bank[:],
                                                t1[:, C_MASK + 512 * k:C_MASK + 512 * k + 512], ALU.mult
                                                ).then_inc(masked_ready, 1)
                    dve.wait_ge(masked_ready, 5 * h + 2 * i + 1)
                    nc.vector.tensor_reduce(out=att[:, i - 1], in_=masked[:].rearrange("p (l t) -> p t l", t=P),
                                            axis=AX.X, op=ALU.add).then_inc(att_ready, 1)

            def add_states(t, pair):
                bank = RA0 if pair % 2 == 0 else RT
                dve.wait_ge(st_done, 5 * t + pair + 2)
                dve.wait_ge(s0_scaled, t + 1)
                nc.vector.tensor_tensor(S0[:, 2 * pair:2 * pair + 2], bank[:].rearrange("p (a n) -> p a n", a=2),
                                        S0[:, 2 * pair:2 * pair + 2], ALU.add).then_inc(st_added, 1)

            def gate_a(t, h):
                dve.wait_ge(oT_done, t + 1)
                dve.wait_ge(g_ready, t + 1)
                if not early(h, 2):
                    dve.wait_ge(og_stored, 16 * t)
                nc.vector.scalar_tensor_tensor(og[:, 0], RO[:, 0:T], vec[:, VO:VO + 1], gs[:, 0], ALU.mult, ALU.mult)
                nc.vector.scalar_tensor_tensor(og[:, 1], RA1[:, 0:T], vec[:, VO + 1:VO + 2], gs[:, 1], ALU.mult, ALU.mult
                                               ).then_inc(og_ready, 1)

            def finish_head(h, s):
                t = h - 1
                if s == 0:
                    attention_tile(t, 2)
                if s == 3:
                    dve.wait_ge(g_sig, t + 1)
                    nc.vector.tensor_tensor(gs[:], sg[:], pz[:, 0:2, 0:T], ALU.mult).then_inc(g_ready, 1)
                if s == 4:
                    add_states(t, 0)
                if s == 5:
                    add_states(t, 1)
                    add_states(t, 2)
                if s == 6:
                    add_states(t, 3)
                if s == 7:
                    gate_a(t, h)

            def head_round(h):
                for s in range(SLABS_H):
                    if not (early(h, 1) and s < RING):
                        split_lo(dve, SLABS_H * h + s, s)
                    if not early(h, 1):
                        finish_head(h, s)
                    if s == 7:
                        dve.wait_ge(sigq_ready, h + 1)
                        nc.vector.scalar_tensor_tensor(qs[:], sigq[:], P ** -0.5, pz[:, 0, 0:T], ALU.mult, ALU.mult
                                                       ).then_inc(qs_ready, 1)
                        dve.wait_ge(fk_ready, h + 1)
                        dve.wait_ge(qs_ready, h + 1)
                        if not early(h, 1):
                            dve.wait_ge(s0_scaled, h)
                        nc.vector.tensor_tensor(qc[0][:], qs[:], fs[:], ALU.mult).then_inc(qc0_ready, 1)
                        dve.wait_ge(qc0_ready, h + 1)
                        for l in range(4):
                            doubling(h, l)
                    if s == 8:
                        for l in range(4, LEVELS):
                            doubling(h, l)
                        dve.wait_ge(lev_mul, LEVELS * (h + 1))
                        dve.wait_ge(lev_copied, LEVELS * (h + 1))
                        last, tail_decay = tot[7][:, 1:2], tot[4][:, TP // 16 - 1:TP // 16]
                        nc.vector.tensor_scalar(kx[:], kr[7][:, 0:P], last, None, ALU.mult).then_inc(kx_ready, 1)
                        nc.vector.tensor_scalar(kf[:, P:2 * P], kr[7][:, P:2 * P], tail_decay, None, ALU.mult)
                        dve.wait_ge(kx_ready, h + 1)
                        nc.vector.tensor_scalar(kf[:, 0:P], kx[:], tail_decay, None, ALU.mult).then_inc(kf_ready, 1)
                        nc.vector.tensor_copy(
                            Qs[:, TAILP:TAILP + NB * QS_W].rearrange("p (b c) -> p b c", c=QS_W)[:, :, 0:TS],
                            qc[3][:, TP:T].rearrange("p (b t) -> p b t", t=TS)).then_inc(Qs_ready, 1)
                    if s == 9:
                        dve.wait_ge(k3h_ready, h + 1)
                        nc.vector.tensor_tensor(k3[:, :, 2], kr[3][:, TP:T].rearrange("p (g t) -> p g t", g=2),
                                                k3[:, :, 0].bitcast(F32), ALU.subtract).then_inc(k3_ready, 1)
                    if s == 10:
                        attention_tile(h, 0)
                    if s == 11:
                        dve.wait_ge(v3h_ready, h + 1)
                        dve.wait_ge(i_copied, h + 1)
                        nc.vector.tensor_tensor(v3[:, :, :, 1], iT[:, :, TP:T].rearrange("p e (g t) -> p e g t", g=2),
                                                v3[:, :, :, 0].bitcast(F32), ALU.subtract).then_inc(v3_ready, 1)
                        attention_tile(h, 1)

            head_round(0)
            head_round(1)
            with dve.Fori(2, H) as h:
                head_round(h)

            def gather(before, pairs, held, n):
                for c in pairs:
                    dve.wait_ge(ogh_ready, before + c + 1)
                    nc.vector.tensor_tensor(pair(ogL, c, n), pair_source(held, c, n), pair(ogH, c, n).bitcast(F32),
                                            ALU.subtract).then_inc(ogl_ready, 1)

            def add_pair(base, c, j, bank, c0, n):
                at = (D // 256) * (c - 1) + j
                dve.wait_ge(mm_done, base + SLABS_OUT * (j + 1))
                x = xT[:, bass.ds(2 * j, 2), c0:c0 + n]
                nc.vector.tensor_tensor(x, x, pz[:, bank:bank + 2, 0:n], ALU.add).then_inc(x_added, 1)
                dve.wait_ge(x_added, at + 1)
                if early(j, 1):
                    nc.vector.tensor_tensor(sqsum[:, :, 0:n], x, x, ALU.mult).then_inc(sqsum_ready, 1)
                elif isinstance(j, int) and j == D // 256 - 1:
                    nc.vector.tensor_tensor(sqo[:, :, 0:n], x, x, ALU.mult).then_inc(sq_ready, 1)
                    return
                else:
                    nc.vector.tensor_tensor(sqo[:, :, 0:n], x, x, ALU.mult).then_inc(sqo_ready, 1)
                    dve.wait_ge(sqo_ready, (D // 256 - 2) * (c - 1) + j)
                    nc.vector.tensor_tensor(sqsum[:, :, 0:n], sqsum[:, :, 0:n], sqo[:, :, 0:n], ALU.add).then_inc(sqsum_ready, 1)
                dve.wait_ge(sqsum_ready, sums_before(c) + j + 1)

            def out_projection(base, c, held, finish, c0, n, last=None):
                def out_round(j, par, hooks=None):
                    for s in range(SLABS_OUT):
                        split_lo(dve, base + SLABS_OUT * j + s, s)
                        if hooks:
                            hooks(SLABS_OUT * j + s)
                        if s == 3 and not early(j, 1):
                            add_pair(base, c, j - 1, 2 * (1 - par), c0, n)

                def hooks(s):
                    before = ET // 2 * (c - 1)
                    if s == 3:
                        gather(before, (0, 1), held, n)
                    finish(s)
                    if s == 3:
                        gather(before, (2, 3), held, n)
                    if 4 <= s < 10:
                        gather(before, (2 * s - 4, 2 * s - 3), held, n)
                out_round(0, 0, hooks)
                out_round(1, 1, hooks)
                with dve.Fori(2, D // 256 - 2, 2) as j:
                    out_round(j, 0)
                    out_round(j + 1, 1)
                out_round(D // 256 - 2, 0)
                out_round(D // 256 - 1, 1, last)

            out_projection(BASE_OUT_A, 1, [og[:]], lambda s: finish_head(H, s), 0, T,
                           lambda s: weighted_dve(dve, range(4)) if s == BASE_KV - BASE_OUT_A - 1 else None)

            def scaled_result(out, banks, slabs, ready):
                dve.wait_ge(mm_done, BASE_KV + slabs)
                nc.vector.tensor_tensor(out, pz[:, banks, 0:T], rstd[:].unsqueeze(1).broadcast_to([P, 2, T]), ALU.mult
                                        ).then_inc(ready, 1)

            for s in range(SLABS_KV):
                split_lo(dve, BASE_KV + s, s)
                if s < 3:
                    weighted_dve(dve, range(4 * s + 4, min(4 * s + 8, KT - 2)))
                if s == 3:
                    add_pair(BASE_OUT_A, 1, D // 256 - 1, 2, 0, T)
                    weighted_dve(dve, range(KT - 2, KT))
                if s == 4:
                    root_dve(dve, 1, T)
                if s == 7:
                    scaled_result(ktmp[:, 0:2], slice(0, 2), 4, k_copied)
                if s == 11:
                    scaled_result(ktmp[:, 2:4], slice(2, 4), 8, k_copied)
                if s == 15:
                    scaled_result(vT[:, 0:2], slice(0, 2), 12, vt_copied)
                    dve.wait_ge(sink_loaded, 16)
                    dve.wait_ge(t2_loaded, 16)
                    nc.vector.tensor_scalar(sinks[:], sinks[:], HD ** 0.5, None, ALU.mult).then_inc(sinks_ready, 1)
            for s in range(RING):
                split_lo(dve, BASE_B + s, s)
                dve.wait_ge(mm_done, BASE_KV + 13 + s)
                if s == 3:
                    scaled_result(vT[:, 2:4], slice(2, 4), 16, vt_copied)
                normalise_dve(dve, 2 * KT, VB, META, TQ, range(4 * s, 4 * s + 4))

            def scores(n, u):
                k, r = UNITS * n + u, u % SCORES
                bank = RA0 if u % 2 == 0 else RA1
                dve.wait_ge(qk_done, k + 1)
                dve.wait_ge(staged, n + 1)
                if not early(k, SCORES):
                    dve.wait_ge(tr_done, k - SCORES + 1)
                if u < G:
                    nc.vector.scalar_tensor_tensor(sc[:, r, 0:SC], t2[:, C_DIST:C_DIST + SC],
                                                   t2[:, C_SLOPE + u:C_SLOPE + u + 1], bank[:, 0:SC],
                                                   ALU.mult, ALU.add).then_inc(biased, 1)
                    parts = [(0, NKEYS), (NKEYS, SC)]
                    sink = sinkg[:, u:u + 1].broadcast_to([P, 2])
                else:
                    slope = C_SLOPE_S + u - G
                    nc.vector.scalar_tensor_tensor(sc[:, r, 0:2 * SS], t2[:, C_DIST_S:C_DIST_S + 2 * SS],
                                                   t2[:, slope:slope + 1], bank[:, 0:2 * SS],
                                                   ALU.mult, ALU.add).then_inc(biased, 1)
                    parts = [(0, SS), (SS, 2 * SS)]
                    sink = sinkg[:, u:u + 1].broadcast_to([P, 2])
                dve.wait_ge(biased, k + 1)
                for i, (a, b) in enumerate(parts):
                    done = nc.vector.reduce_max(stat[:, r, 0, i:i + 1], sc[:, r, a:b], AX.X)
                done.then_inc(max_ready, 1)
                dve.wait_ge(max_ready, k + 1)
                nc.vector.tensor_tensor(stat[:, r, 1], stat[:, r, 0], sink, ALU.max).then_inc(mm_ready, 1)
                dve.wait_ge(mm_ready, k + 1)
                nc.vector.tensor_scalar(stat[:, r, 2], stat[:, r, 1], -HD ** -0.5, None, ALU.mult)
                nc.vector.tensor_tensor(stat[:, r, 3], sink, stat[:, r, 1], ALU.subtract).then_inc(sm_ready, 1)

            def divide(n, u):
                k, r = UNITS * n + u, u % SCORES
                dve.wait_ge(exp_ready, k + 1)
                nc.vector.tensor_tensor(stat[:, r, 5], stat[:, r, 5], stat[:, r, 4], ALU.add).then_inc(den_ready, 1)
                dve.wait_ge(den_ready, k + 1)
                nc.vector.reciprocal(stat[:, r, 6], stat[:, r, 5]).then_inc(rden_ready, 1)
                dve.wait_ge(rden_ready, k + 1)
                for i, (a, b) in enumerate([(0, NKEYS), (NKEYS, SC)] if u < G else [(0, SS), (SS, 2 * SS)]):
                    done = nc.vector.tensor_scalar(sc[:, r, a:b], sc[:, r, a:b], stat[:, r, 6, i:i + 1], None, ALU.mult)
                done.then_inc(p_ready, 1)

            def finish_group(n, s):
                for u in range(UNITS):
                    for at, what in ((11 + u, divide), (9 + u, scores)):
                        if at == s + SLABS_G:
                            what(n - 1, u)
                if s == 4:
                    dve.wait_ge(gb_sig, n)
                    nc.vector.tensor_tensor(gate[:, 0:2], gate[:, 0:2], sgb[:, 0:2], ALU.mult)
                    nc.vector.tensor_tensor(gate[:, 2:4], pz[:, 2:4, 0:TQ], sgb[:, 2:4], ALU.mult).then_inc(gb_ready, 1)
                if s == 8:
                    dve.wait_ge(o_copied, 5 * n)
                    dve.wait_ge(gb_ready, n)
                    nc.vector.tensor_tensor(gate[:], gate[:], ob[:], ALU.mult).then_inc(ob_ready, 1)

            def group_round(n):
                for s in range(SLABS_G):
                    if not (early(n, 1) and s < RING):
                        split_lo(dve, BASE_B + SLABS_G * n + s, s)
                    if not early(n, 1):
                        finish_group(n, s)
                    for u in range(UNITS):
                        for at, what in ((11 + u, divide), (9 + u, scores)):
                            if at == s:
                                what(n, u)
                    if s == 8 and not early(n, 1):
                        nc.vector.tensor_scalar(t2[:, C_SLOPE:C_ALL2], t2[:, C_SLOPE:C_ALL2], 0.5, None, ALU.mult
                                                ).then_inc(slope_ready, 1)
                        dve.wait_ge(slope_ready, n)

            group_round(0)
            with dve.Fori(1, KV) as n:
                group_round(n)
            out_projection(BASE_OUT_B, 2, [gate[:, 0:2], gate[:, 2:4]], lambda s: finish_group(KV, s), META, TQ)
            add_pair(BASE_OUT_B, 2, D // 256 - 1, 2, META, TQ)
            root_dve(dve, 2, TQ)
            dve.wait_ge(xg_ready, KT - 4)
            for c in range(3):
                result(nc.vector, c)

        @block.tensor
        def _(pe):
            pe.wait_ge(ones_loaded, 16)
            sum_squares(pe, 0, T)

            def levels(h, i):
                if i == 0:
                    pe.wait_ge(lev_mul, LEVELS * h + 3)
                    pe.wait_ge(lev_copied, LEVELS * h + 3)
                    if not early(h, 1):
                        pe.wait_ge(st_added, 4 * h)
                        pe.wait_ge(sp_copied, h)
                    cols = slice(2 * P, T)
                    for k, l in enumerate([3, 2, 1, 0, None]):
                        lhs, rhs = (ks, qs) if l is None else (kr[l], qc[l])
                        done = nc.tensor.matmul(RT[0:TAIL, k * TAIL:k * TAIL + TAIL], lhs[:, cols], rhs[:, cols],
                                                start=True, stop=True)
                    done.then_inc(lev_done, 1)
                else:
                    pe.wait_ge(lev_mul, LEVELS * h + LEVELS - 1)
                    pe.wait_ge(lev_copied, LEVELS * h + LEVELS - 1)
                    cols = slice((i - 1) * P, i * P)
                    for b, bank in ((0, RA0), (1, RA1)):
                        if i == 1:
                            if not early(h, 1):
                                pe.wait_ge(og_ready, h)
                        else:
                            pe.wait_ge(masked_ready, 5 * h + 2 + b)
                        for k, l in enumerate([6, 5, 4, 3] if b == 0 else [2, 1, 0, None]):
                            lhs, rhs = (ks, qs) if l is None else (kr[l], qc[l])
                            done = nc.tensor.matmul(bank[:, k * P:k * P + P], lhs[:, cols], rhs[:, cols],
                                                    start=True, stop=True)
                        done.then_inc(lev_done, 1)

            def cross(h):
                pe.wait_ge(kx_ready, h + 1)
                pe.wait_ge(lev_mul, LEVELS * (h + 1))
                pe.wait_ge(lev_copied, LEVELS * (h + 1))
                if not early(h, 1):
                    pe.wait_ge(og_ready, h)
                nc.tensor.matmul(RO[:, 0:P], kr[7][:, 0:P], qc[7][:, P:2 * P], start=True, stop=True)
                nc.tensor.matmul(RO[:, P:P + TAILP], kx[:], qc[4][:, 2 * P:TP], start=True, stop=True)
                nc.tensor.matmul(RO[:, P + TAILP:P + 2 * TAILP], kr[7][:, P:2 * P], qc[4][:, 2 * P:TP],
                                 start=True, stop=True)
                pe.wait_ge(kf_ready, h + 1)
                pe.wait_ge(kft_copied, h + 1)
                pe.wait_ge(masked_ready, 5 * h + 1)
                nc.tensor.transpose(RT[:, 0:P], kf[:, 0:P], ident)
                nc.tensor.transpose(RT[:, P:2 * P], kf[:, P:2 * P], ident)
                nc.tensor.transpose(RT[0:TAIL, 2 * P:3 * P], kf[:, 2 * P:T], ident).then_inc(kfT_done, 1)
                pe.wait_ge(k3_ready, h + 1)
                for g in range(2):
                    done = nc.tensor.transpose(RO[0:STACK, 2 * P + g * P:3 * P + g * P],
                                               k3[:, g].rearrange("p a t -> p (a t)").bitcast(F32), ident)
                done.then_inc(k3_turned, 1)

            def values(h):
                pe.wait_ge(i_copied, h + 1)
                pe.wait_ge(masked_ready, 5 * h + 5)
                for i in range(2):
                    for e in range(2):
                        done = nc.tensor.transpose(RA0[:, i * DV + e * P:i * DV + e * P + P], iT[:, e, i * P:i * P + P], ident)
                done.then_inc(vT_done, 1)
                for e in range(2):
                    done = nc.tensor.transpose(RA1[0:TAIL, e * P:e * P + P], iT[:, e, 2 * P:T], ident)
                done.then_inc(vT_done, 1)
                pe.wait_ge(v3_ready, h + 1)
                for g in range(2):
                    for e in range(2):
                        done = nc.tensor.transpose(pz[0:STACK, 2, g * DV + e * P:g * DV + e * P + P],
                                                   v3[:, e, g].rearrange("p a t -> p (a t)").bitcast(F32), ident)
                done.then_inc(v3_turned, 1)

            def head_outputs(h):
                pe.wait_ge(v_copied, h + 1)
                pe.wait_ge(att_ready, 3 * (h + 1))
                pe.wait_ge(cross_copied, h + 1)
                nc.tensor.matmul(RO[:, 0:DV], att[:, 0], V[:, 0], start=True, stop=True)
                nc.tensor.matmul(RO[:, DV:2 * DV], att[:, 2], V[:, 0], start=True, stop=False)
                nc.tensor.matmul(RO[:, DV:2 * DV], att[:, 1], V[:, 1], start=False, stop=True).then_inc(o_done, 1)
                out = RA1[0:TAIL, 0:DV]
                nc.tensor.matmul(out, att[0:TAIL, 3, 0:TAIL], V[0:TAIL, 2], start=True, stop=False)
                nc.tensor.matmul(out, attX[:, 0], V[:, 0], start=False, stop=False)
                nc.tensor.matmul(out, attX[:, 1], V[:, 1], start=False, stop=False)
                pe.wait_ge(s0_loaded, 16 * (h + 1))
                pe.wait_ge(Qs_ready, h + 1)
                for b in range(NB):
                    done = nc.tensor.matmul(out, Qs[:, TAIL * b:TAIL * b + TAIL], S0[:, b], start=False, stop=b == NB - 1)
                done.then_inc(o_done, 1)

            def states(t, k):
                bank = RT if k % 2 == 0 else RA0
                if k == 0:
                    pe.wait_ge(kt_copied, t + 1)
                    pe.wait_ge(kts_ready, t + 1)
                    nc.tensor.matmul(bank[:, 0:DV], kt[:, 0], V[:, 0], start=True, stop=False)
                    nc.tensor.matmul(bank[:, 0:DV], kt[:, 1], V[:, 1], start=False, stop=False)
                    nc.tensor.matmul(bank[:, 0:DV], kts[0:TAIL], V[0:TAIL, 2], start=False, stop=True).then_inc(st_done, 1)
                    return
                if k == 1:
                    pe.wait_ge(v3_copied, t + 1)
                if k == 2:
                    pe.wait_ge(sp_copied, t + 1)
                if k > 2:
                    pe.wait_ge(st_added, 4 * t + k - 2)
                for i in range(2):
                    b = 2 * k - 2 + i
                    done = nc.tensor.matmul(bank[:, i * DV:i * DV + DV], k3s[0:STACK, b], v3t[0:STACK, b // 4],
                                            start=True, stop=True)
                done.then_inc(st_done, 1)

            def turn_back(t):
                pe.wait_ge(on_ready, t + 1)
                for e, bank in ((0, RO), (1, RA1)):
                    for i, m in ((0, P), (1, P), (2, TAIL)):
                        done = nc.tensor.transpose(bank[:, i * P:i * P + m], on[0:m, i, e * P:e * P + P], ident[0:m, 0:m])
                done.then_inc(oT_done, 1)

            def finish_head(h, s):
                if s in (0, 1):
                    states(h - 1, 2 * s)
                    states(h - 1, 2 * s + 1)
                if s == 2:
                    states(h - 1, 4)
                if s == 3:
                    turn_back(h - 1)

            def head_round(h):
                for s in range(SLABS_H):
                    if s == 0 and not early(h, 1):
                        pe.wait_ge(g_ready, h)
                    if s == 4 and not early(h, 1):
                        pe.wait_ge(v3_copied, h)
                    if s == 8:
                        pe.wait_ge(qs_ready, h + 1)
                        pe.wait_ge(fk_ready, h + 1)
                    made = (lambda kt: (xl_ready, kt + 1)) if early(h, 1) and s < 4 else None
                    products(pe, SLABS_H * h + s, s, 4 * (s % 4), 2 * (s // 4 % 2), [xnH], [xnL], T, s % 4 == 0, s % 4 == 3,
                             made)
                    if not early(h, 1):
                        finish_head(h, s)
                    if s in (6, 7, 8):
                        levels(h, s - 6)
                    if s == 9:
                        cross(h)
                    if s == 10:
                        values(h)
                    if s == 11:
                        head_outputs(h)

            head_round(0)
            with pe.Fori(1, H) as h:
                head_round(h)

            def out_projection(base, c, free, free_next, before_first, finish, n):
                def out_round(j, par):
                    for s in range(SLABS_OUT):
                        if early(j, 1):
                            if s == 0:
                                before_first()
                                pe.wait_ge(*free)
                        if s == 0 and isinstance(j, int) and j == 1:
                            pe.wait_ge(*free_next)
                        if s == 0 and not early(j, 2):
                            pe.wait_ge(x_added, (D // 256) * (c - 1) + j - 1)
                        made = (lambda kt: (ogl_ready, ET // 2 * (c - 1) + kt // 2 + 1)) if early(j, 1) else None
                        products(pe, base + SLABS_OUT * j + s, s, SLAB * s, 2 * par, ogH, ogL, n, s == 0,
                                 s == SLABS_OUT - 1, made)
                        if early(j, 1):
                            finish(s)
                out_round(0, 0)
                out_round(1, 1)
                with pe.Fori(2, D // 256, 2) as j:
                    out_round(j, 0)
                    out_round(j + 1, 1)

            out_projection(BASE_OUT_A, 1, (g_ready, H), (v3_copied, H), lambda: finish_head(H, 0),
                           lambda s: s and finish_head(H, s), T)

            for s in range(SLABS_KV):
                if s == 0:
                    pe.wait_ge(x_added, 7)
                if s == 4:
                    pe.wait_ge(x_added, 8)
                if s in (8, 12):
                    pe.wait_ge(k_copied, s // 4 - 1)
                made = (lambda kt: (xl_ready, KT + kt + 1)) if s < 4 else None
                products(pe, BASE_KV + s, s, 4 * (s % 4), 2 * (s // 4 % 2), [xkH], [xkL], T, s % 4 == 0, s % 4 == 3,
                         made)
                if s == 0:
                    pe.wait_ge(st_added, 4 * H)
                    sum_squares(pe, 1, T)

            def values_by_token():
                pe.wait_ge(vt_copied, 2)
                pe.wait_ge(ms_ready, 2)
                for bank, a, b in ((RA0, 0, META), (RA1, META, META + P), (RO, META + P, TP), (RT, TP, T)):
                    for j in range(4):
                        done = nc.tensor.transpose(bank[0:b - a, j * P:j * P + P], vT[:, j, a:b], ident)
                    done.then_inc(vtok_done, 1)

            def score_products(n, u):
                k = UNITS * n + u
                bank = RA0 if u % 2 == 0 else RA1
                if u == 0:
                    pe.wait_ge(staged, n + 1)
                    pe.wait_ge(q_copied, 2 * n + 1)
                    if early(n, 1):
                        pe.wait_ge(vtok_copied, 4)
                if u == 4:
                    pe.wait_ge(q_copied, 2 * n + 2)
                if not early(k, 2):
                    pe.wait_ge(biased, k - 1)
                if u < G:
                    half = slice(64 * (u % 2), 64 * (u % 2) + 64)
                    nc.tensor.matmul(bank[:, 0:NKEYS], qT[half, u // 2, 0:P], kg[half, 0:NKEYS], start=True, stop=True)
                    nc.tensor.matmul(bank[:, NKEYS:SC], qT[half, u // 2, P:2 * P], kg[half, META:TP], start=True, stop=True
                                     ).then_inc(qk_done, 1)
                    return
                if u == G:
                    pe.wait_ge(ck_loaded, 32 * (n + 1))
                    pe.wait_ge(qsam_ready, n + 1)
                half = slice(64 * (u - G), 64 * (u - G) + 64)
                for four in range(2):
                    first = 4 * four
                    nc.tensor.matmul(bank[:, four * SS + WIN:four * SS + SS], qsam[half, first:first + 4].rearrange("p b w t -> p (b w t)"),
                                     kg[half, TP:T], start=True, stop=True)
                    for j in range(4):
                        done = nc.tensor.matmul(bank[32 * j:32 * j + 32, four * SS:four * SS + WIN],
                                                qsam[half, first + j].rearrange("p w t -> p (w t)"),
                                                ckT[half, first + j], start=True, stop=True)
                done.then_inc(qk_done, 1)

            def turn_p(n, u):
                k, r = UNITS * n + u, u % SCORES
                pe.wait_ge(p_ready, k + 1)
                if not early(k, 1):
                    pe.wait_ge(pt_copied, k)
                if u < G:
                    nc.tensor.transpose(RT[0:META, 0:P], sc[:, r, 0:META], ident)
                    for i in range(3):
                        a = META + i * P
                        done = nc.tensor.transpose(RT[:, P + i * P:2 * P + i * P], sc[:, r, a:a + P], ident)
                else:
                    for four in range(2):
                        nc.tensor.transpose(RT[:, four * 2 * P:four * 2 * P + P], sc[:, r, four * SS:four * SS + WIN], ident)
                        done = nc.tensor.transpose(RT[0:NB * TS, four * 2 * P + P:four * 2 * P + 2 * P],
                                                   sc[:, r, four * SS + WIN:four * SS + SS], ident)
                done.then_inc(tr_done, 1)

            def value_products(n, u):
                k, r = UNITS * n + u, u % 2
                pe.wait_ge(pt_copied, k + 1)
                if u == 0:
                    pe.wait_ge(v_staged, n + 1)
                    if early(n, 1):
                        pe.wait_ge(vtok_copied, 4)
                    else:
                        pe.wait_ge(o_copied, 5 * n)
                if u in (2, 4, 6, 8):
                    pe.wait_ge(o_copied, 5 * n + u // 2)
                if u < G:
                    half = slice(64 * (u % 2), 64 * (u % 2) + 64)
                    nc.tensor.matmul(RO[half, 0:P], vg[0:META, 0], pT[0:META, r, 0:P], start=True, stop=False)
                    nc.tensor.matmul(RO[half, 0:P], vg[:, 1], pT[:, r, P:2 * P], start=False, stop=True)
                    nc.tensor.matmul(RO[half, P:2 * P], vg[:, 1], pT[:, r, 2 * P:3 * P], start=True, stop=False)
                    nc.tensor.matmul(RO[half, P:2 * P], vg[:, 2], pT[:, r, 3 * P:4 * P], start=False, stop=True
                                     ).then_inc(pv_done, 1)
                    return
                half = slice(64 * (u - G), 64 * (u - G) + 64)
                for four in range(2):
                    c0, p0 = four * P, four * 2 * P
                    nc.tensor.matmul(RO[half, c0:c0 + P], vg[:, 3], pT[:, r, p0 + P:p0 + 2 * P], start=True, stop=True)
                    for j in range(4):
                        done = nc.tensor.matmul(RO[half, c0 + 32 * j:c0 + 32 * j + 32], cv[:, 4 * four + j],
                                                pT[:, r, p0 + 32 * j:p0 + 32 * j + 32], start=False, stop=True,
                                                skip_group_check=True)
                done.then_inc(pv_done, 1)

            def finish_group(n, s):
                for u in range(UNITS):
                    for at, what in ((11 + u, value_products), (9 + u, turn_p), (5 + u, score_products)):
                        if at == s + SLABS_G:
                            what(n - 1, u)

            def group_round(n):
                for s in range(SLABS_G):
                    if s == 0 and not early(n, 1):
                        pe.wait_ge(g0_copied, n)
                    if s == 4 and not early(n, 1):
                        pe.wait_ge(gb_ready, n)
                    if s == 4 and early(n, 1):
                        pe.wait_ge(vt_copied, 2)
                    if s in (8, 12):
                        pe.wait_ge(q_copied, 2 * n + s // 4 - 1)
                    made = (lambda kt: (xl_ready, 2 * KT + kt + 1)) if early(n, 1) and s < 4 else None
                    products(pe, BASE_B + SLABS_G * n + s, s, 4 * (s % 4), 2 * (s // 4 % 2), [xkH], [xkL], TQ,
                             s % 4 == 0, s % 4 == 3, made)
                    if early(n, 1) and s == 1:
                        values_by_token()
                    if not early(n, 1):
                        finish_group(n, s)
                    for u in range(UNITS):
                        for at, what in ((11 + u, value_products), (9 + u, turn_p), (5 + u, score_products)):
                            if at == s:
                                what(n, u)

            group_round(0)
            with pe.Fori(1, KV) as n:
                group_round(n)
            out_projection(BASE_OUT_B, 2, (g0_copied, KV), (gb_ready, KV), lambda: None, lambda s: finish_group(KV, s), TQ)
            sum_squares(pe, 2, TQ)


_OUTS = [("y", (KT, P, TQ)), ("st_prompt", (H, P, DV)), ("st_sample", (H, P, NB * DV)), ("k", (4, P, T)),
         ("v", (4, P, T)), ("ck_old", (NB, WIN - TS, KV * HD)), ("cv_old", (NB, WIN - TS, KV * HD))]


def slabs(w):
    k, n = w.shape
    return w.reshape(k // (SLAB * P), SLAB, P, n // 256, 256).transpose(3, 0, 2, 1, 4).reshape(-1, P, SLAB_W)


def kernel(x_prompt, x_sample, state_hgrn, cache_k, cache_v, meta_tokens, norm_a, w_in_a, lb_a, onorm_a,
           w_out_a, norm_kv, w_kv, norm_b, w_in_b, sink_b, w_out_b, norm_f):
    import concourse.bacc as bacc
    from concourse.bass_utils import run_bass_kernel_spmd

    f32 = np.float32
    arr = [np.asarray(a) for a in (x_prompt, x_sample, state_hgrn, cache_k, cache_v, meta_tokens, norm_a, w_in_a,
                                   onorm_a, w_out_a, norm_kv, w_kv, norm_b, w_in_b, sink_b, w_out_b, norm_f)]
    xp, xs, st, ck, cv, meta, na, wa, on, woa, nkv, wkv, nb, wb, sink, wob, nf = arr
    x = np.concatenate([meta, xp[0], xs.reshape(NB * TS, D)], axis=0)
    x_in = x.T.reshape(KT, P, T).transpose(1, 0, 2).reshape(P, KT * T)
    q, f, i, g = np.split(wa[0], [D, 2 * D, 4 * D], axis=1)
    heads = []
    for h in range(H):
        qf = np.concatenate([q[:, h * P:h * P + P], f[:, h * P:h * P + P]], axis=1)
        heads += [qf, i[:, h * DV:h * DV + DV], g[:, h * DV:h * DV + DV]]
    qb, gb = np.split(wb[0], 2, axis=1)
    groups = []
    for n in range(KV):
        groups += [qb[:, n * 512:n * 512 + 512], gb[:, n * 512:n * 512 + 512]]
    w_in = np.concatenate([slabs(w) for w in heads + [woa[0], wkv] + groups + [wob[0]]], axis=0)
    assert w_in.shape[0] == N_SLABS
    s0_in = st[0].transpose(1, 2, 0, 3).reshape(H, P, NB * DV)
    ckd = ck.transpose(2, 3, 0, 1).reshape(KV, HD, NB * WIN)
    ckd = np.concatenate([ckd, ckd], axis=1)
    cvd = cv.transpose(2, 1, 0, 3).reshape(KV, WIN, NB * HD)
    vec = np.concatenate([a.reshape(-1, P).T for a in (na[0], nkv, nb[0], nf, on[0])], axis=1)
    row = np.arange(P) // 8 % 4
    by_head = np.broadcast_to(sink[0].reshape(1, KV, G), (P, KV, G))
    by_row = np.stack([sink[0].reshape(KV, G)[:, 2 * row + par] for par in range(2)], axis=-1).transpose(1, 0, 2)
    sinks = np.concatenate([by_head, by_row], axis=2).reshape(P, KV * (G + 2))
    t1, t2 = tables()

    nc = bacc.Bacc("TRN2", target_bir_lowering=False, num_devices=1)
    feeds, aps = {}, []
    for name, a in (("x", x_in), ("w", w_in), ("s0", s0_in), ("ck", ckd), ("cv", cvd), ("vec", vec), ("sinks", sinks),
                    ("t1", t1), ("t2", t2), ("ck_rest", ck[:, TS:].reshape(NB, WIN - TS, KV * HD)),
                    ("cv_rest", cv[:, TS:].reshape(NB, WIN - TS, KV * HD))):
        a = np.ascontiguousarray(a)
        feeds["in_" + name] = a
        aps.append(nc.dram_tensor("in_" + name, a.shape, mybir.dt.from_np(a.dtype), kind="ExternalInput").ap())
    outs = [nc.dram_tensor("out_" + name, shape, F32, kind="ExternalOutput").ap() for name, shape in _OUTS]
    x_d, w_d, s0_d, ck_d, cv_d, vec_d, sink_d, t1_d, t2_d, ckr_d, cvr_d = aps
    trunk(nc, x_d, w_d, s0_d, cv_d, ck_d, vec_d, sink_d, t1_d, t2_d, ckr_d, cvr_d, *outs)
    r = run_bass_kernel_spmd(nc, [feeds], core_ids=[0]).results[0]
    y, sp, ss, k, v, ck_old, cv_old = (np.asarray(r["out_" + name]) for name, _ in _OUTS)
    y = y.reshape(D, TQ).T
    k, v = (a.reshape(KV * HD, T).T for a in (k, v))

    def window(old, new):
        return np.concatenate([old.reshape(NB, WIN - TS, KV, HD), new[TP:].reshape(NB, TS, KV, HD)], axis=1)
    return (y[:SEQ].reshape(1, SEQ, D), y[SEQ:].reshape(NB, TS, D), sp.reshape(1, 1, H, P, DV),
            k[TP - WIN:TP].reshape(1, WIN, KV, HD), v[TP - WIN:TP].reshape(1, WIN, KV, HD),
            ss.reshape(H, P, NB, DV).transpose(2, 0, 1, 3)[None], window(ck_old, k), window(cv_old, v))
```
